# Optimizing a Trainium2 kernel written in Bass

```python
import jax, jax.numpy as jnp
from jax import lax
import numpy as np

D_MODEL = 1024
BATCH = 1
SEQ = 512
DEPTH = 2

N_MIXERS = 2
N_NSA_LAYERS = (DEPTH + 1) // 2
N_FOX_LAYERS = DEPTH // 2

HEAD_DIM = 64
N_HEADS = D_MODEL // HEAD_DIM
HQ = N_HEADS * HEAD_DIM

NSA_GROUPS = 4
NSA_REP = N_HEADS // NSA_GROUPS
NSA_KV = NSA_GROUPS * HEAD_DIM
CMP_LEN = 32
CMP_STRIDE = 16
SEL_LEN = 64
N_SEL = 16
WINDOW = 512
PHI_HIDDEN = 256
Q_CHUNK = 64
N_BRANCH = 3
NSA_PROJ = HQ + 6 * NSA_KV + N_BRANCH * N_HEADS
FORCE_SCORE = 1e4

FOX_BLOCK = 128
FOX_PROJ = 3 * HQ + N_HEADS

D_FF = 2816
CONV_WIDTH = 3

ROPE_THETA = 10000.0
ALPHA = (2 * DEPTH) ** 0.25
BETA = (8 * DEPTH) ** -0.25
LN_EPS = 1e-5

kernel_name = "nsa_fox_interleaved_deepnorm_convffn"

def layer_norm(x, g, b):
    xf = x.astype(jnp.float32)
    mu = jnp.mean(xf, axis=-1, keepdims=True)
    var = jnp.mean(jnp.square(xf - mu), axis=-1, keepdims=True)
    y = (xf - mu) * lax.rsqrt(var + LN_EPS)
    return (y * g.astype(jnp.float32) + b.astype(jnp.float32)).astype(x.dtype)

def rope_tables(seq, dtype):
    inv = ROPE_THETA ** (-jnp.arange(0, HEAD_DIM, 2, dtype=jnp.float32) / HEAD_DIM)
    ang = jnp.arange(seq, dtype=jnp.float32)[:, None] * inv[None, :]
    ang = jnp.concatenate([ang, ang], axis=-1)
    return jnp.cos(ang).astype(dtype), jnp.sin(ang).astype(dtype)

def apply_rope(x, cos, sin):
    x1, x2 = jnp.split(x, 2, axis=-1)
    return x * cos + jnp.concatenate([-x2, x1], axis=-1) * sin

def masked_softmax(s, mask):
    s = jnp.where(mask, s, -jnp.inf)
    m = jnp.max(s, axis=-1, keepdims=True)
    m = jnp.where(jnp.isfinite(m), m, 0.0)
    e = jnp.exp(s - m)
    d = jnp.sum(e, axis=-1, keepdims=True)
    return e / jnp.where(d > 0, d, 1.0)

def compress(kv, pe, w1, b1, w2):
    S = kv.shape[2]
    n_cmp = (S - CMP_LEN) // CMP_STRIDE + 1
    idx = jnp.arange(n_cmp)[:, None] * CMP_STRIDE + jnp.arange(CMP_LEN)[None, :]
    blocks = kv[:, :, idx] + pe
    flat = blocks.reshape(blocks.shape[0], blocks.shape[1], n_cmp, CMP_LEN * HEAD_DIM)
    return jax.nn.gelu(flat @ w1 + b1) @ w2

def nsa_mixer(x, w_in, b_gate, pe, phik_w1, phik_b1, phik_w2, phiv_w1, phiv_b1, phiv_w2, w_o):
    B, S, _ = x.shape
    G, R, hd = NSA_GROUPS, NSA_REP, HEAD_DIM
    proj = x @ w_in
    cuts = [HQ + i * NSA_KV for i in range(7)]
    q, kc, vc, ks, vs, kw, vw, gl = jnp.split(proj, cuts, axis=-1)

    def kv_heads(t):
        return t.reshape(B, S, G, hd).transpose(0, 2, 1, 3)

    q = q.reshape(B, S, G, R, hd).transpose(0, 2, 3, 1, 4)
    gates = jax.nn.sigmoid((gl + b_gate).astype(jnp.float32))
    gates = gates.reshape(B, S, G, R, N_BRANCH).transpose(0, 2, 3, 1, 4).astype(x.dtype)

    cos, sin = rope_tables(S, x.dtype)
    q_rot = apply_rope(q, cos, sin)
    k_slc = apply_rope(kv_heads(ks), cos, sin)
    v_slc = kv_heads(vs)
    k_win = apply_rope(kv_heads(kw), cos, sin)
    v_win = kv_heads(vw)

    k_cmp = compress(kv_heads(kc), pe, phik_w1, phik_b1, phik_w2)
    v_cmp = compress(kv_heads(vc), pe, phiv_w1, phiv_b1, phiv_w2)
    n_cmp = k_cmp.shape[2]
    n_sb = S // SEL_LEN
    n_sel = min(N_SEL, n_sb)

    cmp_start = jnp.arange(n_cmp) * CMP_STRIDE
    sel_start = jnp.arange(n_sb) * SEL_LEN
    overlap = jnp.clip(jnp.minimum(cmp_start[:, None] + CMP_LEN, sel_start[None, :] + SEL_LEN)
                       - jnp.maximum(cmp_start[:, None], sel_start[None, :]), 0, None
                       ).astype(jnp.float32) / CMP_LEN
    cmp_end = cmp_start + CMP_LEN - 1

    ks_blocks = k_slc.reshape(B, G, n_sb, SEL_LEN, hd)
    vs_blocks = v_slc.reshape(B, G, n_sb, SEL_LEN, hd)
    pad = ((0, 0), (0, 0), (WINDOW, 0), (0, 0))
    kw_pad = jnp.pad(k_win, pad)
    vw_pad = jnp.pad(v_win, pad)
    bi = jnp.arange(B)[:, None, None, None]
    gi = jnp.arange(G)[None, :, None, None]
    blk = jnp.arange(n_sb)
    scale = HEAD_DIM ** -0.5

    def chunk(c):
        start = c * Q_CHUNK
        t = start + jnp.arange(Q_CHUNK)
        qn = lax.dynamic_slice_in_dim(q, start, Q_CHUNK, axis=3)
        qr = lax.dynamic_slice_in_dim(q_rot, start, Q_CHUNK, axis=3)
        gc = lax.dynamic_slice_in_dim(gates, start, Q_CHUNK, axis=3)

        s_c = jnp.einsum('bgrqd,bgkd->bgrqk', qn, k_cmp).astype(jnp.float32) * scale
        p_c = masked_softmax(s_c, cmp_end[None, :] <= t[:, None])
        o_c = jnp.einsum('bgrqk,bgkd->bgrqd', p_c.astype(v_cmp.dtype), v_cmp)

        imp = jnp.einsum('bgrqk,kj->bgqj', p_c, overlap)
        cur = t // SEL_LEN
        forced = (blk[None, :] == 0) | (blk[None, :] == cur[:, None]) | (blk[None, :] == cur[:, None] - 1)
        valid = blk[None, :] * SEL_LEN <= t[:, None]
        score = jnp.where(forced, FORCE_SCORE, jnp.where(valid, imp, -1.0))
        _, sel = lax.top_k(score, n_sel)
        k_sel = ks_blocks[bi, gi, sel].reshape(B, G, Q_CHUNK, n_sel * SEL_LEN, hd)
        v_sel = vs_blocks[bi, gi, sel].reshape(B, G, Q_CHUNK, n_sel * SEL_LEN, hd)
        pos = (sel[..., None] * SEL_LEN + jnp.arange(SEL_LEN)).reshape(B, G, Q_CHUNK, n_sel * SEL_LEN)
        s_s = jnp.einsum('bgrqd,bgqkd->bgrqk', qr, k_sel).astype(jnp.float32) * scale
        p_s = masked_softmax(s_s, (pos <= t[:, None])[:, :, None])
        o_s = jnp.einsum('bgrqk,bgqkd->bgrqd', p_s.astype(v_sel.dtype), v_sel)

        k_band = lax.dynamic_slice_in_dim(kw_pad, start, WINDOW + Q_CHUNK, axis=2)
        v_band = lax.dynamic_slice_in_dim(vw_pad, start, WINDOW + Q_CHUNK, axis=2)
        spos = start - WINDOW + jnp.arange(WINDOW + Q_CHUNK)
        diff = t[:, None] - spos[None, :]
        win_mask = (spos[None, :] >= 0) & (diff >= 0) & (diff < WINDOW)
        s_w = jnp.einsum('bgrqd,bgkd->bgrqk', qr, k_band).astype(jnp.float32) * scale
        p_w = masked_softmax(s_w, win_mask)
        o_w = jnp.einsum('bgrqk,bgkd->bgrqd', p_w.astype(v_band.dtype), v_band)

        return gc[..., 0:1] * o_c + gc[..., 1:2] * o_s + gc[..., 2:3] * o_w

    out = lax.map(chunk, jnp.arange(S // Q_CHUNK))
    out = out.transpose(1, 0, 4, 2, 3, 5).reshape(B, S, HQ)
    return out @ w_o

def fox_mixer(x, w_in, b_f, w_o):
    B, S, _ = x.shape
    proj = x @ w_in
    q, k, v, fl = jnp.split(proj, [HQ, 2 * HQ, 3 * HQ], axis=-1)

    def heads(t):
        return t.reshape(B, S, N_HEADS, HEAD_DIM).transpose(0, 2, 1, 3)

    q, k, v = heads(q), heads(k), heads(v)
    log_f = jax.nn.log_sigmoid((fl + b_f).astype(jnp.float32)).transpose(0, 2, 1)
    cum = jnp.cumsum(log_f, axis=-1)
    scale = HEAD_DIM ** -0.5
    outs = []
    for blk in range(S // FOX_BLOCK):
        s0, s1 = blk * FOX_BLOCK, (blk + 1) * FOX_BLOCK
        logits = jnp.einsum('bhqd,bhkd->bhqk', q[:, :, s0:s1], k[:, :, :s1]).astype(jnp.float32) * scale
        logits = logits + cum[:, :, s0:s1, None] - cum[:, :, None, :s1]
        causal = jnp.arange(s0, s1)[:, None] >= jnp.arange(s1)[None, :]
        p = masked_softmax(logits, causal)
        outs.append(jnp.einsum('bhqk,bhkd->bhqd', p.astype(v.dtype), v[:, :, :s1]))
    o = jnp.concatenate(outs, axis=2)
    return o.transpose(0, 2, 1, 3).reshape(B, S, HQ) @ w_o

def conv_ffn(x, w_up, conv_w, conv_b, w_down):
    h = x @ w_up
    C = h.shape[-1]
    h = lax.conv_general_dilated(h, conv_w[:, None, :], window_strides=(1,),
                                 padding=[(CONV_WIDTH - 1, 0)],
                                 dimension_numbers=('NWC', 'WIO', 'NWC'),
                                 feature_group_count=C) + conv_b
    a, b = jnp.split(h, 2, axis=-1)
    return (jax.nn.gelu(a) * b) @ w_down

def setup_inputs(seed: int = 0) -> dict:
    key = jax.random.key(seed)
    ks = jax.random.split(key, 24)
    nrm = jax.random.normal
    f32 = jnp.float32
    NA, NF = N_NSA_LAYERS, N_FOX_LAYERS
    return {
        "x": nrm(ks[0], (BATCH, SEQ, D_MODEL), f32),
        "nsa_w_in": nrm(ks[1], (NA, D_MODEL, NSA_PROJ), f32) * D_MODEL ** -0.5,
        "nsa_b_gate": nrm(ks[2], (NA, N_BRANCH * N_HEADS), f32) * 0.1,
        "nsa_pe": nrm(ks[3], (NA, CMP_LEN, HEAD_DIM), f32) * 0.1,
        "nsa_phik_w1": nrm(ks[4], (NA, CMP_LEN * HEAD_DIM, PHI_HIDDEN), f32) * (CMP_LEN * HEAD_DIM) ** -0.5,
        "nsa_phik_b1": nrm(ks[5], (NA, PHI_HIDDEN), f32) * 0.02,
        "nsa_phik_w2": nrm(ks[6], (NA, PHI_HIDDEN, HEAD_DIM), f32) * PHI_HIDDEN ** -0.5,
        "nsa_phiv_w1": nrm(ks[7], (NA, CMP_LEN * HEAD_DIM, PHI_HIDDEN), f32) * (CMP_LEN * HEAD_DIM) ** -0.5,
        "nsa_phiv_b1": nrm(ks[8], (NA, PHI_HIDDEN), f32) * 0.02,
        "nsa_phiv_w2": nrm(ks[9], (NA, PHI_HIDDEN, HEAD_DIM), f32) * PHI_HIDDEN ** -0.5,
        "nsa_w_o": nrm(ks[10], (NA, HQ, D_MODEL), f32) * HQ ** -0.5 * BETA,
        "fox_w_in": nrm(ks[11], (NF, D_MODEL, FOX_PROJ), f32) * D_MODEL ** -0.5,
        "fox_b_f": jax.random.uniform(ks[12], (NF, N_HEADS), f32, 1.0, 5.0),
        "fox_w_o": nrm(ks[13], (NF, HQ, D_MODEL), f32) * HQ ** -0.5 * BETA,
        "ffn_w_up": nrm(ks[14], (DEPTH, D_MODEL, 2 * D_FF), f32) * D_MODEL ** -0.5,
        "ffn_conv_w": nrm(ks[15], (DEPTH, CONV_WIDTH, 2 * D_FF), f32) * CONV_WIDTH ** -0.5,
        "ffn_conv_b": nrm(ks[16], (DEPTH, 2 * D_FF), f32) * 0.02,
        "ffn_w_down": nrm(ks[17], (DEPTH, D_FF, D_MODEL), f32) * D_FF ** -0.5 * BETA,
        "ln1_g": 1.0 + nrm(ks[18], (DEPTH, D_MODEL), f32) * 0.02,
        "ln1_b": nrm(ks[19], (DEPTH, D_MODEL), f32) * 0.02,
        "ln2_g": 1.0 + nrm(ks[20], (DEPTH, D_MODEL), f32) * 0.02,
        "ln2_b": nrm(ks[21], (DEPTH, D_MODEL), f32) * 0.02,
    }

def reference(x, nsa_w_in, nsa_b_gate, nsa_pe, nsa_phik_w1, nsa_phik_b1, nsa_phik_w2,
              nsa_phiv_w1, nsa_phiv_b1, nsa_phiv_w2, nsa_w_o, fox_w_in, fox_b_f, fox_w_o,
              ffn_w_up, ffn_conv_w, ffn_conv_b, ffn_w_down, ln1_g, ln1_b, ln2_g, ln2_b):
    for i in range(DEPTH):
        j = i // N_MIXERS
        if i % N_MIXERS == 0:
            y = nsa_mixer(x, nsa_w_in[j], nsa_b_gate[j], nsa_pe[j], nsa_phik_w1[j], nsa_phik_b1[j],
                          nsa_phik_w2[j], nsa_phiv_w1[j], nsa_phiv_b1[j], nsa_phiv_w2[j], nsa_w_o[j])
        else:
            y = fox_mixer(x, fox_w_in[j], fox_b_f[j], fox_w_o[j])
        x = layer_norm(ALPHA * x + y, ln1_g[i], ln1_b[i])
        f = conv_ffn(x, ffn_w_up[i], ffn_conv_w[i], ffn_conv_b[i], ffn_w_down[i])
        x = layer_norm(ALPHA * x + f, ln2_g[i], ln2_b[i])
    return x


_drawn_inputs = setup_inputs


def setup_inputs(seed=0):
    import zlib

    import numpy as np

    out = dict(_drawn_inputs(seed))
    spreads = {}
    factors = {'nsa_b_gate': 8.0,
     'nsa_pe': 5.609,
     'nsa_phik_w1': 2.995,
     'nsa_phik_b1': 58.251,
     'nsa_phik_w2': 2.926,
     'nsa_phiv_b1': 8.0,
     'ffn_conv_b': 6.115}
    for name, (base, spread) in spreads.items():
        noise = np.random.default_rng([zlib.crc32(name.encode()), seed]).standard_normal(out[name].shape)
        drawn = base * np.exp(spread * noise) if base else spread * noise
        out[name] = __import__('jax').numpy.asarray(drawn.astype(out[name].dtype))
    for name, factor in factors.items():
        out[name] = (out[name] * factor).astype(out[name].dtype)
    return out
```

```python
from contextlib import ExitStack

import concourse.bass as bass
from concourse import mybir

F32 = mybir.dt.float32
F32R = mybir.dt.float32r
BF16 = mybir.dt.bfloat16
ALU = mybir.AluOpType
ACT = mybir.ActivationFunctionType
AX = mybir.AxisListType

P = 128
D, SEQ, DEPTH = 1024, 512, 2
HD = 64
HEADS = D // HD
GROUPS, REP = 4, 4
KV = GROUPS * HD
CMP_LEN, CMP_STRIDE, PHI = 32, 16, 256
NCMP = (SEQ - CMP_LEN) // CMP_STRIDE + 1
NG = 3 * HEADS
FF = 2816
FB = FF // P
KB = D // P
QT = SEQ // P
LP = CMP_LEN // 2
ALPHA = (2 * DEPTH) ** 0.25
EPS = 1e-5
SCALE = HD ** -0.5
NEG = -1e30
FLOOR = -1e28

R = 3
C_NSA = 0
C_WO0 = C_NSA + 4 + 4 * GROUPS
C_UP0 = C_WO0 + KB
C_DN0 = C_UP0 + 2 * FB
C_FOX = C_DN0 + 3 * KB
C_WO1 = C_FOX + 3 * KB
C_UP1 = C_WO1 + KB
C_DN1 = C_UP1 + 2 * FB
C_END = C_DN1 + 3 * KB
DN_BLOCKS = (8, 8, FB - 16)

NSA_UNITS = HEADS * QT * 2
FOX_UNITS = HEADS * QT
NSA_ITEMS = 4 * GROUPS
Z0 = 8
FOX_STEPS = [(0, 3), (3, 6), (6, 8), (8, 11), (11, 14), (14, 16), (16, 20), (20, 24)]


def build_trunk(nc, t, out):
    with ExitStack() as ctx:
        def sb(name, shape, dt=F32):
            return ctx.enter_context(nc.sbuf_tensor(name, shape, dt))

        def sem(name):
            return ctx.enter_context(nc.semaphore(name))

        xh = sb("xh", [P, KB, SEQ], F32R)
        xl = sb("xl", [P, KB, SEQ], F32R)
        raw = sb("raw", [P, R, KB, P])
        wh = sb("wh", [P, R, KB, P], F32R)
        wl = sb("wl", [P, R, KB, P], F32R)
        work = sb("work", [P, 5 * SEQ])
        ident = sb("ident", [P, P])
        identb = sb("identb", [P, P], BF16)
        causal = sb("causal", [P, P])
        causalb = sb("causalb", [P, P], BF16)
        onesd = sb("onesd", [P, P])
        rotm = sb("rotm", [P, P])
        cmask = sb("cmask", [P, QT, NCMP])
        conv_nat = sb("conv_nat", [FB * 2, 4, P])
        vec_nat = sb("vec_nat", [68, P])
        pe_nat = sb("pe_nat", [LP, P])
        conv = sb("conv", [P, DEPTH, 4, 2 * FB])
        vecs = sb("vecs", [P, 68])
        pe2 = sb("pe2", [P, LP])
        eps = sb("eps", [P, 1])
        bgate = sb("bgate", [P, NG])
        gate = sb("gate", [P, QT, NG])
        kcd = sb("kcd", [P, GROUPS * NCMP])
        vcd = sb("vcd", [NCMP, GROUPS, HD])
        ghid = sb("ghid", [P, 2, GROUPS * NCMP])
        w2k = sb("w2k", [P, 2, HD])
        w2v = sb("w2v", [P, 2, HD])
        negmax = sb("negmax", [P, 4])
        psumrow = sb("psumrow", [P, 4])
        rinv = sb("rinv", [P, 4])
        csm = sb("csm", [P, QT, NCMP])
        cstat = sb("cstat", [P, 4, QT])
        bf = sb("bf", [HEADS, 1])
        ps = ctx.enter_context(nc.psum_tensor("ps", [P, 8, 512], F32))

        def overlay(*phases):
            made = []
            for n, phase in enumerate(phases):
                stay = ctx if n == len(phases) - 1 else ExitStack()
                made.append([stay.enter_context(nc.sbuf_tensor(name, shape, dt)) for name, shape, dt in phase])
                if stay is not ctx:
                    stay.close()
            return made

        (prob, pth, ptl), (cstack,), (z,) = overlay(
            [("prob", [P, 4, SEQ], F32), ("pth", [P, 2, SEQ], F32R), ("ptl", [P, 2, SEQ], F32R)],
            [("cstack", [P, 4, SEQ], F32R)],
            [("z", [P, KB, SEQ], F32)])

        def parities(names):
            return [(f"{name}{p}", shape, dt) for p in range(2) for name, shape, dt in names]

        o_parts = [("oh{}", [P, KB, SEQ], F32R), ("ol{}", [P, KB, SEQ], F32R)]
        nsa_state = [("qh", [P, 2, SEQ], F32R), ("ql", [P, 2, SEQ], F32R), ("ka", [P, 2, SEQ], F32R),
                     ("kb", [P, 2, SEQ], F32R), ("vh", [P, QT, P], F32R), ("vl", [P, QT, P], F32R), ("qf", [P, 2, SEQ], F32)]
        fox_state = [("fqh", [P, SEQ], F32R), ("fql", [P, SEQ], F32R), ("fkh", [P, SEQ], F32R), ("fkl", [P, SEQ], F32R),
                     ("fvh", [P, QT, P], F32R), ("fvl", [P, QT, P], F32R), ("biasq", [P, 2, SEQ], F32R), ("biask", [P, 2, SEQ], F32R)]
        prologue, nsa, fox, (onat,), (gh, gl) = overlay(
            [("w1k", [P, LP, PHI], F32), ("w1v", [P, LP, PHI], F32), ("parity0", [P, 12 * SEQ], F32),
             ("kc2", [P, GROUPS, SEQ], F32), ("kp", [P, LP, GROUPS * NCMP], F32),
             ("wg_raw", [P, KB, NG], F32), ("wg_h", [P, KB, NG], F32R), ("wg_l", [P, KB, NG], F32R)],
            [("oh", [P, KB, SEQ], F32R), ("ol", [P, KB, SEQ], F32R)] + parities(nsa_state)
            + [("cosT", [P, SEQ], F32), ("sinT", [P, SEQ], F32)],
            [("oh2", [P, KB, SEQ], F32R), ("ol2", [P, KB, SEQ], F32R)] + parities(fox_state)
            + [("wf_raw", [P, KB, HEADS], F32), ("wf_h", [P, KB, HEADS], F32R), ("wf_l", [P, KB, HEADS], F32R),
               ("fz", [P, SEQ], F32), ("fe", [P, SEQ], F32), ("fone", [P, SEQ], F32), ("fcum", [P, SEQ], F32)],
            [("onat", [P, QT, D], F32)],
            [("gh", [P, FB, SEQ], F32R), ("gl", [P, FB, SEQ], F32R)])
        w1k, w1v, _, kc2, kp, wg_raw, wg_h, wg_l = prologue
        oh, ol = nsa[0:2]
        qh, ql, ka, kb, vh, vl, qf = ([nsa[2 + n], nsa[9 + n]] for n in range(7))
        cosT, sinT = nsa[16:18]
        oh2, ol2 = fox[0:2]
        fqh, fql, fkh, fkl, fvh, fvl, biasq, biask = ([fox[2 + n], fox[10 + n]] for n in range(8))
        wf_raw, wf_h, wf_l, fz, fe, fone, fcum = fox[18:25]
        xnat = z[:, :, :].rearrange("p (m a) s -> p m (a s)", m=QT)
        tmpf, rot1, rot2 = (work[:, n * SEQ:(n + 1) * SEQ] for n in range(3))
        pct = work[:, 3 * SEQ:5 * SEQ].rearrange("p (a s) -> p a s", a=2)
        ua, ub, ga, gf = (work[:, n * SEQ:(n + 1) * SEQ] for n in range(4))
        zsum = work[:, 4 * SEQ:5 * SEQ]
        sq = work[:, 0:2 * SEQ].rearrange("p (a s) -> p a s", a=2)
        std = work[:, 2 * SEQ:3 * SEQ]
        rstd = work[:, 3 * SEQ:4 * SEQ]

        BP, BX, BS, BT, BO = 0, 1, 2, 4, 6

        s_raw = [sem(f"raw_landed{n}") for n in range(R)]
        s_wh = sem("w_hi")
        s_wl = sem("w_lo")
        s_wu = sem("w_used")
        s_ld = [sem(f"loaded{n}") for n in range(12)]
        s_cst = sem("consts_ready")
        s_vt = sem("vectors_turned")
        s_vc = sem("vectors_ready")
        s_xn = [sem(f"x_landed{n}") for n in range(QT)]
        s_xt = sem("x_turned")
        s_xh = sem("x_hi")
        s_x = sem("x_lo")
        s_gw = sem("gate_w_split")
        s_gp = sem("gate_products")
        s_ge = sem("gate_steps")
        s_kc = sem("cmp_source")
        s_kp = sem("cmp_blocks")
        s_hid = sem("cmp_hidden")
        s_gel = sem("cmp_gelu")
        s_cmpo = sem("cmp_out")
        s_cmpr = sem("cmp_ready")
        s_pf = sem("proj_copied")
        s_px = sem("proj_turned")
        s_r1 = sem("rope_cos")
        s_r2 = sem("rope_sin")
        s_r3 = sem("rope_sum")
        s_ph = sem("proj_hi")
        s_pl = sem("proj_lo")
        s_sw = [sem(f"keys_swapped{p}") for p in range(2)]
        s_sc = sem("scores")
        s_nm = sem("neg_max")
        s_ex = sem("exps")
        s_ri = sem("sum_inverse")
        s_pr = sem("probs")
        s_pt = sem("probs_turned")
        s_pth = sem("pt_hi")
        s_ptl = sem("pt_lo")
        s_pv = sem("pv_done")
        s_oh = sem("o_hi")
        s_ol = sem("o_lo")
        s_cs = sem("cmp_scores")
        s_cmask = sem("cmp_masked")
        s_cmax = sem("cmp_max")
        s_cfl = sem("cmp_max_finite")
        s_cdf = sem("cmp_differences")
        s_csum = sem("cmp_sum")
        s_csf = sem("cmp_sum_floored")
        s_cinv = sem("cmp_sum_inverse")
        s_cg = sem("cmp_gated_inverse")
        s_cp = sem("cmp_probs")
        s_ce = sem("cmp_exp")
        s_ct = sem("cmp_probs_turned")
        s_cc = sem("cmp_probs_copied")
        s_fw = sem("forget_w_split")
        s_fp = sem("forget_products")
        s_fa = sem("forget_act_steps")
        s_fd = sem("forget_dve_steps")
        s_cd = sem("cum_stored")
        s_bl = [sem(f"cum_rows{p}") for p in range(2)]
        s_c0 = sem("conv_tap2")
        s_c1 = sem("conv_tap1")
        s_c2 = sem("conv_tap0")
        s_gelu = sem("gelu")
        s_g = sem("gated")
        s_gh = sem("gated_hi")
        s_gl = sem("gated_lo")
        s_zs0 = sem("zsum_cleared")
        s_z1 = sem("z_first")
        s_z2 = sem("z_second")
        s_zs = sem("z_summed")
        s_mean = sem("mean")
        s_cent = sem("centred")
        s_sq = sem("squared")
        s_var = sem("variance")
        s_std = sem("std")
        s_rstd = sem("rstd")
        s_nrm = sem("normed")
        s_y = sem("affine")
        s_yt = sem("y_turned")
        s_yc = sem("y_copied_act")
        s_yd = sem("y_copied_dve")
        s_out = sem("out_stored")

        block = ctx.enter_context(nc.Block())

        @block.sync
        def _(sp):
            small = [
                (ident[:, :], t["c_ident"]), (causal[:, :], t["c_causal"]), (onesd[:, :], t["c_ones"]),
                (rotm[:, :], t["c_rot"]), (cmask[:, :, :], t["c_cmask"]),
            ]
            for m in range(QT):
                sp.dma_start(xnat[:, m, :], t["x"][0, m * P:(m + 1) * P, :]).then_inc(s_xn[m], 16)
                if m == 0:
                    sp.dma_start(small[0][0], small[0][1]).then_inc(s_ld[0], 16)

            def load(c, slot, src, nk=KB):
                if not isinstance(c, int) or c >= R:
                    sp.wait_ge(s_wl, c - (R - 1))
                sp.dma_start(raw[:, slot, 0:nk, :], src).then_inc(s_raw[slot], 16)

            def cols(w, a):
                return w[:, bass.ds(a, P)].rearrange("(k p) c -> p k c", p=P)

            w_nsa = t["nsa_w_in"][0]
            for c in range(2):
                load(c, c % R, cols(w_nsa, D + c * P))
            for n, (dst, src) in enumerate(small[1:]):
                sp.dma_start(dst, src).then_inc(s_ld[1 + n], 16)
            sp.dma_start(vec_nat[0:16, :], t["ln1_g"].rearrange("l (k p) -> (l k) p", p=P)).then_inc(s_ld[5], 16)
            sp.dma_start(vec_nat[16:32, :], t["ln1_b"].rearrange("l (k p) -> (l k) p", p=P)).then_inc(s_ld[5], 16)
            sp.dma_start(vec_nat[32:48, :], t["ln2_g"].rearrange("l (k p) -> (l k) p", p=P)).then_inc(s_ld[5], 16)
            sp.dma_start(vec_nat[48:64, :], t["ln2_b"].rearrange("l (k p) -> (l k) p", p=P)).then_inc(s_ld[5], 16)
            sp.dma_start(vec_nat[64:66, :], t["nsa_phik_b1"].rearrange("l (k p) -> (l k) p", p=P)).then_inc(s_ld[5], 16)
            sp.dma_start(vec_nat[66:68, :], t["nsa_phiv_b1"].rearrange("l (k p) -> (l k) p", p=P)).then_inc(s_ld[5], 16)
            sp.dma_start(pe_nat[:, :], t["nsa_pe"][0].rearrange("(l two) d -> l (two d)", two=2)).then_inc(s_ld[5], 16)
            sp.dma_start(wg_raw[:, :, :], t["nsa_w_in"][0][:, D + 6 * KV:D + 6 * KV + NG].rearrange("(k p) c -> p k c", p=P)).then_inc(s_ld[6], 16)
            sp.dma_start(bgate[:, :], t["nsa_b_gate"][0].rearrange("(a n) -> a n", a=1).to_broadcast([P, NG])).then_inc(s_ld[6], 16)
            sp.dma_start(w2k[:, :, :], t["nsa_phik_w2"][0].rearrange("(k p) c -> p k c", p=P)).then_inc(s_ld[7], 16)
            sp.dma_start(w2v[:, :, :], t["nsa_phiv_w2"][0].rearrange("(k p) c -> p k c", p=P)).then_inc(s_ld[7], 16)
            sp.dma_start(w1k[:, :, :], t["nsa_phik_w1"][0].rearrange("(k p) c -> p k c", p=P)).then_inc(s_ld[8], 16)
            for c in range(2, 4):
                load(c, c % R, cols(w_nsa, D + c * P))
            sp.dma_start(w1v[:, :, :], t["nsa_phiv_w1"][0].rearrange("(k p) c -> p k c", p=P)).then_inc(s_ld[9], 16)
            sp.dma_start(cosT[:, :], t["c_cos"]).then_inc(s_ld[10], 16)
            sp.dma_start(sinT[:, :], t["c_sin"]).then_inc(s_ld[10], 16)
            for l in range(DEPTH):
                if l == 1:
                    sp.wait_ge(s_vt, 6)
                sp.dma_start(conv_nat[:, 0:3, :], t["ffn_conv_w"][l].rearrange("w (b p) -> b w p", p=P)).then_inc(s_ld[11], 16)
                sp.dma_start(conv_nat[:, 3, :], t["ffn_conv_b"][l].rearrange("(b p) -> b p", p=P)).then_inc(s_ld[11], 16)

            wsv = w_nsa[:, D + 2 * KV:D + 6 * KV].rearrange("(k p) (two r) -> p k two r", p=P, two=2)
            for g in range(GROUPS):
                c = 4 + 4 * g
                for n, r0 in ((0, 0), (1, KV)):
                    sp.wait_ge(s_wl, c + n - (R - 1))
                    for b in range(2):
                        sp.dma_start(raw[:, (c + n) % R, :, b * HD:(b + 1) * HD],
                                     wsv[:, :, b, r0 + g * HD:r0 + (g + 1) * HD]).then_inc(s_raw[(c + n) % R], 16)
                for n in range(2):
                    load(c + 2 + n, (c + 2 + n) % R, cols(w_nsa, g * REP * HD + n * P))

            def load_out(c0, w):
                with sp.Fori(0, 2) as i:
                    for r in range(3):
                        load(c0 + 3 * i + r, (c0 + r) % R, cols(w, (3 * i + r) * P))
                for j in range(6, KB):
                    load(c0 + j, (c0 + j) % R, cols(w, j * P))

            def load_ffn(l, c_up, c_dn):
                up, dn = t["ffn_w_up"][l], t["ffn_w_down"][l]
                load(c_up, c_up % R, cols(up, 0))
                load(c_up + 1, (c_up + 1) % R, cols(up, FF))
                with sp.Fori(0, (FB - 1) // 3) as i:
                    for r in range(3):
                        c = c_up + 2 + 2 * r
                        load(c + 6 * i, c % R, cols(up, (1 + 3 * i + r) * P))
                        load(c + 1 + 6 * i, (c + 1) % R, cols(up, FF + (1 + 3 * i + r) * P))
                with sp.Fori(0, KB) as i:
                    for r in range(3):
                        nk = DN_BLOCKS[r]
                        src = dn[r * 8 * P:(r * 8 + nk) * P, bass.ds(i * P, P)].rearrange("(k p) c -> p k c", p=P)
                        load(c_dn + 3 * i + r, (c_dn + r) % R, src, nk)

            load_out(C_WO0, t["nsa_w_o"][0])
            load_ffn(0, C_UP0, C_DN0)

            w_fox = t["fox_w_in"][0]
            for r in range(3):
                load(C_FOX + r, (C_FOX + r) % R, cols(w_fox, r * D))
            sp.wait_ge(s_wu, C_FOX)
            sp.dma_start(wf_raw[:, :, :], w_fox[:, 3 * D:3 * D + HEADS].rearrange("(k p) c -> p k c", p=P)).then_inc(s_ld[6], 16)
            sp.dma_start(bf[:, :], t["fox_b_f"].rearrange("a h -> h a")).then_inc(s_ld[6], 16)
            sp.wait_ge(s_fd, 12)
            sp.dma_start(t["cum"].rearrange("r h s -> h r s"), cstack[0:HEADS, :, :].bitcast(F32)).then_inc(s_cd, 16)
            sp.wait_ge(s_cd, 16)

            def load_rows(pair, par, used):
                if used is not None:
                    sp.wait_ge(s_sc, used)
                sp.dma_start(biasq[par][2:4, :, :].bitcast(F32), t["cum"][0:2, bass.ds(2 * pair, 2), :]).then_inc(s_bl[par], 16)
                sp.dma_start(biask[par][0:2, :, :].bitcast(F32), t["cum"][2:4, bass.ds(2 * pair, 2), :]).then_inc(s_bl[par], 16)

            load_rows(0, 0, None)
            load_rows(1, 1, None)
            for r in range(3):
                load(C_FOX + 3 + r, (C_FOX + r) % R, cols(w_fox, P + r * D))
            with sp.Fori(0, 3) as i:
                for par in range(2):
                    pair = 2 * i + par + 2
                    for r in range(3):
                        load(C_FOX + 3 * pair + r, (C_FOX + r) % R, cols(w_fox, pair * P + r * D))
                    load_rows(pair, par, NSA_UNITS + 8 * (2 * i + par + 1))
            load_out(C_WO1, t["fox_w_o"][0])
            load_ffn(1, C_UP1, C_DN1)
            for m in range(QT):
                sp.wait_ge(s_yc, m + 1)
                sp.wait_ge(s_yd, m + 1)
                sp.dma_start(out[0, m * P:(m + 1) * P, :], onat[:, m, :]).then_inc(s_out, 16)
            sp.wait_ge(s_out, 16 * QT)

        @block.gpsimd
        def _(pool):
            def lo(c, slot, nk=KB):
                pool.wait_ge(s_wh, c + 1)
                nc.gpsimd.tensor_tensor(wl[:, slot, 0:nk, :], raw[:, slot, 0:nk, :],
                                        wh[:, slot, 0:nk, :].bitcast(F32), ALU.subtract).then_inc(s_wl, 1)

            def los(c0, n):
                with pool.Fori(0, n // R) as i:
                    for r in range(R):
                        lo(c0 + R * i + r, (c0 + r) % R)
                for c in range(c0 + n // R * R, c0 + n):
                    lo(c, c % R)

            def los_down(c0):
                with pool.Fori(0, KB) as i:
                    for r in range(R):
                        lo(c0 + R * i + r, (c0 + r) % R, DN_BLOCKS[r])

            los(0, C_DN0)
            los_down(C_DN0)
            los(C_FOX, C_DN1 - C_FOX)
            los_down(C_DN1)

        @block.scalar
        def _(act):
            RAW_EXTRA = [0, 0, 0]
            for g in range(GROUPS):
                for n in range(2):
                    RAW_EXTRA[(4 + 4 * g + n) % R] += 1

            def landed(c):
                return sum(2 if 4 <= x < C_WO0 and (x - 4) % 4 < 2 else 1 for x in range(c + 1) if x % R == c % R)

            def hi(c, slot, nk=KB, n=None):
                act.wait_ge(s_raw[slot], 16 * (landed(c) if n is None else n))
                if not isinstance(c, int) or c >= R:
                    act.wait_ge(s_wu, c - (R - 1))
                nc.scalar.activation(wh[:, slot, 0:nk, :], raw[:, slot, 0:nk, :], ACT.Copy).then_inc(s_wh, 1)

            def hi_at(base, k, i=0, step=0, nk=KB):
                c = base + k
                n = c // R + 1 + RAW_EXTRA[c % R]
                hi(c + step * i if step else c, c % R, nk, n + (step // R) * i if step else n)

            for k in range(KB):
                act.wait_ge(s_xt, k + 1)
                nc.scalar.activation(xh[:, k, :], ps[:, k, :], ACT.Copy).then_inc(s_xh, 1)
                if k == 1:
                    hi(0, 0)
                if k == 4:
                    hi(1, 1)
            act.wait_ge(s_ld[6], 32)
            nc.scalar.activation(wg_h[:, :, :], wg_raw[:, :, :], ACT.Copy).then_inc(s_gw, 1)
            for src in range(2):
                for cc in range(2):
                    c = 2 * src + cc
                    hi(c + 2, (c + 2) % R)
                    act.wait_ge(s_wu, c + 1)
                    if src:
                        act.wait_ge(s_kp, 8)
                    for half in range(2):
                        g = 2 * cc + half
                        nc.scalar.activation(kc2[0:HD, g, :], ps[half * HD:(half + 1) * HD, BP, :], ACT.Copy)
                        last = nc.scalar.activation(kc2[HD:P, g, 0:SEQ - 1], ps[half * HD:(half + 1) * HD, BP, 1:SEQ], ACT.Copy)
                    last.then_inc(s_kc, 1)
                if src == 0:
                    act.wait_ge(s_ge, 1)
                    nc.scalar.activation(gate[:, :, :], gate[:, :, :], ACT.Exp, scale=-1.0).then_inc(s_ge, 1)
                act.wait_ge(s_hid, src + 1)
                act.wait_ge(s_vc, 1)
                if src:
                    act.wait_ge(s_cmpo, 1)
                for hb in range(2):
                    last = nc.scalar.activation(ghid[:, hb, :], ps[:, 2, hb * P:hb * P + GROUPS * NCMP], ACT.Gelu_apprx_tanh,
                                                bias=vecs[:, 64 + 2 * src + hb:65 + 2 * src + hb])
                last.then_inc(s_gel, 1)
                act.wait_ge(s_cmpo, src + 1)
                if src == 0:
                    nc.scalar.activation(kcd[0:HD, :], ps[0:HD, 3, 0:GROUPS * NCMP], ACT.Copy)
                    nc.scalar.activation(kcd[HD:P, :], ps[0:HD, 3, 0:GROUPS * NCMP], ACT.Copy).then_inc(s_cmpr, 1)
                else:
                    nc.scalar.activation(vcd[:, :, :], ps[0:NCMP, 4, 0:GROUPS * HD].rearrange("p (g d) -> p g d", g=GROUPS), ACT.Copy).then_inc(s_cmpr, 1)

            def item_copy(g, k):
                n = 4 * g + k
                act.wait_ge(s_wu, 4 + n + 1)
                if n:
                    act.wait_ge(s_pl, n)
                if g >= 2:
                    act.wait_ge(s_pv, 32 * (g - 1))
                if k < 2:
                    nc.scalar.activation(tmpf, ps[:, BP, :], ACT.Copy).then_inc(s_pf, 1)
                else:
                    nc.scalar.activation(qf[g % 2][:, k - 2, :], ps[:, BP, :], ACT.Copy, scale=SCALE).then_inc(s_pf, 1)

            def item_hi(g, k):
                n, par = 4 * g + k, g % 2
                if k == 1:
                    act.wait_ge(s_px, n + 1)
                    nc.scalar.activation(vh[par][:, :, :], ps[:, BX, :].rearrange("p (m c) -> p m c", m=QT), ACT.Copy).then_inc(s_ph, 1)
                else:
                    act.wait_ge(s_r3, n - (n + 2) // 4 + 1)
                    dst = ka[par][:, 0, :] if k == 0 else qh[par][:, k - 2, :]
                    nc.scalar.activation(dst, rot1, ACT.Copy).then_inc(s_ph, 1)
                if k == 0:
                    act.wait_ge(s_pl, n + 1)
                    act.dma_start(kb[par][0:HD, :, :].bitcast(F32), ka[par][HD:P, :, :].bitcast(F32)).then_inc(s_sw[par], 16)
                    act.dma_start(kb[par][HD:P, :, :].bitcast(F32), ka[par][0:HD, :, :].bitcast(F32)).then_inc(s_sw[par], 16)

            def unit_exp(u, loc):
                act.wait_ge(s_nm, u + 1)
                if not isinstance(u, int) or u >= 4:
                    act.wait_ge(s_pt, u - 3)
                i = loc[1]
                n = (i + 1) * P
                nc.scalar.activation(prob[:, loc[0] % 4, 0:n], ps[:, BS + loc[0] % 2, 0:n], ACT.Exp,
                                     bias=negmax[:, loc[0] % 4:loc[0] % 4 + 1],
                                     accum_out=psumrow[:, loc[0] % 4:loc[0] % 4 + 1]).then_inc(s_ex, 1)

            def unit_hi(u, loc):
                act.wait_ge(s_pt, u + 1)
                if not isinstance(u, int) or u >= 2:
                    act.wait_ge(s_pv, u - 1)
                n = (loc[1] + 1) * P
                nc.scalar.activation(pth[:, loc[0] % 2, 0:n], ps[:, BT + loc[0] % 2, 0:n], ACT.Copy).then_inc(s_pth, 1)

            def head_hi(u_end, par, half, pair, oh=oh):
                act.wait_ge(s_pv, u_end)
                nc.scalar.activation(oh[half * HD:(half + 1) * HD, pair, :] if isinstance(pair, int) else
                                     oh[half * HD:(half + 1) * HD, bass.ds(pair, 1), :].rearrange("p a s -> p (a s)"),
                                     ps[0:HD, BO + par, :], ACT.Copy).then_inc(s_oh, 1)

            for k in range(4):
                hi(4 + k + 2, (4 + k + 2) % R)
                if k == 0:
                    act.wait_ge(s_cmpr, 2)
                item_copy(0, k)
                item_hi(0, k)
            for g in range(GROUPS):
                for v in range(32):
                    u = 32 * g + v
                    for x in ([0, 1, 2] if u == 0 else [v + 2]):
                        uu = 32 * g + x
                        if x % 8 == 0 and uu < NSA_UNITS:
                            act.wait_ge(s_cdf, uu // 8 + 1)
                            nc.scalar.activation(csm[:, :, :], csm[:, :, :], ACT.Exp).then_inc(s_ce, 1)
                        if uu < NSA_UNITS:
                            unit_exp(uu, (uu, uu % 8 // 2))
                    unit_hi(u, (u, v % 8 // 2))
                    if v % 8 == 1 and u > 8:
                        head_hi(u - 1, (u // 8 - 1) % 2, (u // 8 - 1) % 2, (u // 8 - 1) // 2)
                    if g < GROUPS - 1 and v % 8 == 7:
                        c = 4 + 4 * (g + 1) + v // 8
                        hi(c + 2, (c + 2) % R)
                        item_copy(g + 1, v // 8)
                    if v % 8 == 3 and (v > 3 and g < GROUPS - 1 or v == 3 and g > 0):
                        item_hi(*((g + 1, v // 8 - 1) if v > 3 else (g, 3)))
            head_hi(NSA_UNITS, 1, 1, KB - 1)

            def out_act(c0):
                with act.Fori(0, 2) as i:
                    for r in range(3):
                        hi_at(c0, r + 2, i, 3)
                for j in range(6, KB):
                    hi_at(c0, j + 2)

            def ln_act(n, final):
                g0 = (n // 2) * 8 + (0 if n % 2 == 0 else 32)
                for k in range(KB):
                    act.wait_ge(s_cent, 8 * n + k + 1)
                    if k >= 2:
                        act.wait_ge(s_var, 8 * n + k - 1)
                    nc.scalar.activation(sq[:, k % 2, :], z[:, k, :], ACT.Square).then_inc(s_sq, 1)
                act.wait_ge(s_var, 8 * n + KB)
                nc.scalar.activation(std, ps[:, 7, :], ACT.Sqrt, bias=eps[:, 0:1]).then_inc(s_std, 1)
                for k in range(KB):
                    act.wait_ge(s_nrm, 8 * n + k + 1)
                    nc.scalar.activation(z[:, k, :], z[:, k, :], ACT.Identity, scale=vecs[:, g0 + k:g0 + k + 1],
                                         bias=vecs[:, g0 + 16 + k:g0 + 17 + k]).then_inc(s_y, 1)
                    if not final:
                        act.wait_ge(s_y, 8 * n + k + 1)
                        nc.scalar.activation(xh[:, k, :], z[:, k, :], ACT.Copy).then_inc(s_xh, 1)

            def ffn_act(l, c_up, c_dn):
                def pair(j, ca, i=0, step=0):
                    c = ca + step * i
                    jj = FB * l + j
                    hi_at(ca, 2, i, step)
                    act.wait_ge(s_wu, c + 1)
                    if not isinstance(j, int) or jj > 0:
                        act.wait_ge(s_g, jj)
                    bk = (ca - c_up) % 6
                    nc.scalar.activation(ua, ps[:, bk, :], ACT.Identity, scale=conv[:, l, 2, bass.ds(j, 1)],
                                         bias=conv[:, l, 3, bass.ds(j, 1)]).then_inc(s_c0, 1)
                    act.wait_ge(s_c2, 2 * jj + 1)
                    nc.scalar.activation(ga, ua, ACT.Gelu_apprx_tanh).then_inc(s_gelu, 1)
                    hi_at(ca, 3, i, step)
                    act.wait_ge(s_wu, c + 2)
                    nc.scalar.activation(ub, ps[:, bk + 1, :], ACT.Identity, scale=conv[:, l, 2, bass.ds(FB + j, 1)],
                                         bias=conv[:, l, 3, bass.ds(FB + j, 1)]).then_inc(s_c0, 1)
                    act.wait_ge(s_g, jj + 1)
                    nc.scalar.activation(gh[:, bass.ds(j, 1), :].rearrange("p a s -> p (a s)"), gf, ACT.Copy).then_inc(s_gh, 1)

                pair(0, c_up)
                with act.Fori(0, (FB - 1) // 3) as i:
                    for r in range(3):
                        pair(1 + 3 * i + r, c_up + 2 + 2 * r, i, 6)
                with act.Fori(0, KB - 1) as i:
                    for r in range(3):
                        hi_at(c_dn, r + 2, i, 3, DN_BLOCKS[(r + 2) % 3])
                hi_at(c_dn + 3 * (KB - 1), 2, nk=DN_BLOCKS[2])
                if l == 0:
                    hi_at(c_dn + 3 * KB, 0)
                    hi_at(c_dn + 3 * KB, 1)

            out_act(C_WO0)
            ln_act(0, False)
            ffn_act(0, C_UP0, C_DN0)
            ln_act(1, False)

            act.wait_ge(s_ld[6], 64)
            nc.scalar.activation(wf_h[:, :, :], wf_raw[:, :, :], ACT.Copy).then_inc(s_fw, 1)
            act.wait_ge(s_fd, 6)
            nc.scalar.activation(fe[0:HEADS, :], fz[0:HEADS, :], ACT.Abs).then_inc(s_fa, 1)
            act.wait_ge(s_fa, 1)
            nc.scalar.activation(fe[0:HEADS, :], fe[0:HEADS, :], ACT.Exp, scale=-1.0).then_inc(s_fa, 1)
            act.wait_ge(s_fd, 7)
            nc.scalar.activation(fe[0:HEADS, :], fe[0:HEADS, :], ACT.Ln).then_inc(s_fa, 1)
            act.wait_ge(s_fd, 9)
            nc.scalar.activation(cstack[0:HEADS, 0, :], fcum[0:HEADS, :], ACT.Copy).then_inc(s_fa, 1)

            def fox_hi(n, par, r, free):
                if r < 2:
                    act.wait_ge(s_wu, C_FOX + n - NSA_ITEMS + 1)
                    if free is not None:
                        act.wait_ge(s_sc, free)
                    nc.scalar.activation(fqh[par][:, :] if r == 0 else fkh[par][:, :], ps[:, BP, :], ACT.Copy,
                                         scale=SCALE if r == 0 else 1.0).then_inc(s_ph, 1)
                else:
                    act.wait_ge(s_px, NSA_ITEMS + (n - NSA_ITEMS) // 3 + 1 if isinstance(n, int) else n)
                    if free is not None:
                        act.wait_ge(s_pv, free)
                    nc.scalar.activation(fvh[par][:, :, :], ps[:, BX, :].rearrange("p (m c) -> p m c", m=QT), ACT.Copy).then_inc(s_ph, 1)

            def fox_value_copy(c, n_lo):
                act.wait_ge(s_wu, c + 1)
                act.wait_ge(s_pl, n_lo)
                nc.scalar.activation(tmpf, ps[:, BP, :], ACT.Copy).then_inc(s_pf, 1)

            for r in range(3):
                hi_at(C_FOX, r + 2)
                if r == 2:
                    fox_value_copy(C_FOX + 2, NSA_ITEMS + 2)
                fox_hi(NSA_ITEMS + r, 0, r, None)

            def fox_value_hi(par, nv, used):
                act.wait_ge(s_px, nv)
                act.wait_ge(s_pv, used)
                nc.scalar.activation(fvh[par][:, :, :], ps[:, BX, :].rearrange("p (m c) -> p m c", m=QT), ACT.Copy).then_inc(s_ph, 1)

            def fox_stages(pair, p0, i, step, first=False, more=True):
                par = p0 % 2
                U = NSA_UNITS + 8 * pair
                for v in range(8):
                    if more or v + 2 < 8:
                        unit_exp(U + v + 2, (v + 2, (v + 2) % 4))
                    unit_hi(U + v, (v, v % 4))
                    if v == 0 and not first:
                        fox_value_hi(par, NSA_ITEMS + pair + 1, U - 8)
                    if v == 1 and not first:
                        head_hi(U, 1, 1, pair - 1, oh2)
                    if v == 5:
                        head_hi(U + 4, 0, 0, pair, oh2)
                    if more and v in (2, 5, 7):
                        r = (2, 5, 7).index(v)
                        hi_at(C_FOX, 3 * (p0 + 1) + r + 2, i, 3 * step)
                        if r < 2:
                            act.wait_ge(s_wu, C_FOX + 3 * (pair + 1) + r + 1)
                            act.wait_ge(s_sc, U)
                            nc.scalar.activation(fqh[1 - par][:, :] if r == 0 else fkh[1 - par][:, :], ps[:, BP, :], ACT.Copy,
                                                 scale=SCALE if r == 0 else 1.0).then_inc(s_ph, 1)
                        else:
                            fox_value_copy(C_FOX + 3 * (pair + 1) + 2, NSA_ITEMS + 3 * (pair + 1) + 2)

            act.wait_ge(s_cd, 16)
            unit_exp(NSA_UNITS, (0, 0))
            unit_exp(NSA_UNITS + 1, (1, 1))
            fox_stages(0, 0, 0, 0, first=True)
            with act.Fori(0, 3) as i:
                for r in range(2):
                    fox_stages(1 + r + 2 * i, 1 + r, i, 2)
            fox_stages(7, 7, 0, 0, more=False)
            head_hi(NSA_UNITS + FOX_UNITS, 1, 1, KB - 1, oh2)

            out_act(C_WO1)
            ln_act(2, False)
            ffn_act(1, C_UP1, C_DN1)
            ln_act(3, True)
            for m in range(QT):
                act.wait_ge(s_yt, 2 * m + 1)
                nc.scalar.activation(onat[:, m, 0:512], ps[:, 2 * m, :], ACT.Copy).then_inc(s_yc, 1)

        @block.tensor
        def _(pe):
            def mm3(o, ah, al, bh, bl, start, stop):
                nc.tensor.matmul(o, ah, bh, start=start, stop=False)
                nc.tensor.matmul(o, ah, bl, start=False, stop=False)
                return nc.tensor.matmul(o, al, bh, start=False, stop=stop)

            pe.wait_ge(s_ld[0], 16)
            for k in range(KB):
                for m in range(QT):
                    if k == 0:
                        pe.wait_ge(s_xn[m], 16)
                    last = nc.tensor.transpose(ps[:, k, m * P:(m + 1) * P], xnat[:, m, k * P:(k + 1) * P], ident[:, :])
                last.then_inc(s_xt, 1)

            def chunk(c, slot, bank, srch, srcl, k0=0, nk=KB, first=True, final=True, fresh=None):
                pe.wait_ge(s_wl, c + 1)
                for k in range(nk):
                    if fresh is not None:
                        pe.wait_ge(s_x, fresh + k)
                    last = mm3(ps[:, bank, :], wh[:, slot, k, :], wl[:, slot, k, :], srch[:, k0 + k, :], srcl[:, k0 + k, :],
                               first and k == 0, final and k == nk - 1)
                last.then_inc(s_wu, 1)

            def kstep(c, slot, k):
                if k == 0:
                    pe.wait_ge(s_wl, c + 1)
                last = mm3(ps[:, BP, :], wh[:, slot, k, :], wl[:, slot, k, :], xh[:, k, :], xl[:, k, :], k == 0, k == KB - 1)
                if k == KB - 1:
                    last.then_inc(s_wu, 1)

            for src in range(2):
                for cc in range(2):
                    c = 2 * src + cc
                    if c:
                        pe.wait_ge(s_kc, c)
                    chunk(c, c % R, BP, xh, xl, fresh=1 if c == 0 else None)
                if src == 0:
                    pe.wait_ge(s_gw, 2)
                    for m in range(QT):
                        for k in range(KB):
                            last = mm3(ps[:, 5, m * NG:(m + 1) * NG], xh[:, k, m * P:(m + 1) * P], xl[:, k, m * P:(m + 1) * P],
                                       wg_h[:, k, :], wg_l[:, k, :], k == 0, k == KB - 1)
                    last.then_inc(s_gp, 1)
                    pe.wait_ge(s_ld[5], 16 * 7)
                    nc.tensor.transpose(ps[:, 6, 0:68], vec_nat[:, :], ident[0:68, 0:68]).then_inc(s_vt, 1)
                    nc.tensor.transpose(ps[:, 6, 128:128 + LP], pe_nat[:, :], ident[0:LP, 0:LP]).then_inc(s_vt, 1)
                    pe.wait_ge(s_ld[11], 32)
                    for w in range(4):
                        nc.tensor.transpose(ps[:, 7, w * P:w * P + 2 * FB], conv_nat[:, w, :], ident[0:2 * FB, 0:2 * FB]).then_inc(s_vt, 1)
                pe.wait_ge(s_kp, 8 * (src + 1))
                pe.wait_ge(s_ld[8 + src], 16)
                for hb in range(2):
                    for lp in range(LP):
                        last = nc.tensor.matmul(ps[:, 2, hb * P:hb * P + GROUPS * NCMP], (w1k, w1v)[src][:, lp, hb * P:(hb + 1) * P],
                                                kp[:, lp, :], start=(lp == 0), stop=(lp == LP - 1))
                last.then_inc(s_hid, 1)
                pe.wait_ge(s_gel, src + 1)
                pe.wait_ge(s_ld[7], 32)
                if src == 0:
                    for hb in range(2):
                        last = nc.tensor.matmul(ps[0:HD, 3, 0:GROUPS * NCMP], w2k[:, hb, :], ghid[:, hb, :], start=(hb == 0), stop=(hb == 1))
                else:
                    for g in range(GROUPS):
                        for hb in range(2):
                            last = nc.tensor.matmul(ps[0:NCMP, 4, g * HD:(g + 1) * HD], ghid[:, hb, g * NCMP:(g + 1) * NCMP], w2v[:, hb, :],
                                                    start=(hb == 0), stop=(hb == 1))
                last.then_inc(s_cmpo, 1)
                if src == 0:
                    pe.wait_ge(s_vc, 3)
                    pe.wait_ge(s_ld[11], 64)
                    for w in range(4):
                        nc.tensor.transpose(ps[:, 7, w * P:w * P + 2 * FB], conv_nat[:, w, :], ident[0:2 * FB, 0:2 * FB]).then_inc(s_vt, 1)

            def item_turn(g, k):
                n = 4 * g + k
                pe.wait_ge(s_pf, n + 1)
                if k == 1:
                    for m in range(QT):
                        last = nc.tensor.transpose(ps[:, BX, m * P:(m + 1) * P], tmpf[:, m * P:(m + 1) * P], ident[:, :])
                else:
                    src = tmpf if k == 0 else qf[g % 2][:, k - 2, :]
                    last = nc.tensor.matmul(ps[:, BX, :], rotm[:, :], src, start=True, stop=True)
                last.then_inc(s_px, 1)

            pe.wait_ge(s_ld[3], 16)
            pe.wait_ge(s_kc, 4)
            for k in range(4):
                c = 4 + k
                if k:
                    pe.wait_ge(s_pf, k)
                for kk in range(KB):
                    kstep(c, c % R, kk)
                if k:
                    pe.wait_ge(s_pl, k)
                item_turn(0, k)

            def mask(bank, i, stop=True):
                return nc.tensor.matmul(ps[:, bank, i * P:(i + 1) * P], identb[:, :], causalb[:, :], start=False, stop=stop)

            def nsa_scores(u):
                g, v = u // 32, u % 32
                h, i, br = v // 8, v % 8 // 2, v % 2
                par, half = g % 2, h % 2
                if v % 8 == 0:
                    pe.wait_ge(s_pl, 4 * g + 3 + h // 2)
                    if h == 0:
                        pe.wait_ge(s_sw[par], 32 * (g // 2 + 1))
                if u >= 2:
                    pe.wait_ge(s_ex, u - 1)
                keys = (ka if half == br else kb)[par]
                rows = slice(half * HD, (half + 1) * HD)
                n, b = (i + 1) * P, BS + u % 2
                mm3(ps[:, b, 0:n], qh[par][rows, h // 2, i * P:n], ql[par][rows, h // 2, i * P:n],
                    keys[rows, 0, 0:n], keys[rows, 1, 0:n], True, False)
                mask(b, i).then_inc(s_sc, 1)

            def cmp_scores(H):
                g, h = H // 4, H % 4
                rows = slice(h % 2 * HD, h % 2 * HD + HD)
                pe.wait_ge(s_pl, max(4, min(H + 3, NSA_ITEMS)))
                pe.wait_ge(s_pf, 4 * g + 3 + h // 2)
                for i in range(QT):
                    last = nc.tensor.matmul(ps[:, BX, i * NCMP:(i + 1) * NCMP], qf[g % 2][rows, h // 2, i * P:(i + 1) * P],
                                            kcd[rows, g * NCMP:(g + 1) * NCMP], start=True, stop=True)
                last.then_inc(s_cs, 1)

            def cmp_turn(H):
                pe.wait_ge(s_cp, H + 1)
                for i in range(QT):
                    last = nc.tensor.transpose(ps[0:NCMP, BX, i * P:(i + 1) * P], csm[:, i, :], ident[:, :])
                last.then_inc(s_ct, 1)

            def turn(u, loc):
                pe.wait_ge(s_pr, u + 1)
                if not isinstance(u, int) or u >= 2:
                    pe.wait_ge(s_ptl, u - 1)
                for kt in range(loc[1] + 1):
                    last = nc.tensor.transpose(ps[:, BT + loc[0] % 2, kt * P:(kt + 1) * P], prob[:, loc[0] % 4, kt * P:(kt + 1) * P], ident[:, :])
                last.then_inc(s_pt, 1)

            def pv(u, loc, bank, v_h, v_l, start, stop):
                pe.wait_ge(s_ptl, u + 1)
                i, b = loc[1], loc[0] % 2
                o = ps[0:HD, bank, i * P:(i + 1) * P]
                for kt in range(i + 1):
                    last = mm3(o, v_h[:, kt, :], v_l[:, kt, :], pth[:, b, kt * P:(kt + 1) * P], ptl[:, b, kt * P:(kt + 1) * P],
                               start and kt == 0, stop and kt == i)
                last.then_inc(s_pv, 1)

            def nsa_pv(u):
                g, v = u // 32, u % 32
                h, i, br = v // 8, v % 8 // 2, v % 2
                H = 4 * g + h
                bank = BO + H % 2
                if v % 8 == 0:
                    if H >= 2:
                        pe.wait_ge(s_ol, H - 1)
                    pe.wait_ge(s_cc, H + 1)
                if br == 0:
                    nc.tensor.matmul(ps[0:HD, bank, i * P:(i + 1) * P], vcd[:, g, :], pct[0:NCMP, H % 2, i * P:(i + 1) * P], start=True, stop=False)
                cs = slice(br * HD, (br + 1) * HD)
                pv(u, (u, i), bank, vh[g % 2][:, :, cs], vl[g % 2][:, :, cs], False, br == 1)

            pe.wait_ge(s_cst, 2)
            pe.wait_ge(s_cmpr, 2)
            pe.wait_ge(s_vc, 4)
            pe.wait_ge(s_ge, 4)
            cmp_scores(0)
            nsa_scores(0)
            nsa_scores(1)
            for g in range(GROUPS):
                for v in range(32):
                    u = 32 * g + v
                    if v % 8 == 0:
                        cmp_turn(u // 8)
                    if v % 8 == 6 and u + 2 < NSA_UNITS:
                        cmp_scores((u + 2) // 8)
                    if u + 2 < NSA_UNITS:
                        nsa_scores(u + 2)
                    if g < GROUPS - 1:
                        n = 4 * (g + 1) + v // 8
                        if v % 8 == 0:
                            pe.wait_ge(s_pf, n)
                        kstep(4 + n, (4 + n) % R, v % 8)
                    turn(u, (u, v % 8 // 2))
                    if u:
                        nsa_pv(u - 1)
                    if v % 8 == 2 and (v > 2 and g < GROUPS - 1 or v == 2 and g > 0):
                        pe.wait_ge(s_cc, u // 8 + 1)
                        item_turn(*((g + 1, v // 8 - 1) if v > 2 else (g, 3)))
            nsa_pv(NSA_UNITS - 1)

            def out_pe(c0, heads, zb, oh, ol):
                pe.wait_ge(s_ol, heads)

                def one(j, ca, i, step):
                    bank = (ca - c0) % 3
                    pe.wait_ge(s_z1, zb + j - 2)
                    chunk(ca + step * i if step else ca, ca % R, bank, oh, ol)

                with pe.Fori(0, 2) as i:
                    for r in range(3):
                        one(3 * i + r, c0 + r, i, 3)
                for j in range(6, KB):
                    one(j, c0 + j, 0, 0)

            def ln_pe(n):
                pe.wait_ge(s_ld[2], 16)
                pe.wait_ge(s_zs, 8 * (n + 1))
                nc.tensor.matmul(ps[:, 6, :], onesd[:, :], zsum, start=True, stop=True).then_inc(s_mean, 1)
                for k in range(KB):
                    pe.wait_ge(s_sq, 8 * n + k + 1)
                    nc.tensor.matmul(ps[:, 7, :], onesd[:, :], sq[:, k % 2, :], start=(k == 0), stop=(k == KB - 1)).then_inc(s_var, 1)

            def ffn_pe(l, c_up, c_dn, fresh, zb):
                for r in range(2):
                    chunk(c_up + r, (c_up + r) % R, r, xh, xl, fresh=fresh if r == 0 else None)
                with pe.Fori(0, (FB - 1) // 3) as i:
                    for r in range(3):
                        for b in range(2):
                            c = c_up + 2 + 2 * r + b
                            chunk(c + 6 * i, c % R, (c - c_up) % 6, xh, xl)
                pe.wait_ge(s_gl, FB * (l + 1))
                with pe.Fori(0, KB // 2) as i:
                    for q in range(2):
                        for r in range(3):
                            c = c_dn + 3 * q + r
                            if r == 0:
                                pe.wait_ge(s_z1, zb + 2 * i + q - 1)
                            chunk(c + 6 * i, c % R, q, gh, gl, k0=8 * r, nk=DN_BLOCKS[r], first=r == 0, final=r == 2)

            out_pe(C_WO0, HEADS, Z0, oh, ol)
            ln_pe(0)
            ffn_pe(0, C_UP0, C_DN0, 8 + 1, Z0 + 8)
            ln_pe(1)

            pe.wait_ge(s_fw, 2)
            pe.wait_ge(s_x, 24)
            for k in range(KB):
                last = mm3(ps[0:HEADS, BX, :], wf_h[:, k, :], wf_l[:, k, :], xh[:, k, :], xl[:, k, :], k == 0, k == KB - 1)
            last.then_inc(s_fp, 1)

            def value_turn(n):
                pe.wait_ge(s_pf, n)
                for m in range(QT):
                    last = nc.tensor.transpose(ps[:, BX, m * P:(m + 1) * P], tmpf[:, m * P:(m + 1) * P], ident[:, :])
                last.then_inc(s_px, 1)

            for r in range(3):
                if r:
                    pe.wait_ge(s_pl, NSA_ITEMS + r)
                for k in range(KB):
                    kstep(C_FOX + r, (C_FOX + r) % R, k)
            pe.wait_ge(s_fd, 6)
            value_turn(NSA_ITEMS + 1)

            def fox_scores(u, v, par, pair, rows_landed):
                h, i = v // 4, v % 4
                if v == 0:
                    pe.wait_ge(s_pl, NSA_ITEMS + 3 * pair + 2)
                    pe.wait_ge(s_bl[par], rows_landed)
                pe.wait_ge(s_ex, u - 1)
                rows = slice(h * HD, (h + 1) * HD)
                n, b = (i + 1) * P, BS + v % 2
                mm3(ps[:, b, 0:n], fqh[par][rows, i * P:n], fql[par][rows, i * P:n], fkh[par][rows, 0:n], fkl[par][rows, 0:n], True, False)
                nc.tensor.matmul(ps[:, b, 0:n], biasq[par][0:4, h, i * P:n], biask[par][0:4, h, 0:n], start=False, stop=False)
                mask(b, i).then_inc(s_sc, 1)

            def fox_pv(u, v, par, pair):
                h, i = v // 4, v % 4
                if i == 0:
                    pe.wait_ge(s_ol, HEADS + 2 * pair + h - 1)
                if v == 0:
                    pe.wait_ge(s_pl, NSA_ITEMS + 3 * pair + 3)
                cs = slice(h * HD, (h + 1) * HD)
                pv(u, (v, i), BO + h, fvh[par][:, :, cs], fvl[par][:, :, cs], True, True)

            def fox_stages(pair, par, rows_next, first=False, more=True):
                U = NSA_UNITS + 8 * pair
                for v in range(8):
                    if v + 2 < 8:
                        fox_scores(U + v + 2, v + 2, par, pair, None)
                    elif more:
                        fox_scores(U + v + 2, v - 6, 1 - par, pair + 1, rows_next)
                    if more:
                        for s in range(*FOX_STEPS[v]):
                            r, k = s // KB, s % KB
                            if k == 0 and r:
                                pe.wait_ge(s_pl, NSA_ITEMS + 3 * (pair + 1) + r)
                            if k == 0 and not r:
                                pe.wait_ge(s_pf, NSA_ITEMS + pair + 1)
                            kstep(C_FOX + 3 * (pair + 1) + r, (C_FOX + r) % R, k)
                    turn(U + v, (v, v % 4))
                    if v == 0 and not first:
                        pe.wait_ge(s_pl, NSA_ITEMS + 3 * pair)
                        value_turn(NSA_ITEMS + pair + 1)
                    if v:
                        fox_pv(U + v - 1, v - 1, par, pair)
                    elif not first:
                        fox_pv(U - 1, 7, 1 - par, pair - 1)

            fox_scores(NSA_UNITS, 0, 0, 0, 32)
            fox_scores(NSA_UNITS + 1, 1, 0, 0, None)
            fox_stages(0, 0, 32, first=True)
            with pe.Fori(0, 3) as i:
                for r in range(2):
                    fox_stages(1 + r + 2 * i, (1 + r) % 2, 32 * (2 + i))
            fox_stages(7, 1, None, more=False)
            fox_pv(NSA_UNITS + FOX_UNITS - 1, 7, 1, 7)

            out_pe(C_WO1, 2 * HEADS, Z0 + 16, oh2, ol2)
            ln_pe(2)
            ffn_pe(1, C_UP1, C_DN1, 24 + 1, Z0 + 24)
            ln_pe(3)
            pe.wait_ge(s_y, 32)
            for m in range(QT):
                for half in range(2):
                    for k in range(4):
                        last = nc.tensor.transpose(ps[:, 2 * m + half, k * P:(k + 1) * P], z[:, 4 * half + k, m * P:(m + 1) * P], ident[:, :])
                    last.then_inc(s_yt, 1)

        @block.vector
        def _(dve):
            nc.vector.memset(eps[:, :], EPS).then_inc(s_z1, Z0)
            dve.wait_ge(s_ld[0], 16)
            nc.vector.tensor_copy(identb[:, :], ident[:, :]).then_inc(s_cst, 1)
            for k in range(KB):
                dve.wait_ge(s_xh, k + 1)
                nc.vector.tensor_tensor(xl[:, k, :], ps[:, k, :], xh[:, k, :].bitcast(F32), ALU.subtract).then_inc(s_x, 1)
            dve.wait_ge(s_gw, 1)
            nc.vector.tensor_tensor(wg_l[:, :, :], wg_raw[:, :, :], wg_h[:, :, :].bitcast(F32), ALU.subtract).then_inc(s_gw, 1)
            for n in range(2):
                dve.wait_ge(s_ld[1 + n], 16)
            nc.vector.tensor_copy(causalb[:, :], causal[:, :]).then_inc(s_cst, 1)
            dve.wait_ge(s_ld[4], 16)

            dve.wait_ge(s_gp, 1)
            nc.vector.tensor_tensor(gate[:, :, :], ps[:, 5, 0:QT * NG].rearrange("p (m n) -> p m n", m=QT),
                                    bgate[:, :].unsqueeze(1).to_broadcast([P, QT, NG]), ALU.add).then_inc(s_ge, 1)
            dve.wait_ge(s_vt, 2)
            nc.vector.tensor_copy(vecs[:, :], ps[:, 6, 0:68]).then_inc(s_vc, 1)
            nc.vector.tensor_copy(pe2[:, :], ps[:, 6, 128:128 + LP]).then_inc(s_vc, 1)
            dve.wait_ge(s_vt, 6)
            nc.vector.tensor_copy(conv[:, 0, :, :], ps[:, 7, :].rearrange("p (w c) -> p w c", w=4)[:, :, 0:2 * FB]).then_inc(s_vc, 1)
            dve.wait_ge(s_ge, 2)
            nc.vector.tensor_scalar(gate[:, :, :], gate[:, :, :], 1.0, None, ALU.add).then_inc(s_ge, 1)
            dve.wait_ge(s_ge, 3)
            nc.vector.reciprocal(gate[:, :, :], gate[:, :, :]).then_inc(s_ge, 1)
            for src in range(2):
                dve.wait_ge(s_kc, 2 * src + 2)
                dve.wait_ge(s_vc, 2)
                if src:
                    dve.wait_ge(s_hid, 1)
                for g in range(GROUPS):
                    view = kc2[:, g, :].rearrange("p (n l two) -> p l n two", l=8, two=2)
                    for h in range(2):
                        nc.vector.tensor_tensor(kp[:, 8 * h:8 * h + 8, g * NCMP:(g + 1) * NCMP], view[:, :, h:h + NCMP, 0],
                                                pe2[:, 8 * h:8 * h + 8].unsqueeze(2).to_broadcast([P, 8, NCMP]), ALU.add).then_inc(s_kp, 1)
                if src == 0:
                    dve.wait_ge(s_vt, 10)
                    nc.vector.tensor_copy(conv[:, 1, :, :], ps[:, 7, :].rearrange("p (w c) -> p w c", w=4)[:, :, 0:2 * FB]).then_inc(s_vc, 1)

            dve.wait_ge(s_ld[10], 32)

            def item_lo(g, k):
                n, par = 4 * g + k, g % 2
                dve.wait_ge(s_px, n + 1)
                if k == 1:
                    dve.wait_ge(s_ph, n + 1)
                    nc.vector.tensor_tensor(vl[par][:, :, :], ps[:, BX, :].rearrange("p (m c) -> p m c", m=QT), vh[par][:, :, :].bitcast(F32),
                                            ALU.subtract).then_inc(s_pl, 1)
                    return
                rn = n - (n + 2) // 4
                src = tmpf if k == 0 else qf[par][:, k - 2, :]
                nc.vector.tensor_tensor(rot1, src, cosT[:, :], ALU.mult).then_inc(s_r1, 1)
                nc.vector.tensor_tensor(rot2, ps[:, BX, :], sinT[:, :], ALU.mult).then_inc(s_r2, 1)
                dve.wait_ge(s_r1, rn + 1)
                dve.wait_ge(s_r2, rn + 1)
                nc.vector.tensor_tensor(rot1, rot1, rot2, ALU.add).then_inc(s_r3, 1)
                dve.wait_ge(s_ph, n + 1)
                dh, dl = (ka[par][:, 0, :], ka[par][:, 1, :]) if k == 0 else (qh[par][:, k - 2, :], ql[par][:, k - 2, :])
                nc.vector.tensor_tensor(dl, rot1, dh.bitcast(F32), ALU.subtract).then_inc(s_pl, 1)

            def unit_max(u, loc):
                dve.wait_ge(s_sc, u + 1)
                n = (loc[1] + 1) * P
                nc.vector.tensor_reduce(negmax[:, loc[0] % 4:loc[0] % 4 + 1], ps[:, BS + loc[0] % 2, 0:n], AX.X, ALU.max,
                                        negate=True).then_inc(s_nm, 1)

            def unit_scale(u, loc, gated, gcol=None):
                i, b = loc[1], loc[0] % 4
                n = (i + 1) * P
                dve.wait_ge(s_ex, u + 1)
                nc.vector.reciprocal(rinv[:, b:b + 1], psumrow[:, b:b + 1]).then_inc(s_ri, 1)
                dve.wait_ge(s_ri, u + 1)
                if gated:
                    nc.vector.tensor_scalar(prob[:, b, 0:n], prob[:, b, 0:n], rinv[:, b:b + 1], gate[:, i, gcol:gcol + 1],
                                            ALU.mult, ALU.mult).then_inc(s_pr, 1)
                else:
                    nc.vector.tensor_scalar(prob[:, b, 0:n], prob[:, b, 0:n], rinv[:, b:b + 1], None, ALU.mult).then_inc(s_pr, 1)

            def unit_lo(u, loc):
                dve.wait_ge(s_pth, u + 1)
                n, b = (loc[1] + 1) * P, loc[0] % 2
                nc.vector.tensor_tensor(ptl[:, b, 0:n], ps[:, BT + b, 0:n], pth[:, b, 0:n].bitcast(F32), ALU.subtract).then_inc(s_ptl, 1)

            def head_lo(count, par, half, pair, oh=oh, ol=ol):
                dve.wait_ge(s_oh, count)
                rows = slice(half * HD, (half + 1) * HD)
                sel = (lambda a: a[rows, pair, :]) if isinstance(pair, int) else \
                    (lambda a: a[rows, bass.ds(pair, 1), :].rearrange("p a s -> p (a s)"))
                nc.vector.tensor_tensor(sel(ol), ps[0:HD, BO + par, :], sel(oh).bitcast(F32), ALU.subtract).then_inc(s_ol, 1)

            def cmp_softmax(H):
                dve.wait_ge(s_cs, H + 1)
                if H:
                    dve.wait_ge(s_ct, H)
                nc.vector.tensor_tensor(csm[:, :, :], ps[:, BX, 0:QT * NCMP].rearrange("p (m n) -> p m n", m=QT), cmask[:, :, :],
                                        ALU.add).then_inc(s_cmask, 1)
                dve.wait_ge(s_cmask, H + 1)
                nc.vector.tensor_reduce(cstat[:, 0, :], csm[:, :, :], AX.X, ALU.max).then_inc(s_cmax, 1)
                dve.wait_ge(s_cmax, H + 1)
                nc.vector.tensor_scalar(cstat[:, 1, :], cstat[:, 0, :], FLOOR, None, ALU.max).then_inc(s_cfl, 1)
                dve.wait_ge(s_cfl, H + 1)
                nc.vector.tensor_tensor(csm[:, :, :], csm[:, :, :], cstat[:, 1, :].unsqueeze(2).to_broadcast([P, QT, NCMP]),
                                        ALU.subtract).then_inc(s_cdf, 1)

            def cmp_norm(H):
                dve.wait_ge(s_ce, H + 1)
                nc.vector.tensor_reduce(cstat[:, 2, :], csm[:, :, :], AX.X, ALU.add).then_inc(s_csum, 1)
                dve.wait_ge(s_csum, H + 1)
                nc.vector.tensor_scalar(cstat[:, 2, :], cstat[:, 2, :], 1e-30, None, ALU.max).then_inc(s_csf, 1)
                dve.wait_ge(s_csf, H + 1)
                nc.vector.reciprocal(cstat[:, 3, :], cstat[:, 2, :]).then_inc(s_cinv, 1)
                dve.wait_ge(s_cinv, H + 1)
                nc.vector.tensor_tensor(cstat[:, 3, :], cstat[:, 3, :], gate[:, :, 3 * H], ALU.mult).then_inc(s_cg, 1)
                dve.wait_ge(s_cg, H + 1)
                nc.vector.tensor_tensor(csm[:, :, :], csm[:, :, :], cstat[:, 3, :].unsqueeze(2).to_broadcast([P, QT, NCMP]),
                                        ALU.mult).then_inc(s_cp, 1)

            def cmp_copy(H):
                dve.wait_ge(s_ct, H + 1)
                nc.vector.tensor_copy(pct[0:NCMP, H % 2, :], ps[0:NCMP, BX, :]).then_inc(s_cc, 1)

            for k in range(4):
                item_lo(0, k)
            cmp_softmax(0)
            unit_max(0, (0, 0))
            unit_max(1, (1, 0))
            cmp_norm(0)
            unit_scale(0, (0, 0), True, 1)
            for g in range(GROUPS):
                for v in range(32):
                    u = 32 * g + v
                    if v % 8 == 6 and u + 2 < NSA_UNITS:
                        cmp_softmax((u + 2) // 8)
                    if v % 8 == 7 and u + 1 < NSA_UNITS:
                        cmp_norm((u + 1) // 8)
                    if u + 2 < NSA_UNITS:
                        unit_max(u + 2, (u + 2, (u + 2) % 8 // 2))
                    if u + 1 < NSA_UNITS:
                        unit_scale(u + 1, (u + 1, (u + 1) % 8 // 2), True, 3 * ((u + 1) // 8) + 1 + (u + 1) % 2)
                    if v % 8 == 0:
                        cmp_copy(u // 8)
                    unit_lo(u, (u, v % 8 // 2))
                    if v % 8 == 1 and u > 8:
                        H = u // 8 - 1
                        head_lo(H + 1, H % 2, H % 2, H // 2)
                    if v % 8 == 3 and (v > 3 and g < GROUPS - 1 or v == 3 and g > 0):
                        item_lo(*((g + 1, v // 8 - 1) if v > 3 else (g, 3)))
            head_lo(HEADS, 1, 1, KB - 1)

            def z_one(c, j, bank, zn):
                xs = lambda a: a[:, bass.ds(j, 1), :].rearrange("p a s -> p (a s)")
                dve.wait_ge(s_wu, c + 1)
                nc.vector.scalar_tensor_tensor(out=xs(z), in0=xs(xh).bitcast(F32), scalar=ALPHA, in1=ps[:, bank, :],
                                               op0=ALU.mult, op1=ALU.add).then_inc(s_z1, 1)
                dve.wait_ge(s_z1, Z0 + zn + 1)
                nc.vector.scalar_tensor_tensor(out=xs(z), in0=xs(xl).bitcast(F32), scalar=ALPHA, in1=xs(z),
                                               op0=ALU.mult, op1=ALU.add).then_inc(s_z2, 1)
                dve.wait_ge(s_z2, zn + 1)
                nc.vector.tensor_tensor(zsum, zsum, xs(z), ALU.add).then_inc(s_zs, 1)

            def out_dve(c0, n):
                nc.vector.memset(zsum, 0.0).then_inc(s_zs0, 1)
                dve.wait_ge(s_zs0, n + 1)
                with dve.Fori(0, 2) as i:
                    for r in range(3):
                        z_one(c0 + 3 * i + r, 3 * i + r, r, 8 * n + 3 * i + r)
                for j in range(6, KB):
                    z_one(c0 + j, j, j % 3, 8 * n + j)

            def ln_dve(n, final):
                dve.wait_ge(s_mean, n + 1)
                for k in range(KB):
                    nc.vector.tensor_tensor(z[:, k, :], z[:, k, :], ps[:, 6, :], ALU.subtract).then_inc(s_cent, 1)
                dve.wait_ge(s_std, n + 1)
                nc.vector.reciprocal(rstd, std).then_inc(s_rstd, 1)
                dve.wait_ge(s_rstd, n + 1)
                dve.wait_ge(s_cent, 8 * (n + 1))
                for k in range(KB + 1):
                    if k < KB:
                        nc.vector.tensor_tensor(z[:, k, :], z[:, k, :], rstd, ALU.mult).then_inc(s_nrm, 1)
                    if k and not final:
                        dve.wait_ge(s_xh, 8 * (n + 1) + k)
                        nc.vector.tensor_tensor(xl[:, k - 1, :], z[:, k - 1, :], xh[:, k - 1, :].bitcast(F32), ALU.subtract).then_inc(s_x, 1)

            def ffn_dve(l, c_up, c_dn, n):
                def taps(buf, j, blk, bank, c2):
                    dve.wait_ge(s_c0, c2 + 1)
                    nc.vector.scalar_tensor_tensor(out=buf[:, 1:SEQ], in0=ps[:, bank, 0:SEQ - 1], scalar=conv[:, l, 1, bass.ds(blk, 1)],
                                                   in1=buf[:, 1:SEQ], op0=ALU.mult, op1=ALU.add).then_inc(s_c1, 1)
                    dve.wait_ge(s_c1, c2 + 1)
                    nc.vector.scalar_tensor_tensor(out=buf[:, 2:SEQ], in0=ps[:, bank, 0:SEQ - 2], scalar=conv[:, l, 0, bass.ds(blk, 1)],
                                                   in1=buf[:, 2:SEQ], op0=ALU.mult, op1=ALU.add).then_inc(s_c2, 1)

                def pair(j, bank):
                    jj = FB * l + j
                    taps(ua, j, j, bank, 2 * jj)
                    taps(ub, j, FB + j, bank + 1, 2 * jj + 1)
                    dve.wait_ge(s_gelu, jj + 1)
                    dve.wait_ge(s_c2, 2 * jj + 2)
                    nc.vector.tensor_tensor(gf, ga, ub, ALU.mult).then_inc(s_g, 1)
                    dve.wait_ge(s_gh, jj + 1)
                    sel = lambda a: a[:, bass.ds(j, 1), :].rearrange("p a s -> p (a s)")
                    nc.vector.tensor_tensor(sel(gl), gf, sel(gh).bitcast(F32), ALU.subtract).then_inc(s_gl, 1)

                pair(0, 0)
                with dve.Fori(0, (FB - 1) // 3) as i:
                    for r in range(3):
                        pair(1 + 3 * i + r, (2 + 2 * r) % 6)
                nc.vector.memset(zsum, 0.0).then_inc(s_zs0, 1)
                dve.wait_ge(s_zs0, n + 1)
                with dve.Fori(0, KB // 2) as i:
                    for q in range(2):
                        z_one(c_dn + 6 * i + 3 * q + 2, 2 * i + q, q, 8 * n + 2 * i + q)

            out_dve(C_WO0, 0)
            ln_dve(0, False)
            ffn_dve(0, C_UP0, C_DN0, 1)
            ln_dve(1, False)

            nc.vector.memset(fone[:, :], 1.0).then_inc(s_fd, 1)
            for par in range(2):
                nc.vector.memset(biasq[par][0:4, :, :].bitcast(F32), 1.0).then_inc(s_fd, 1)
                nc.vector.memset(biask[par][0:4, :, :].bitcast(F32), 1.0).then_inc(s_fd, 1)
            dve.wait_ge(s_fw, 1)
            nc.vector.tensor_tensor(wf_l[:, :, :], wf_raw[:, :, :], wf_h[:, :, :].bitcast(F32), ALU.subtract).then_inc(s_fw, 1)
            hs = slice(0, HEADS)
            dve.wait_ge(s_fp, 1)
            nc.vector.tensor_scalar(fz[hs, :], ps[hs, BX, :], bf[:, 0:1], None, ALU.add).then_inc(s_fd, 1)
            dve.wait_ge(s_fa, 2)
            nc.vector.tensor_scalar(fe[hs, :], fe[hs, :], 1.0, None, ALU.add).then_inc(s_fd, 1)
            dve.wait_ge(s_fa, 3)
            dve.wait_ge(s_fd, 7)
            nc.vector.scalar_tensor_tensor(out=fz[hs, :], in0=fz[hs, :], scalar=0.0, in1=fe[hs, :], op0=ALU.min, op1=ALU.subtract).then_inc(s_fd, 1)
            dve.wait_ge(s_fd, 8)
            nc.vector.tensor_tensor_scan(fcum[hs, :], fone[hs, :], fz[hs, :], 0.0, ALU.mult, ALU.add).then_inc(s_fd, 1)
            dve.wait_ge(s_fa, 4)
            dve.wait_ge(s_fd, 9)
            nc.vector.tensor_tensor(cstack[hs, 1, :], fcum[hs, :], cstack[hs, 0, :].bitcast(F32), ALU.subtract).then_inc(s_fd, 1)
            nc.vector.tensor_scalar(cstack[hs, 2, :], cstack[hs, 0, :].bitcast(F32), -1.0, None, ALU.mult).then_inc(s_fd, 1)
            dve.wait_ge(s_fd, 10)
            nc.vector.tensor_scalar(cstack[hs, 3, :], cstack[hs, 1, :].bitcast(F32), -1.0, None, ALU.mult).then_inc(s_fd, 1)

            def fox_lo(par, r, n):
                dve.wait_ge(s_ph, n + 1)
                if r == 0:
                    nc.vector.scalar_tensor_tensor(out=fql[par][:, :], in0=ps[:, BP, :], scalar=SCALE, in1=fqh[par][:, :].bitcast(F32),
                                                   op0=ALU.mult, op1=ALU.subtract).then_inc(s_pl, 1)
                elif r == 1:
                    nc.vector.tensor_tensor(fkl[par][:, :], ps[:, BP, :], fkh[par][:, :].bitcast(F32), ALU.subtract).then_inc(s_pl, 1)
                else:
                    nc.vector.tensor_tensor(fvl[par][:, :, :], ps[:, BX, :].rearrange("p (m c) -> p m c", m=QT), fvh[par][:, :, :].bitcast(F32),
                                            ALU.subtract).then_inc(s_pl, 1)

            for r in range(3):
                fox_lo(0, r, NSA_ITEMS + r)
            unit_max(NSA_UNITS, (0, 0))
            unit_max(NSA_UNITS + 1, (1, 1))
            unit_scale(NSA_UNITS, (0, 0), False)

            def fox_stages(pair, par, first=False, more=True):
                U = NSA_UNITS + 8 * pair
                for v in range(8):
                    if more or v + 2 < 8:
                        unit_max(U + v + 2, (v + 2, (v + 2) % 4))
                    if more or v + 1 < 8:
                        unit_scale(U + v + 1, (v + 1, (v + 1) % 4), False)
                    unit_lo(U + v, (v, v % 4))
                    if v == 0 and not first:
                        fox_lo(par, 2, NSA_ITEMS + 3 * pair + 2)
                    if v == 1 and not first:
                        head_lo(HEADS + 2 * pair, 1, 1, pair - 1, oh2, ol2)
                    if v == 5:
                        head_lo(HEADS + 2 * pair + 1, 0, 0, pair, oh2, ol2)
                    if more and v in (2, 5):
                        fox_lo(1 - par, v // 4, NSA_ITEMS + 3 * (pair + 1) + v // 4)

            fox_stages(0, 0, first=True)
            with dve.Fori(0, 3) as i:
                for r in range(2):
                    fox_stages(1 + r + 2 * i, (1 + r) % 2)
            fox_stages(7, 1, more=False)
            head_lo(2 * HEADS, 1, 1, KB - 1, oh2, ol2)

            out_dve(C_WO1, 2)
            ln_dve(2, False)
            ffn_dve(1, C_UP1, C_DN1, 3)
            ln_dve(3, True)
            for m in range(QT):
                dve.wait_ge(s_yt, 2 * m + 2)
                nc.vector.tensor_copy(onat[:, m, 512:1024], ps[:, 2 * m + 1, :]).then_inc(s_yd, 1)


_INS = ["x", "nsa_w_in", "nsa_b_gate", "nsa_pe", "nsa_phik_w1", "nsa_phik_b1", "nsa_phik_w2", "nsa_phiv_w1", "nsa_phiv_b1",
        "nsa_phiv_w2", "nsa_w_o", "fox_w_in", "fox_b_f", "fox_w_o", "ffn_w_up", "ffn_conv_w", "ffn_conv_b", "ffn_w_down",
        "ln1_g", "ln1_b", "ln2_g", "ln2_b"]


def shape_constants():
    import numpy as np
    f = np.float32
    inv = (f(10000.0) ** (-np.arange(0, HD, 2, dtype=f) / f(HD))).astype(f)
    ang = np.arange(SEQ, dtype=f)[:, None] * inv[None, :]
    ang = np.concatenate([ang, ang, ang, ang], axis=1)
    rot = np.zeros((P, P), f)
    for d in range(P):
        if d % HD < HD // 2:
            rot[d + HD // 2, d] = -1.0
        else:
            rot[d - HD // 2, d] = 1.0
    q, k = np.arange(P)[:, None], np.arange(P)[None, :]
    tok = np.arange(QT)[None, :, None] * P + np.arange(P)[:, None, None]
    end = np.arange(NCMP)[None, None, :] * CMP_STRIDE + CMP_LEN - 1
    return {
        "c_ident": np.eye(P, dtype=f), "c_causal": np.where(k <= q, 0.0, NEG).astype(f), "c_ones": np.full((P, P), 1.0 / D, f),
        "c_rot": rot, "c_cmask": np.where(end <= tok, 0.0, NEG).astype(f),
        "c_cos": np.ascontiguousarray(np.cos(ang).T.astype(f)), "c_sin": np.ascontiguousarray(np.sin(ang).T.astype(f)),
    }


def kernel(**inputs):
    import numpy as np
    import concourse.bacc as bacc
    from concourse.bass_utils import run_bass_kernel_spmd

    nc = bacc.Bacc("TRN2", target_bir_lowering=False, num_devices=1)
    arrays, t = {}, {}
    for name, a in [(n, inputs[n]) for n in _INS] + list(shape_constants().items()):
        a = np.ascontiguousarray(a)
        arrays[f"in_{name}"] = a
        t[name] = nc.dram_tensor(f"in_{name}", a.shape, F32, kind="ExternalInput").ap()
    t["cum"] = nc.dram_tensor("cum", (4, HEADS, SEQ), F32, kind="Internal").ap()
    out = nc.dram_tensor("out_0", (1, SEQ, D), F32, kind="ExternalOutput").ap()
    build_trunk(nc, t, out)
    r = run_bass_kernel_spmd(nc, [arrays], core_ids=[0])
    return r.results[0]["out_0"]
```

```python
from contextlib import ExitStack

import concourse.bass as bass
from concourse import mybir

F32 = mybir.dt.float32
F32R = mybir.dt.float32r
BF16 = mybir.dt.bfloat16
ALU = mybir.AluOpType
ACT = mybir.ActivationFunctionType
AX = mybir.AxisListType

P = 128
D, SEQ, DEPTH = 1024, 512, 2
HD = 64
HEADS = D // HD
GROUPS, REP = 4, 4
KV = GROUPS * HD
CMP_LEN, CMP_STRIDE, PHI = 32, 16, 256
NCMP = (SEQ - CMP_LEN) // CMP_STRIDE + 1
NG = 3 * HEADS
FF = 2816
FB = FF // P
KB = D // P
QT = SEQ // P
LP = CMP_LEN // 2
ALPHA = (2 * DEPTH) ** 0.25
EPS = 1e-5
SCALE = HD ** -0.5
NEG = -1e30
FLOOR = -1e28

R = 3
C_NSA = 0
C_WO0 = C_NSA + 4 + 4 * GROUPS
C_UP0 = C_WO0 + KB
C_DN0 = C_UP0 + 2 * FB
C_FOX = C_DN0 + 3 * KB
C_WO1 = C_FOX + 3 * KB
C_UP1 = C_WO1 + KB
C_DN1 = C_UP1 + 2 * FB
C_END = C_DN1 + 3 * KB
DN_BLOCKS = (8, 8, FB - 16)

NSA_UNITS = HEADS * QT * 2
FOX_UNITS = HEADS * QT
NSA_ITEMS = 4 * GROUPS
Z0 = 8
FOX_STEPS = [(0, 4), (4, 8), (8, 11), (11, 14), (14, 16), (16, 18), (18, 21), (21, 24)]
XL_DVE = (4, 7)
XL_POOL = tuple(k for k in range(KB) if k not in XL_DVE)


def build_trunk(nc, t, out):
    with ExitStack() as ctx:
        def sb(name, shape, dt=F32):
            return ctx.enter_context(nc.sbuf_tensor(name, shape, dt))

        def sem(name):
            return ctx.enter_context(nc.semaphore(name))

        xh = sb("xh", [P, KB, SEQ], F32R)
        xl = sb("xl", [P, KB, SEQ], F32R)
        raw = sb("raw", [P, R, KB, P])
        wh = sb("wh", [P, R, KB, P], F32R)
        wl = sb("wl", [P, R, KB, P], F32R)
        work = sb("work", [P, 5 * SEQ])
        ident = sb("ident", [P, P])
        identb = sb("identb", [P, P], BF16)
        causal = sb("causal", [P, P])
        causalb = sb("causalb", [P, P], BF16)
        onesd = sb("onesd", [P, P])
        rotm = sb("rotm", [P, P])
        cmask = sb("cmask", [P, QT, NCMP])
        conv_nat = sb("conv_nat", [FB * 2, 4, P])
        vec_nat = sb("vec_nat", [68, P])
        pe_nat = sb("pe_nat", [LP, P])
        conv = sb("conv", [P, DEPTH, 4, 2 * FB])
        vecs = sb("vecs", [P, 68])
        pe2 = sb("pe2", [P, LP])
        eps = sb("eps", [P, 1])
        bgate = sb("bgate", [P, NG])
        gate = sb("gate", [P, QT, NG])
        kcd = sb("kcd", [P, GROUPS * NCMP])
        vcd = sb("vcd", [NCMP, GROUPS, HD])
        ghid = sb("ghid", [P, 2, GROUPS * NCMP])
        w2k = sb("w2k", [P, 2, HD])
        w2v = sb("w2v", [P, 2, HD])
        negmax = sb("negmax", [P, 4])
        psumrow = sb("psumrow", [P, 4])
        rinv = sb("rinv", [P, 4])
        csm = sb("csm", [P, QT, NCMP])
        cstat = sb("cstat", [P, 4, QT])
        bf = sb("bf", [HEADS, 1])
        ps = ctx.enter_context(nc.psum_tensor("ps", [P, 8, 512], F32))

        def overlay(*phases):
            made = []
            for n, phase in enumerate(phases):
                stay = ctx if n == len(phases) - 1 else ExitStack()
                made.append([stay.enter_context(nc.sbuf_tensor(name, shape, dt)) for name, shape, dt in phase])
                if stay is not ctx:
                    stay.close()
            return made

        (prob, pth, ptl), (cstack,), (z,) = overlay(
            [("prob", [P, 4, SEQ], F32), ("pth", [P, 2, SEQ], F32R), ("ptl", [P, 2, SEQ], F32R)],
            [("cstack", [P, 4, SEQ], F32R)],
            [("z", [P, KB, SEQ], F32)])

        def parities(names):
            return [(f"{name}{p}", shape, dt) for p in range(2) for name, shape, dt in names]

        o_parts = [("oh{}", [P, KB, SEQ], F32R), ("ol{}", [P, KB, SEQ], F32R)]
        nsa_state = [("qh", [P, 2, SEQ], F32R), ("ql", [P, 2, SEQ], F32R), ("ka", [P, 2, SEQ], F32R),
                     ("kb", [P, 2, SEQ], F32R), ("vh", [P, QT, P], F32R), ("vl", [P, QT, P], F32R), ("qf", [P, 2, SEQ], F32)]
        fox_state = [("fqh", [P, SEQ], F32R), ("fql", [P, SEQ], F32R), ("fkh", [P, SEQ], F32R), ("fkl", [P, SEQ], F32R),
                     ("fvh", [P, QT, P], F32R), ("fvl", [P, QT, P], F32R), ("biasq", [P, 2, SEQ], F32R), ("biask", [P, 2, SEQ], F32R)]
        prologue, nsa, fox, (onat,), (gh, gl) = overlay(
            [("w1k", [P, LP, PHI], F32), ("w1v", [P, LP, PHI], F32), ("parity0", [P, 12 * SEQ], F32),
             ("kc2", [P, GROUPS, SEQ], F32), ("kp", [P, LP, GROUPS * NCMP], F32),
             ("wg_raw", [P, KB, NG], F32), ("wg_h", [P, KB, NG], F32R), ("wg_l", [P, KB, NG], F32R)],
            [("oh", [P, KB, SEQ], F32R), ("ol", [P, KB, SEQ], F32R)] + parities(nsa_state)
            + [("cosT", [P, SEQ], F32), ("sinT", [P, SEQ], F32)],
            [("oh2", [P, KB, SEQ], F32R), ("ol2", [P, KB, SEQ], F32R)] + parities(fox_state)
            + [("wf_raw", [P, KB, HEADS], F32), ("wf_h", [P, KB, HEADS], F32R), ("wf_l", [P, KB, HEADS], F32R),
               ("fz", [P, SEQ], F32), ("fe", [P, SEQ], F32), ("fone", [P, SEQ], F32), ("fcum", [P, SEQ], F32)],
            [("onat", [P, QT, D], F32)],
            [("gh", [P, FB, SEQ], F32R), ("gl", [P, FB, SEQ], F32R)])
        w1k, w1v, _, kc2, kp, wg_raw, wg_h, wg_l = prologue
        oh, ol = nsa[0:2]
        qh, ql, ka, kb, vh, vl, qf = ([nsa[2 + n], nsa[9 + n]] for n in range(7))
        cosT, sinT = nsa[16:18]
        oh2, ol2 = fox[0:2]
        fqh, fql, fkh, fkl, fvh, fvl, biasq, biask = ([fox[2 + n], fox[10 + n]] for n in range(8))
        wf_raw, wf_h, wf_l, fz, fe, fone, fcum = fox[18:25]
        xnat = z[:, :, :].rearrange("p (m a) s -> p m (a s)", m=QT)
        tmpf, rot1, rot2 = (work[:, n * SEQ:(n + 1) * SEQ] for n in range(3))
        pct = work[:, 3 * SEQ:5 * SEQ].rearrange("p (a s) -> p a s", a=2)
        ua, ub, ga, gf = (work[:, n * SEQ:(n + 1) * SEQ] for n in range(4))
        zsum = work[:, 4 * SEQ:5 * SEQ]
        sq = work[:, 0:4 * SEQ].rearrange("p (a s) -> p a s", a=4)
        std = zsum
        rstd = work[:, 1 * SEQ:2 * SEQ]

        BP, BX, BS, BT, BO = 0, 1, 2, 4, 6

        s_raw = [sem(f"raw_landed{n}") for n in range(R)]
        s_wh = sem("w_hi")
        s_wl = sem("w_lo")
        s_wu = sem("w_used")
        s_ld = [sem(f"loaded{n}") for n in range(12)]
        s_cst = sem("consts_ready")
        s_vt = sem("vectors_turned")
        s_vc = sem("vectors_ready")
        s_xn = [sem(f"x_landed{n}") for n in range(QT)]
        s_xt = sem("x_turned")
        s_xh = sem("x_hi")
        s_x = sem("x_lo")
        s_xp = sem("x_lo_pool")
        s_gw = sem("gate_w_split")
        s_gp = sem("gate_products")
        s_ge = sem("gate_steps")
        s_kc = sem("cmp_source")
        s_kp = sem("cmp_blocks")
        s_hid = sem("cmp_hidden")
        s_gel = sem("cmp_gelu")
        s_cmpo = sem("cmp_out")
        s_cmpr = sem("cmp_ready")
        s_pf = sem("proj_copied")
        s_px = sem("proj_turned")
        s_r1 = sem("rope_cos")
        s_r2 = sem("rope_sin")
        s_r3 = sem("rope_sum")
        s_ph = sem("proj_hi")
        s_pl = sem("proj_lo")
        s_sw = [sem(f"keys_swapped{p}") for p in range(2)]
        s_sc = sem("scores")
        s_nm = sem("neg_max")
        s_ex = sem("exps")
        s_ri = sem("sum_inverse")
        s_pr = sem("probs")
        s_pt = sem("probs_turned")
        s_pth = sem("pt_hi")
        s_ptl = sem("pt_lo")
        s_pv = sem("pv_done")
        s_oh = sem("o_hi")
        s_ol = sem("o_lo")
        s_cs = sem("cmp_scores")
        s_cmask = sem("cmp_masked")
        s_cmax = sem("cmp_max")
        s_cfl = sem("cmp_max_finite")
        s_cdf = sem("cmp_differences")
        s_csum = sem("cmp_sum")
        s_csf = sem("cmp_sum_floored")
        s_cinv = sem("cmp_sum_inverse")
        s_cg = sem("cmp_gated_inverse")
        s_cp = sem("cmp_probs")
        s_ce = sem("cmp_exp")
        s_ct = sem("cmp_probs_turned")
        s_cc = sem("cmp_probs_copied")
        s_fw = sem("forget_w_split")
        s_fp = sem("forget_products")
        s_fa = sem("forget_act_steps")
        s_fd = sem("forget_dve_steps")
        s_cd = sem("cum_stored")
        s_bl = [sem(f"cum_rows{p}") for p in range(2)]
        s_c0 = sem("conv_tap2")
        s_c1 = sem("conv_tap1")
        s_c2 = sem("conv_tap0")
        s_gelu = sem("gelu")
        s_g = sem("gated")
        s_gh = sem("gated_hi")
        s_gl = sem("gated_lo")
        s_zs0 = sem("zsum_cleared")
        s_z1 = sem("z_first")
        s_z2 = sem("z_second")
        s_zs = sem("z_summed")
        s_mean = sem("mean")
        s_cent = sem("centred")
        s_sq = sem("squared")
        s_sp = sem("squares_paired")
        s_var = sem("variance")
        s_std = sem("std")
        s_rstd = sem("rstd")
        s_nrm = sem("normed")
        s_y = sem("affine_dve")
        s_ya = sem("affine_act")
        s_yt = sem("y_turned")
        s_yc = sem("y_copied_act")
        s_yd = sem("y_copied_dve")
        s_out = sem("out_stored")

        block = ctx.enter_context(nc.Block())

        @block.sync
        def _(sp):
            small = [
                (ident[:, :], t["c_ident"]), (causal[:, :], t["c_causal"]), (onesd[:, :], t["c_ones"]),
                (rotm[:, :], t["c_rot"]), (cmask[:, :, :], t["c_cmask"]),
            ]
            for m in range(QT):
                sp.dma_start(xnat[:, m, :], t["x"][0, m * P:(m + 1) * P, :]).then_inc(s_xn[m], 16)
                if m == 0:
                    sp.dma_start(small[0][0], small[0][1]).then_inc(s_ld[0], 16)

            def load(c, slot, src, nk=KB):
                if not isinstance(c, int) or c >= R:
                    sp.wait_ge(s_wl, c - (R - 1))
                sp.dma_start(raw[:, slot, 0:nk, :], src).then_inc(s_raw[slot], 16)

            def cols(w, a):
                return w[:, bass.ds(a, P)].rearrange("(k p) c -> p k c", p=P)

            w_nsa = t["nsa_w_in"][0]
            for c in range(R):
                load(c, c % R, cols(w_nsa, D + c * P))
            sp.dma_start(wg_raw[:, :, :], t["nsa_w_in"][0][:, D + 6 * KV:D + 6 * KV + NG].rearrange("(k p) c -> p k c", p=P)).then_inc(s_ld[6], 16)
            sp.dma_start(bgate[:, :], t["nsa_b_gate"][0].rearrange("(a n) -> a n", a=1).to_broadcast([P, NG])).then_inc(s_ld[6], 16)
            sp.dma_start(pe_nat[:, :], t["nsa_pe"][0].rearrange("(l two) d -> l (two d)", two=2)).then_inc(s_ld[5], 16)
            sp.dma_start(vec_nat[0:16, :], t["ln1_g"].rearrange("l (k p) -> (l k) p", p=P)).then_inc(s_ld[5], 16)
            sp.dma_start(vec_nat[16:32, :], t["ln1_b"].rearrange("l (k p) -> (l k) p", p=P)).then_inc(s_ld[5], 16)
            sp.dma_start(vec_nat[32:48, :], t["ln2_g"].rearrange("l (k p) -> (l k) p", p=P)).then_inc(s_ld[5], 16)
            sp.dma_start(vec_nat[48:64, :], t["ln2_b"].rearrange("l (k p) -> (l k) p", p=P)).then_inc(s_ld[5], 16)
            sp.dma_start(vec_nat[64:66, :], t["nsa_phik_b1"].rearrange("l (k p) -> (l k) p", p=P)).then_inc(s_ld[5], 16)
            sp.dma_start(vec_nat[66:68, :], t["nsa_phiv_b1"].rearrange("l (k p) -> (l k) p", p=P)).then_inc(s_ld[5], 16)
            sp.dma_start(w1k[:, :, :], t["nsa_phik_w1"][0].rearrange("(k p) c -> p k c", p=P)).then_inc(s_ld[8], 16)
            load(3, 3 % R, cols(w_nsa, D + 3 * P))
            sp.dma_start(w2k[:, :, :], t["nsa_phik_w2"][0].rearrange("(k p) c -> p k c", p=P)).then_inc(s_ld[7], 16)
            sp.dma_start(w2v[:, :, :], t["nsa_phiv_w2"][0].rearrange("(k p) c -> p k c", p=P)).then_inc(s_ld[7], 16)
            for n, (dst, src) in enumerate(small[1:]):
                sp.dma_start(dst, src).then_inc(s_ld[1 + n], 16)
            sp.dma_start(w1v[:, :, :], t["nsa_phiv_w1"][0].rearrange("(k p) c -> p k c", p=P)).then_inc(s_ld[9], 16)
            sp.dma_start(cosT[:, :], t["c_cos"]).then_inc(s_ld[10], 16)
            sp.dma_start(sinT[:, :], t["c_sin"]).then_inc(s_ld[10], 16)
            sp.dma_start(conv_nat[:, 0:3, :], t["ffn_conv_w"][0].rearrange("w (b p) -> b w p", p=P)).then_inc(s_ld[11], 16)
            sp.dma_start(conv_nat[:, 3, :], t["ffn_conv_b"][0].rearrange("(b p) -> b p", p=P)).then_inc(s_ld[11], 16)
            wsv = w_nsa[:, D + 2 * KV:D + 6 * KV].rearrange("(k p) (two r) -> p k two r", p=P, two=2)
            for g in range(GROUPS):
                c = 4 + 4 * g
                for n, r0 in ((0, 0), (1, KV)):
                    sp.wait_ge(s_wl, c + n - (R - 1))
                    for b in range(2):
                        sp.dma_start(raw[:, (c + n) % R, :, b * HD:(b + 1) * HD],
                                     wsv[:, :, b, r0 + g * HD:r0 + (g + 1) * HD]).then_inc(s_raw[(c + n) % R], 16)
                for n in range(2):
                    load(c + 2 + n, (c + 2 + n) % R, cols(w_nsa, g * REP * HD + n * P))
                if g == 0:
                    sp.wait_ge(s_vt, 6)
                    sp.dma_start(conv_nat[:, 0:3, :], t["ffn_conv_w"][1].rearrange("w (b p) -> b w p", p=P)).then_inc(s_ld[11], 16)
                    sp.dma_start(conv_nat[:, 3, :], t["ffn_conv_b"][1].rearrange("(b p) -> b p", p=P)).then_inc(s_ld[11], 16)

            def load_out(c0, w):
                with sp.Fori(0, 2) as i:
                    for r in range(3):
                        load(c0 + 3 * i + r, (c0 + r) % R, cols(w, (3 * i + r) * P))
                for j in range(6, KB):
                    load(c0 + j, (c0 + j) % R, cols(w, j * P))

            def load_ffn(l, c_up, c_dn):
                up, dn = t["ffn_w_up"][l], t["ffn_w_down"][l]
                load(c_up, c_up % R, cols(up, 0))
                load(c_up + 1, (c_up + 1) % R, cols(up, FF))
                with sp.Fori(0, (FB - 1) // 3) as i:
                    for r in range(3):
                        c = c_up + 2 + 2 * r
                        load(c + 6 * i, c % R, cols(up, (1 + 3 * i + r) * P))
                        load(c + 1 + 6 * i, (c + 1) % R, cols(up, FF + (1 + 3 * i + r) * P))
                with sp.Fori(0, KB) as i:
                    for r in range(3):
                        nk = DN_BLOCKS[r]
                        src = dn[r * 8 * P:(r * 8 + nk) * P, bass.ds(i * P, P)].rearrange("(k p) c -> p k c", p=P)
                        load(c_dn + 3 * i + r, (c_dn + r) % R, src, nk)

            load_out(C_WO0, t["nsa_w_o"][0])
            load_ffn(0, C_UP0, C_DN0)

            w_fox = t["fox_w_in"][0]
            for r in range(3):
                load(C_FOX + r, (C_FOX + r) % R, cols(w_fox, r * D))
            sp.wait_ge(s_wu, C_FOX)
            sp.dma_start(wf_raw[:, :, :], w_fox[:, 3 * D:3 * D + HEADS].rearrange("(k p) c -> p k c", p=P)).then_inc(s_ld[6], 16)
            sp.dma_start(bf[:, :], t["fox_b_f"].rearrange("a h -> h a")).then_inc(s_ld[6], 16)
            sp.wait_ge(s_fd, 12)
            sp.dma_start(t["cum"].rearrange("r h s -> h r s"), cstack[0:HEADS, :, :].bitcast(F32)).then_inc(s_cd, 16)
            sp.wait_ge(s_cd, 16)

            def load_rows(pair, par, used):
                if used is not None:
                    sp.wait_ge(s_sc, used)
                sp.dma_start(biasq[par][2:4, :, :].bitcast(F32), t["cum"][0:2, bass.ds(2 * pair, 2), :]).then_inc(s_bl[par], 16)
                sp.dma_start(biask[par][0:2, :, :].bitcast(F32), t["cum"][2:4, bass.ds(2 * pair, 2), :]).then_inc(s_bl[par], 16)

            load_rows(0, 0, None)
            load_rows(1, 1, None)
            for r in range(3):
                load(C_FOX + 3 + r, (C_FOX + r) % R, cols(w_fox, P + r * D))
            with sp.Fori(0, 3) as i:
                for par in range(2):
                    pair = 2 * i + par + 2
                    for r in range(3):
                        load(C_FOX + 3 * pair + r, (C_FOX + r) % R, cols(w_fox, pair * P + r * D))
                    load_rows(pair, par, NSA_UNITS + 8 * (2 * i + par + 1))
            load_out(C_WO1, t["fox_w_o"][0])
            load_ffn(1, C_UP1, C_DN1)
            for n in range(2 * QT):
                m, half = n % QT, n // QT
                sp.wait_ge((s_yc, s_yd)[m % 2], n // 2 + 1)
                sp.dma_start(out[0, m * P:(m + 1) * P, half * 512:(half + 1) * 512],
                             onat[:, m, half * 512:(half + 1) * 512]).then_inc(s_out, 16)
            sp.wait_ge(s_out, 16 * 2 * QT)

        @block.gpsimd
        def _(pool):
            def lo(c, slot, nk=KB):
                pool.wait_ge(s_wh, c + 1)
                nc.gpsimd.tensor_tensor(wl[:, slot, 0:nk, :], raw[:, slot, 0:nk, :],
                                        wh[:, slot, 0:nk, :].bitcast(F32), ALU.subtract).then_inc(s_wl, 1)

            def los(c0, n):
                with pool.Fori(0, n // R) as i:
                    for r in range(R):
                        lo(c0 + R * i + r, (c0 + r) % R)
                for c in range(c0 + n // R * R, c0 + n):
                    lo(c, c % R)

            def los_down(c0):
                with pool.Fori(0, KB) as i:
                    for r in range(R):
                        lo(c0 + R * i + r, (c0 + r) % R, DN_BLOCKS[r])

            def rope_pool(g, k):
                n, par = 4 * g + k, g % 2
                rn = n - (n + 2) // 4
                pool.wait_ge(s_pf, n + 1)
                if g == 0 and k == 0:
                    pool.wait_ge(s_ld[10], 32)
                if n:
                    pool.wait_ge(s_pl, n)
                nc.gpsimd.tensor_tensor(rot1, tmpf if k == 0 else qf[par][:, k - 2, :], cosT[:, :], ALU.mult).then_inc(s_r1, 1)
                pool.wait_ge(s_r1, rn + 1)
                pool.wait_ge(s_r2, rn + 1)
                nc.gpsimd.tensor_tensor(rot1, rot1, rot2, ALU.add).then_inc(s_r3, 1)
                pool.wait_ge(s_ph, n + 1)
                pool.wait_ge(s_r3, rn + 1)
                dh, dl = (ka[par][:, 0, :], ka[par][:, 1, :]) if k == 0 else (qh[par][:, k - 2, :], ql[par][:, k - 2, :])
                nc.gpsimd.tensor_tensor(dl, rot1, dh.bitcast(F32), ALU.subtract).then_inc(s_pl, 1)

            def ln_pool(n, final):
                for m in range(KB // 2):
                    pool.wait_ge(s_sq, 8 * n + 2 * m + 2)
                    a = 2 * (m % 2)
                    nc.gpsimd.tensor_tensor(sq[:, a, :], sq[:, a, :], sq[:, a + 1, :], ALU.add).then_inc(s_sp, 1)
                if final:
                    return
                for k in XL_POOL:
                    pool.wait_ge(s_y, 8 * n + k + 1)
                    nc.gpsimd.tensor_tensor(xl[:, k, :], z[:, k, :], xh[:, k, :].bitcast(F32), ALU.subtract).then_inc(s_xp, 1)

            for c in range(7):
                lo(c, c % R)
            for n in range(NSA_ITEMS):
                if n % 4 != 1:
                    rope_pool(n // 4, n % 4)
                lo(n + 7, (n + 7) % R)
            los(NSA_ITEMS + 7, C_UP0 + 3 - (NSA_ITEMS + 7))
            ln_pool(0, False)
            los(C_UP0 + 3, C_DN0 - (C_UP0 + 3))
            los_down(C_DN0)
            los(C_FOX, 3)
            ln_pool(1, False)
            los(C_FOX + 3, C_UP1 + 3 - (C_FOX + 3))
            ln_pool(2, False)
            los(C_UP1 + 3, C_DN1 - (C_UP1 + 3))
            los_down(C_DN1)
            ln_pool(3, True)

        @block.scalar
        def _(act):
            RAW_EXTRA = [0, 0, 0]
            for g in range(GROUPS):
                for n in range(2):
                    RAW_EXTRA[(4 + 4 * g + n) % R] += 1

            def landed(c):
                return sum(2 if 4 <= x < C_WO0 and (x - 4) % 4 < 2 else 1 for x in range(c + 1) if x % R == c % R)

            def hi(c, slot, nk=KB, n=None):
                act.wait_ge(s_raw[slot], 16 * (landed(c) if n is None else n))
                if not isinstance(c, int) or c >= R:
                    act.wait_ge(s_wu, c - (R - 1))
                nc.scalar.activation(wh[:, slot, 0:nk, :], raw[:, slot, 0:nk, :], ACT.Copy).then_inc(s_wh, 1)

            def hi_at(base, k, i=0, step=0, nk=KB):
                c = base + k
                n = c // R + 1 + RAW_EXTRA[c % R]
                hi(c + step * i if step else c, c % R, nk, n + (step // R) * i if step else n)

            for k in range(KB):
                act.wait_ge(s_xt, k + 1)
                nc.scalar.activation(xh[:, k, :], ps[:, k, :], ACT.Copy).then_inc(s_xh, 1)
                if k == 1:
                    hi(0, 0)
                if k == 4:
                    hi(1, 1)
            hi(2, 2)
            act.wait_ge(s_ld[6], 32)
            nc.scalar.activation(wg_h[:, :, :], wg_raw[:, :, :], ACT.Copy).then_inc(s_gw, 1)

            def cmp_source(c):
                act.wait_ge(s_wu, c + 1)
                if c >= 2:
                    act.wait_ge(s_kp, 8)
                for half in range(2):
                    g = 2 * (c % 2) + half
                    nc.scalar.activation(kc2[0:HD, g, :], ps[half * HD:(half + 1) * HD, c % 2, :], ACT.Copy)
                    last = nc.scalar.activation(kc2[HD:P, g, 0:SEQ - 1], ps[half * HD:(half + 1) * HD, c % 2, 1:SEQ], ACT.Copy)
                last.then_inc(s_kc, 1)

            def cmp_gelu(src):
                act.wait_ge(s_hid, src + 1)
                act.wait_ge(s_vc, 1)
                if src:
                    act.wait_ge(s_cmpo, 1)
                for hb in range(2):
                    last = nc.scalar.activation(ghid[:, hb, :], ps[:, 2, hb * P:hb * P + GROUPS * NCMP], ACT.Gelu_apprx_tanh,
                                                bias=vecs[:, 64 + 2 * src + hb:65 + 2 * src + hb])
                last.then_inc(s_gel, 1)

            for c in range(2):
                cmp_source(c)
                hi(c + 3, (c + 3) % R)
            act.wait_ge(s_ge, 1)
            nc.scalar.activation(gate[:, :, :], gate[:, :, :], ACT.Exp, scale=-1.0).then_inc(s_ge, 1)
            cmp_source(2)
            hi(5, 5 % R)
            cmp_gelu(0)
            cmp_source(3)
            hi(6, 6 % R)
            act.wait_ge(s_cmpo, 1)
            nc.scalar.activation(kcd[0:HD, :], ps[0:HD, 3, 0:GROUPS * NCMP], ACT.Copy)
            nc.scalar.activation(kcd[HD:P, :], ps[0:HD, 3, 0:GROUPS * NCMP], ACT.Copy).then_inc(s_cmpr, 1)

            def item_copy(g, k):
                n = 4 * g + k
                act.wait_ge(s_wu, 4 + n + 1)
                if n and k < 2:
                    act.wait_ge(s_pl, n)
                if g >= 2:
                    act.wait_ge(s_pv, 32 * (g - 1))
                if k < 2:
                    nc.scalar.activation(tmpf, ps[:, BP, :], ACT.Copy).then_inc(s_pf, 1)
                else:
                    nc.scalar.activation(qf[g % 2][:, k - 2, :], ps[:, BP, :], ACT.Copy, scale=SCALE).then_inc(s_pf, 1)

            def item_hi(g, k):
                n, par = 4 * g + k, g % 2
                if k == 1:
                    act.wait_ge(s_px, n + 1)
                    nc.scalar.activation(vh[par][:, :, :], ps[:, BX, :].rearrange("p (m c) -> p m c", m=QT), ACT.Copy).then_inc(s_ph, 1)
                else:
                    act.wait_ge(s_r3, n - (n + 2) // 4 + 1)
                    dst = ka[par][:, 0, :] if k == 0 else qh[par][:, k - 2, :]
                    nc.scalar.activation(dst, rot1, ACT.Copy).then_inc(s_ph, 1)

            def swap_keys(g):
                par = g % 2
                act.wait_ge(s_pl, 4 * g + 1)
                act.dma_start(kb[par][0:HD, :, :].bitcast(F32), ka[par][HD:P, :, :].bitcast(F32)).then_inc(s_sw[par], 16)
                act.dma_start(kb[par][HD:P, :, :].bitcast(F32), ka[par][0:HD, :, :].bitcast(F32)).then_inc(s_sw[par], 16)

            def unit_exp(u, loc):
                act.wait_ge(s_nm, u + 1)
                if not isinstance(u, int) or u >= 4:
                    act.wait_ge(s_pt, u - 3)
                i = loc[1]
                n = (i + 1) * P
                nc.scalar.activation(prob[:, loc[0] % 4, 0:n], ps[:, BS + loc[0] % 2, 0:n], ACT.Exp,
                                     bias=negmax[:, loc[0] % 4:loc[0] % 4 + 1],
                                     accum_out=psumrow[:, loc[0] % 4:loc[0] % 4 + 1]).then_inc(s_ex, 1)

            def unit_hi(u, loc):
                act.wait_ge(s_pt, u + 1)
                if not isinstance(u, int) or u >= 2:
                    act.wait_ge(s_pv, u - 1)
                n = (loc[1] + 1) * P
                nc.scalar.activation(pth[:, loc[0] % 2, 0:n], ps[:, BT + loc[0] % 2, 0:n], ACT.Copy).then_inc(s_pth, 1)

            def head_hi(u_end, par, half, pair, oh=oh):
                act.wait_ge(s_pv, u_end)
                nc.scalar.activation(oh[half * HD:(half + 1) * HD, pair, :] if isinstance(pair, int) else
                                     oh[half * HD:(half + 1) * HD, bass.ds(pair, 1), :].rearrange("p a s -> p (a s)"),
                                     ps[0:HD, BO + par, :], ACT.Copy).then_inc(s_oh, 1)

            def cmp_exp(H):
                act.wait_ge(s_cdf, H + 1)
                nc.scalar.activation(csm[:, :, :], csm[:, :, :], ACT.Exp).then_inc(s_ce, 1)

            item_copy(0, 0)
            hi(7, 7 % R)
            cmp_gelu(1)
            item_hi(0, 0)
            item_copy(0, 1)
            hi(8, 8 % R)
            act.wait_ge(s_cmpo, 2)
            nc.scalar.activation(vcd[:, :, :], ps[0:NCMP, 4, 0:GROUPS * HD].rearrange("p (g d) -> p g d", g=GROUPS), ACT.Copy).then_inc(s_cmpr, 1)
            item_hi(0, 1)
            swap_keys(0)
            item_copy(0, 2)
            hi(9, 9 % R)
            item_hi(0, 2)
            cmp_exp(0)
            item_copy(0, 3)
            for g in range(GROUPS):
                for v in range(32):
                    u, w = 32 * g + v, v % 8
                    item = (g, 3) if v < 8 else (g + 1, v // 8 - 1)
                    turned = v < 8 or g < GROUPS - 1
                    for x in ([0, 1, 2] if u == 0 else [v + 2]):
                        uu = 32 * g + x
                        if uu < NSA_UNITS:
                            unit_exp(uu, (uu, uu % 8 // 2))
                    if w == 0:
                        act.wait_ge(s_ct, u // 8 + 1)
                        nc.scalar.activation(pct[0:NCMP, u // 8 % 2, :], ps[0:NCMP, BX, :], ACT.Copy).then_inc(s_cc, 1)
                    if w == 6 and u + 2 < NSA_UNITS:
                        cmp_exp(u // 8 + 1)
                    if w == 5 and turned and item[1] == 0:
                        swap_keys(item[0])
                    if g < GROUPS - 1 and w == 7:
                        item_copy(g + 1, v // 8)
                    unit_hi(u, (u, w // 2))
                    if w == 1 and u > 8:
                        head_hi(u - 1, (u // 8 - 1) % 2, (u // 8 - 1) % 2, (u // 8 - 1) // 2)
                    if turned and w == (2 if item[1] == 1 else 3):
                        item_hi(*item)
                    if g < GROUPS - 1 and w == 4:
                        c = 4 + 4 * (g + 1) + v // 8
                        hi(c + 2, (c + 2) % R)
            head_hi(NSA_UNITS, 1, 1, KB - 1)

            def out_act(c0):
                with act.Fori(0, 2) as i:
                    for r in range(3):
                        hi_at(c0, r + 2, i, 3)
                for j in range(6, KB + 1):
                    hi_at(c0, j + 2)

            def ln_act(n, final):
                g0 = (n // 2) * 8 + (0 if n % 2 == 0 else 32)
                for k in range(KB):
                    act.wait_ge(s_cent, 8 * n + k + 1)
                    if k >= 4:
                        act.wait_ge(s_var, 4 * n + k // 2 - 1)
                    nc.scalar.activation(sq[:, k % 4, :], z[:, k, :], ACT.Square).then_inc(s_sq, 1)
                if n == 1:
                    act.wait_ge(s_ld[6], 64)
                    nc.scalar.activation(wf_h[:, :, :], wf_raw[:, :, :], ACT.Copy).then_inc(s_fw, 1)
                act.wait_ge(s_var, 4 * n + KB // 2)
                nc.scalar.activation(std, ps[:, 7, :], ACT.Sqrt, bias=eps[:, 0:1]).then_inc(s_std, 1)
                for k in range(KB):
                    if final and k in (3, 6):
                        continue
                    act.wait_ge(s_nrm, 8 * n + k + 1)
                    scale, bias = vecs[:, g0 + k:g0 + k + 1], vecs[:, g0 + 16 + k:g0 + 17 + k]
                    if final:
                        nc.scalar.activation(z[:, k, :], z[:, k, :], ACT.Identity, scale=scale, bias=bias).then_inc(s_ya, 1)
                    else:
                        nc.scalar.activation(xh[:, k, :], z[:, k, :], ACT.Identity, scale=scale, bias=bias).then_inc(s_xh, 1)

            def ffn_act(l, c_up, c_dn):
                def pair(j, ca, i=0, step=0):
                    c = ca + step * i
                    jj = FB * l + j
                    if step:
                        hi_at(ca, 2, i, step)
                    act.wait_ge(s_wu, c + 1)
                    if not isinstance(j, int) or jj > 0:
                        act.wait_ge(s_g, jj)
                    bk = (ca - c_up) % 6
                    nc.scalar.activation(ua, ps[:, bk, :], ACT.Identity, scale=conv[:, l, 2, bass.ds(j, 1)],
                                         bias=conv[:, l, 3, bass.ds(j, 1)]).then_inc(s_c0, 1)
                    act.wait_ge(s_c2, 2 * jj + 1)
                    nc.scalar.activation(ga, ua, ACT.Gelu_apprx_tanh).then_inc(s_gelu, 1)
                    hi_at(ca, 3, i, step)
                    act.wait_ge(s_wu, c + 2)
                    nc.scalar.activation(ub, ps[:, bk + 1, :], ACT.Identity, scale=conv[:, l, 2, bass.ds(FB + j, 1)],
                                         bias=conv[:, l, 3, bass.ds(FB + j, 1)]).then_inc(s_c0, 1)
                    act.wait_ge(s_g, jj + 1)
                    nc.scalar.activation(gh[:, bass.ds(j, 1), :].rearrange("p a s -> p (a s)"), gf, ACT.Copy).then_inc(s_gh, 1)

                pair(0, c_up)
                with act.Fori(0, (FB - 1) // 3) as i:
                    for r in range(3):
                        pair(1 + 3 * i + r, c_up + 2 + 2 * r, i, 6)
                with act.Fori(0, KB - 1) as i:
                    for r in range(3):
                        hi_at(c_dn, r + 2, i, 3, DN_BLOCKS[(r + 2) % 3])
                hi_at(c_dn + 3 * (KB - 1), 2, nk=DN_BLOCKS[2])
                if l == 0:
                    hi_at(c_dn + 3 * KB, 0)
                    hi_at(c_dn + 3 * KB, 1)
                    hi_at(c_dn + 3 * KB, 2)

            out_act(C_WO0)
            ln_act(0, False)
            ffn_act(0, C_UP0, C_DN0)
            ln_act(1, False)

            act.wait_ge(s_fd, 6)
            nc.scalar.activation(fe[0:HEADS, :], fz[0:HEADS, :], ACT.Abs).then_inc(s_fa, 1)
            act.wait_ge(s_fa, 1)
            nc.scalar.activation(fe[0:HEADS, :], fe[0:HEADS, :], ACT.Exp, scale=-1.0).then_inc(s_fa, 1)
            act.wait_ge(s_wu, C_FOX + 1)
            nc.scalar.activation(fqh[0][:, :], ps[:, BP, :], ACT.Copy, scale=SCALE).then_inc(s_ph, 1)
            act.wait_ge(s_fd, 7)
            nc.scalar.activation(fe[0:HEADS, :], fe[0:HEADS, :], ACT.Ln).then_inc(s_fa, 1)
            act.wait_ge(s_wu, C_FOX + 2)
            nc.scalar.activation(fkh[0][:, :], ps[:, BX, :], ACT.Copy).then_inc(s_ph, 1)
            act.wait_ge(s_fd, 9)
            nc.scalar.activation(cstack[0:HEADS, 0, :], fcum[0:HEADS, :], ACT.Copy).then_inc(s_fa, 1)
            hi_at(C_FOX, 3)
            hi_at(C_FOX, 4)

            def fox_value_copy(c, n_lo, bank=BP):
                act.wait_ge(s_wu, c + 1)
                act.wait_ge(s_pl, n_lo)
                nc.scalar.activation(tmpf, ps[:, bank, :], ACT.Copy).then_inc(s_pf, 1)

            fox_value_copy(C_FOX + 2, NSA_ITEMS, BT + 1)
            act.wait_ge(s_px, NSA_ITEMS + 1)
            nc.scalar.activation(fvh[0][:, :, :], ps[:, BX, :].rearrange("p (m c) -> p m c", m=QT), ACT.Copy).then_inc(s_ph, 1)

            def fox_value_hi(par, nv, used):
                act.wait_ge(s_px, nv)
                act.wait_ge(s_pv, used)
                nc.scalar.activation(fvh[par][:, :, :], ps[:, BX, :].rearrange("p (m c) -> p m c", m=QT), ACT.Copy).then_inc(s_ph, 1)

            def fox_stages(pair, p0, i, step, first=False, more=True):
                par = p0 % 2
                U = NSA_UNITS + 8 * pair
                for v in range(8):
                    if more or v + 2 < 8:
                        unit_exp(U + v + 2, (v + 2, (v + 2) % 4))
                    if more and v == 7:
                        fox_value_copy(C_FOX + 3 * (pair + 1) + 2, NSA_ITEMS + 3 * (pair + 1))
                    unit_hi(U + v, (v, v % 4))
                    if v == 0 and not first:
                        fox_value_hi(par, NSA_ITEMS + pair + 1, U - 8)
                    if v == 1 and not first:
                        head_hi(U, 1, 1, pair - 1, oh2)
                    if v == 5:
                        head_hi(U + 4, 0, 0, pair, oh2)
                    if more and v in (1, 4):
                        r = v // 4
                        act.wait_ge(s_wu, C_FOX + 3 * (pair + 1) + r + 1)
                        act.wait_ge(s_sc, U)
                        nc.scalar.activation(fqh[1 - par][:, :] if r == 0 else fkh[1 - par][:, :], ps[:, (BP, BX)[r], :], ACT.Copy,
                                             scale=SCALE if r == 0 else 1.0).then_inc(s_ph, 1)
                    if more and v in (0, 2, 5):
                        hi_at(C_FOX, 3 * (p0 + 1) + (0, 2, 5).index(v) + 2, i, 3 * step)

            act.wait_ge(s_cd, 16)
            unit_exp(NSA_UNITS, (0, 0))
            unit_exp(NSA_UNITS + 1, (1, 1))
            fox_stages(0, 0, 0, 0, first=True)
            with act.Fori(0, 3) as i:
                for r in range(2):
                    fox_stages(1 + r + 2 * i, 1 + r, i, 2)
            fox_stages(7, 7, 0, 0, more=False)
            head_hi(NSA_UNITS + FOX_UNITS, 1, 1, KB - 1, oh2)

            out_act(C_WO1)
            ln_act(2, False)
            ffn_act(1, C_UP1, C_DN1)
            ln_act(3, True)
            for half in range(2):
                for m in range(0, QT, 2):
                    act.wait_ge(s_yt, 4 * half + m + 1)
                    nc.scalar.activation(onat[:, m, half * 512:(half + 1) * 512], ps[:, 2 * m + half, :], ACT.Copy).then_inc(s_yc, 1)

        @block.tensor
        def _(pe):
            def mm3(o, ah, al, bh, bl, start, stop):
                nc.tensor.matmul(o, ah, bh, start=start, stop=False)
                nc.tensor.matmul(o, ah, bl, start=False, stop=False)
                return nc.tensor.matmul(o, al, bh, start=False, stop=stop)

            pe.wait_ge(s_ld[0], 16)
            for k in range(KB):
                for m in range(QT):
                    if k == 0:
                        pe.wait_ge(s_xn[m], 16)
                    last = nc.tensor.transpose(ps[:, k, m * P:(m + 1) * P], xnat[:, m, k * P:(k + 1) * P], ident[:, :])
                last.then_inc(s_xt, 1)

            def chunk(c, slot, bank, srch, srcl, k0=0, nk=KB, first=True, final=True):
                pe.wait_ge(s_wl, c + 1)
                for k in range(nk):
                    last = mm3(ps[:, bank, :], wh[:, slot, k, :], wl[:, slot, k, :], srch[:, k0 + k, :], srcl[:, k0 + k, :],
                               first and k == 0, final and k == nk - 1)
                last.then_inc(s_wu, 1)

            def kstep(c, slot, k, bank=BP):
                if k == 0:
                    pe.wait_ge(s_wl, c + 1)
                last = mm3(ps[:, bank, :], wh[:, slot, k, :], wl[:, slot, k, :], xh[:, k, :], xl[:, k, :], k == 0, k == KB - 1)
                if k == KB - 1:
                    last.then_inc(s_wu, 1)

            def x_fresh(n, k):
                if n == 0:
                    pe.wait_ge(s_x, k + 1)
                elif k in XL_DVE:
                    pe.wait_ge(s_x, KB + len(XL_DVE) * (n - 1) + XL_DVE.index(k) + 1)
                else:
                    pe.wait_ge(s_xp, len(XL_POOL) * (n - 1) + XL_POOL.index(k) + 1)

            for k in range(KB):
                x_fresh(0, k)
                kstep(0, 0, k)
            chunk(1, 1, BX, xh, xl)
            pe.wait_ge(s_gw, 2)
            for m in range(QT):
                for k in range(KB):
                    last = mm3(ps[:, 5, m * NG:(m + 1) * NG], xh[:, k, m * P:(m + 1) * P], xl[:, k, m * P:(m + 1) * P],
                               wg_h[:, k, :], wg_l[:, k, :], k == 0, k == KB - 1)
            last.then_inc(s_gp, 1)
            pe.wait_ge(s_ld[5], 16 * 7)
            nc.tensor.transpose(ps[:, 6, 0:68], vec_nat[:, :], ident[0:68, 0:68]).then_inc(s_vt, 1)
            nc.tensor.transpose(ps[:, 6, 128:128 + LP], pe_nat[:, :], ident[0:LP, 0:LP]).then_inc(s_vt, 1)
            pe.wait_ge(s_kc, 1)
            chunk(2, 2, BP, xh, xl)

            def cmp_hidden(src):
                pe.wait_ge(s_kp, 8 * (src + 1))
                pe.wait_ge(s_ld[8 + src], 16)
                if src:
                    pe.wait_ge(s_gel, 1)
                for hb in range(2):
                    for lp in range(LP):
                        last = nc.tensor.matmul(ps[:, 2, hb * P:hb * P + GROUPS * NCMP], (w1k, w1v)[src][:, lp, hb * P:(hb + 1) * P],
                                                kp[:, lp, :], start=(lp == 0), stop=(lp == LP - 1))
                last.then_inc(s_hid, 1)

            def conv_turn(l):
                pe.wait_ge(s_ld[11], 32 * (l + 1))
                if l:
                    pe.wait_ge(s_vc, 3)
                for w in range(4):
                    nc.tensor.transpose(ps[:, 7, w * P:w * P + 2 * FB], conv_nat[:, w, :], ident[0:2 * FB, 0:2 * FB]).then_inc(s_vt, 1)

            cmp_hidden(0)
            pe.wait_ge(s_kc, 2)
            chunk(3, 0, BX, xh, xl)
            pe.wait_ge(s_gel, 1)
            pe.wait_ge(s_ld[7], 32)
            for hb in range(2):
                last = nc.tensor.matmul(ps[0:HD, 3, 0:GROUPS * NCMP], w2k[:, hb, :], ghid[:, hb, :], start=(hb == 0), stop=(hb == 1))
            last.then_inc(s_cmpo, 1)

            def item_turn(g, k):
                n = 4 * g + k
                pe.wait_ge(s_pf, n + 1)
                if k == 1:
                    for m in range(QT):
                        last = nc.tensor.transpose(ps[:, BX, m * P:(m + 1) * P], tmpf[:, m * P:(m + 1) * P], ident[:, :])
                else:
                    src = tmpf if k == 0 else qf[g % 2][:, k - 2, :]
                    last = nc.tensor.matmul(ps[:, BX, :], rotm[:, :], src, start=True, stop=True)
                last.then_inc(s_px, 1)

            def item_steps(n):
                if n:
                    pe.wait_ge(s_pf, n)
                for kk in range(KB):
                    kstep(4 + n, (4 + n) % R, kk)

            pe.wait_ge(s_kc, 3)
            item_steps(0)
            conv_turn(0)
            cmp_hidden(1)
            pe.wait_ge(s_ld[3], 16)
            pe.wait_ge(s_kc, 4)
            item_turn(0, 0)
            item_steps(1)
            pe.wait_ge(s_gel, 2)
            for g in range(GROUPS):
                for hb in range(2):
                    last = nc.tensor.matmul(ps[0:NCMP, 4, g * HD:(g + 1) * HD], ghid[:, hb, g * NCMP:(g + 1) * NCMP], w2v[:, hb, :],
                                            start=(hb == 0), stop=(hb == 1))
            last.then_inc(s_cmpo, 1)
            pe.wait_ge(s_pl, 1)
            item_turn(0, 1)
            item_steps(2)
            conv_turn(1)
            pe.wait_ge(s_pl, 2)
            item_turn(0, 2)

            def mask(bank, i, stop=True):
                return nc.tensor.matmul(ps[:, bank, i * P:(i + 1) * P], identb[:, :], causalb[:, :], start=False, stop=stop)

            def nsa_scores(u):
                g, v = u // 32, u % 32
                h, i, br = v // 8, v % 8 // 2, v % 2
                par, half = g % 2, h % 2
                if v % 8 == 0:
                    pe.wait_ge(s_pl, 4 * g + 3 + h // 2)
                    if h == 0:
                        pe.wait_ge(s_sw[par], 32 * (g // 2 + 1))
                if u >= 2:
                    pe.wait_ge(s_ex, u - 1)
                keys = (ka if half == br else kb)[par]
                rows = slice(half * HD, (half + 1) * HD)
                n, b = (i + 1) * P, BS + u % 2
                mm3(ps[:, b, 0:n], qh[par][rows, h // 2, i * P:n], ql[par][rows, h // 2, i * P:n],
                    keys[rows, 0, 0:n], keys[rows, 1, 0:n], True, False)
                mask(b, i).then_inc(s_sc, 1)

            def cmp_scores(H):
                g, h = H // 4, H % 4
                rows = slice(h % 2 * HD, h % 2 * HD + HD)
                n = min(H + 3, NSA_ITEMS) - 1
                if n % 4 == 1:
                    pe.wait_ge(s_pl, n + 1)
                else:
                    pe.wait_ge(s_r2, n - (n + 2) // 4 + 1)
                pe.wait_ge(s_pf, 4 * g + 3 + h // 2)
                for i in range(QT):
                    last = nc.tensor.matmul(ps[:, BX, i * NCMP:(i + 1) * NCMP], qf[g % 2][rows, h // 2, i * P:(i + 1) * P],
                                            kcd[rows, g * NCMP:(g + 1) * NCMP], start=True, stop=True)
                last.then_inc(s_cs, 1)

            def cmp_turn(H):
                pe.wait_ge(s_cp, H + 1)
                for i in range(QT):
                    last = nc.tensor.transpose(ps[0:NCMP, BX, i * P:(i + 1) * P], csm[:, i, :], ident[:, :])
                last.then_inc(s_ct, 1)

            def turn(u, loc):
                pe.wait_ge(s_pr, u + 1)
                if not isinstance(u, int) or u >= 2:
                    pe.wait_ge(s_ptl, u - 1)
                for kt in range(loc[1] + 1):
                    last = nc.tensor.transpose(ps[:, BT + loc[0] % 2, kt * P:(kt + 1) * P], prob[:, loc[0] % 4, kt * P:(kt + 1) * P], ident[:, :])
                last.then_inc(s_pt, 1)

            def pv(u, loc, bank, v_h, v_l, start, stop):
                pe.wait_ge(s_ptl, u + 1)
                i, b = loc[1], loc[0] % 2
                o = ps[0:HD, bank, i * P:(i + 1) * P]
                for kt in range(i + 1):
                    last = mm3(o, v_h[:, kt, :], v_l[:, kt, :], pth[:, b, kt * P:(kt + 1) * P], ptl[:, b, kt * P:(kt + 1) * P],
                               start and kt == 0, stop and kt == i)
                last.then_inc(s_pv, 1)

            def nsa_pv(u):
                g, v = u // 32, u % 32
                h, i, br = v // 8, v % 8 // 2, v % 2
                H = 4 * g + h
                bank = BO + H % 2
                if v % 8 == 0:
                    if H >= 2:
                        pe.wait_ge(s_ol, H - 1)
                    pe.wait_ge(s_cc, H + 1)
                if br == 0:
                    nc.tensor.matmul(ps[0:HD, bank, i * P:(i + 1) * P], vcd[:, g, :], pct[0:NCMP, H % 2, i * P:(i + 1) * P], start=True, stop=False)
                cs = slice(br * HD, (br + 1) * HD)
                pv(u, (u, i), bank, vh[g % 2][:, :, cs], vl[g % 2][:, :, cs], False, br == 1)

            pe.wait_ge(s_cst, 2)
            pe.wait_ge(s_cmpr, 2)
            cmp_scores(0)
            item_steps(3)
            pe.wait_ge(s_vc, 4)
            pe.wait_ge(s_ge, 4)
            nsa_scores(0)
            nsa_scores(1)
            for g in range(GROUPS):
                for v in range(32):
                    u = 32 * g + v
                    if v % 8 == 0:
                        cmp_turn(u // 8)
                    if v % 8 == 4 and u + 4 < NSA_UNITS:
                        cmp_scores(u // 8 + 1)
                    if u + 2 < NSA_UNITS:
                        nsa_scores(u + 2)
                    if g < GROUPS - 1:
                        n = 4 * (g + 1) + v // 8
                        if v % 8 == 0:
                            pe.wait_ge(s_pf, n)
                        kstep(4 + n, (4 + n) % R, v % 8)
                    turn(u, (u, v % 8 // 2))
                    if u:
                        nsa_pv(u - 1)
                    if v % 8 == 1 and (g < GROUPS - 1 or v == 1):
                        pe.wait_ge(s_cc, u // 8 + 1)
                        item_turn(*((g + 1, v // 8 - 1) if v > 1 else (g, 3)))
            nsa_pv(NSA_UNITS - 1)

            def out_pe(c0, heads, zb, oh, ol):
                pe.wait_ge(s_ol, heads)

                def one(j, ca, i, step):
                    bank = (ca - c0) % 3
                    pe.wait_ge(s_z1, zb + j - 2)
                    chunk(ca + step * i if step else ca, ca % R, bank, oh, ol)

                with pe.Fori(0, 2) as i:
                    for r in range(3):
                        one(3 * i + r, c0 + r, i, 3)
                for j in range(6, KB):
                    one(j, c0 + j, 0, 0)

            def ln_pe(n):
                pe.wait_ge(s_ld[2], 16)
                pe.wait_ge(s_zs, 8 * (n + 1))
                nc.tensor.matmul(ps[:, 6, :], onesd[:, :], zsum, start=True, stop=True).then_inc(s_mean, 1)
                for m in range(KB // 2):
                    pe.wait_ge(s_sp, 4 * n + m + 1)
                    nc.tensor.matmul(ps[:, 7, :], onesd[:, :], sq[:, 2 * (m % 2), :], start=(m == 0), stop=(m == KB // 2 - 1)).then_inc(s_var, 1)

            def ffn_pe(l, c_up, c_dn, fresh, zb):
                pe.wait_ge(s_wl, c_up + 2)
                for k in range(KB):
                    x_fresh(fresh, k)
                    for r in range(2):
                        slot = (c_up + r) % R
                        last = mm3(ps[:, r, :], wh[:, slot, k, :], wl[:, slot, k, :], xh[:, k, :], xl[:, k, :], k == 0, k == KB - 1)
                last.then_inc(s_wu, 2)
                with pe.Fori(0, (FB - 1) // 3) as i:
                    for r in range(3):
                        for b in range(2):
                            c = c_up + 2 + 2 * r + b
                            chunk(c + 6 * i, c % R, (c - c_up) % 6, xh, xl)
                pe.wait_ge(s_gl, FB * (l + 1))
                with pe.Fori(0, KB // 2) as i:
                    for q in range(2):
                        for r in range(3):
                            c = c_dn + 3 * q + r
                            if r == 0:
                                pe.wait_ge(s_z1, zb + 2 * i + q - 1)
                            chunk(c + 6 * i, c % R, q, gh, gl, k0=8 * r, nk=DN_BLOCKS[r], first=r == 0, final=r == 2)

            out_pe(C_WO0, HEADS, Z0, oh, ol)
            ln_pe(0)
            ffn_pe(0, C_UP0, C_DN0, 1, Z0 + 8)
            ln_pe(1)

            pe.wait_ge(s_fw, 2)
            for k in range(KB):
                x_fresh(2, k)
                last = mm3(ps[0:HEADS, BT, :], wf_h[:, k, :], wf_l[:, k, :], xh[:, k, :], xl[:, k, :], k == 0, k == KB - 1)
                if k == KB - 1:
                    last.then_inc(s_fp, 1)
                kstep(C_FOX, C_FOX % R, k)
                kstep(C_FOX + 1, (C_FOX + 1) % R, k, BX)

            def value_turn(n):
                pe.wait_ge(s_pf, n)
                for m in range(QT):
                    last = nc.tensor.transpose(ps[:, BX, m * P:(m + 1) * P], tmpf[:, m * P:(m + 1) * P], ident[:, :])
                last.then_inc(s_px, 1)

            for k in range(KB):
                kstep(C_FOX + 2, (C_FOX + 2) % R, k, BT + 1)
            pe.wait_ge(s_pl, NSA_ITEMS + 2)
            value_turn(NSA_ITEMS + 1)

            def fox_scores(u, v, par, pair, rows_landed):
                h, i = v // 4, v % 4
                if v == 0:
                    pe.wait_ge(s_pl, NSA_ITEMS + 3 * pair + 2)
                    pe.wait_ge(s_bl[par], rows_landed)
                pe.wait_ge(s_ex, u - 1)
                rows = slice(h * HD, (h + 1) * HD)
                n, b = (i + 1) * P, BS + v % 2
                mm3(ps[:, b, 0:n], fqh[par][rows, i * P:n], fql[par][rows, i * P:n], fkh[par][rows, 0:n], fkl[par][rows, 0:n], True, False)
                nc.tensor.matmul(ps[:, b, 0:n], biasq[par][0:4, h, i * P:n], biask[par][0:4, h, 0:n], start=False, stop=False)
                mask(b, i).then_inc(s_sc, 1)

            def fox_pv(u, v, par, pair):
                h, i = v // 4, v % 4
                if i == 0:
                    pe.wait_ge(s_ol, HEADS + 2 * pair + h - 1)
                if v == 0:
                    pe.wait_ge(s_pl, NSA_ITEMS + 3 * pair + 3)
                cs = slice(h * HD, (h + 1) * HD)
                pv(u, (v, i), BO + h, fvh[par][:, :, cs], fvl[par][:, :, cs], True, True)

            def fox_stages(pair, par, rows_next, first=False, more=True):
                U = NSA_UNITS + 8 * pair
                for v in range(8):
                    if v + 2 < 8:
                        fox_scores(U + v + 2, v + 2, par, pair, None)
                    elif more:
                        fox_scores(U + v + 2, v - 6, 1 - par, pair + 1, rows_next)
                    if more:
                        for s in range(*FOX_STEPS[v]):
                            r, k = s // KB, s % KB
                            if k == 0 and r:
                                pe.wait_ge(s_pl, NSA_ITEMS + 3 * (pair + 1) + r - 1)
                            if k == 0 and not r:
                                pe.wait_ge(s_pf, NSA_ITEMS + pair + 1)
                            kstep(C_FOX + 3 * (pair + 1) + r, (C_FOX + r) % R, k, (BP, BX, BP)[r])
                    turn(U + v, (v, v % 4))
                    if v == 0 and not first:
                        pe.wait_ge(s_pl, NSA_ITEMS + 3 * pair)
                        value_turn(NSA_ITEMS + pair + 1)
                    if v:
                        fox_pv(U + v - 1, v - 1, par, pair)
                    elif not first:
                        fox_pv(U - 1, 7, 1 - par, pair - 1)

            fox_scores(NSA_UNITS, 0, 0, 0, 32)
            fox_scores(NSA_UNITS + 1, 1, 0, 0, None)
            fox_stages(0, 0, 32, first=True)
            with pe.Fori(0, 3) as i:
                for r in range(2):
                    fox_stages(1 + r + 2 * i, (1 + r) % 2, 32 * (2 + i))
            fox_stages(7, 1, None, more=False)
            fox_pv(NSA_UNITS + FOX_UNITS - 1, 7, 1, 7)

            out_pe(C_WO1, 2 * HEADS, Z0 + 16, oh2, ol2)
            ln_pe(2)
            ffn_pe(1, C_UP1, C_DN1, 3, Z0 + 24)
            ln_pe(3)
            for k in range(KB):
                if k in (3, 6):
                    pe.wait_ge(s_y, 3 * KB + k // 3)
                else:
                    pe.wait_ge(s_ya, k + 1 - k // 3)
                for m in range(QT):
                    last = nc.tensor.transpose(ps[:, 2 * m + k // 4, k % 4 * P:(k % 4 + 1) * P], z[:, k, m * P:(m + 1) * P], ident[:, :])
                    if k % 4 == 3:
                        last.then_inc(s_yt, 1)

        @block.vector
        def _(dve):
            nc.vector.memset(eps[:, :], EPS).then_inc(s_z1, Z0)
            dve.wait_ge(s_ld[0], 16)
            nc.vector.tensor_copy(identb[:, :], ident[:, :]).then_inc(s_cst, 1)
            for k in range(KB):
                dve.wait_ge(s_xh, k + 1)
                nc.vector.tensor_tensor(xl[:, k, :], ps[:, k, :], xh[:, k, :].bitcast(F32), ALU.subtract).then_inc(s_x, 1)
            dve.wait_ge(s_gw, 1)
            nc.vector.tensor_tensor(wg_l[:, :, :], wg_raw[:, :, :], wg_h[:, :, :].bitcast(F32), ALU.subtract).then_inc(s_gw, 1)
            def cmp_blocks(src):
                dve.wait_ge(s_vc, 2)
                if src:
                    dve.wait_ge(s_hid, 1)
                for g in range(GROUPS):
                    if g % 2 == 0:
                        dve.wait_ge(s_kc, 2 * src + g // 2 + 1)
                    view = kc2[:, g, :].rearrange("p (n l two) -> p l n two", l=8, two=2)
                    for h in range(2):
                        nc.vector.tensor_tensor(kp[:, 8 * h:8 * h + 8, g * NCMP:(g + 1) * NCMP], view[:, :, h:h + NCMP, 0],
                                                pe2[:, 8 * h:8 * h + 8].unsqueeze(2).to_broadcast([P, 8, NCMP]), ALU.add).then_inc(s_kp, 1)

            dve.wait_ge(s_gp, 1)
            nc.vector.tensor_tensor(gate[:, :, :], ps[:, 5, 0:QT * NG].rearrange("p (m n) -> p m n", m=QT),
                                    bgate[:, :].unsqueeze(1).to_broadcast([P, QT, NG]), ALU.add).then_inc(s_ge, 1)
            dve.wait_ge(s_vt, 2)
            nc.vector.tensor_copy(vecs[:, :], ps[:, 6, 0:68]).then_inc(s_vc, 1)
            nc.vector.tensor_copy(pe2[:, :], ps[:, 6, 128:128 + LP]).then_inc(s_vc, 1)
            cmp_blocks(0)
            dve.wait_ge(s_ge, 2)
            nc.vector.tensor_scalar(gate[:, :, :], gate[:, :, :], 1.0, None, ALU.add).then_inc(s_ge, 1)
            dve.wait_ge(s_ge, 3)
            nc.vector.reciprocal(gate[:, :, :], gate[:, :, :]).then_inc(s_ge, 1)
            for n in range(4):
                dve.wait_ge(s_ld[1 + n], 16)
            nc.vector.tensor_copy(causalb[:, :], causal[:, :]).then_inc(s_cst, 1)
            cmp_blocks(1)

            def conv_copy(l):
                dve.wait_ge(s_vt, 6 + 4 * l)
                nc.vector.tensor_copy(conv[:, l, :, :], ps[:, 7, :].rearrange("p (w c) -> p w c", w=4)[:, :, 0:2 * FB]).then_inc(s_vc, 1)

            conv_copy(0)

            dve.wait_ge(s_ld[10], 32)

            def item_dve(g, k):
                n, par = 4 * g + k, g % 2
                dve.wait_ge(s_px, n + 1)
                if k == 1:
                    dve.wait_ge(s_ph, n + 1)
                    nc.vector.tensor_tensor(vl[par][:, :, :], ps[:, BX, :].rearrange("p (m c) -> p m c", m=QT), vh[par][:, :, :].bitcast(F32),
                                            ALU.subtract).then_inc(s_pl, 1)
                    return
                rn = n - (n + 2) // 4
                if rn:
                    dve.wait_ge(s_r3, rn)
                nc.vector.tensor_tensor(rot2, ps[:, BX, :], sinT[:, :], ALU.mult).then_inc(s_r2, 1)

            def unit_max(u, loc):
                dve.wait_ge(s_sc, u + 1)
                n = (loc[1] + 1) * P
                nc.vector.tensor_reduce(negmax[:, loc[0] % 4:loc[0] % 4 + 1], ps[:, BS + loc[0] % 2, 0:n], AX.X, ALU.max,
                                        negate=True).then_inc(s_nm, 1)

            def unit_scale(u, loc, gated, gcol=None):
                i, b = loc[1], loc[0] % 4
                n = (i + 1) * P
                dve.wait_ge(s_ex, u + 1)
                nc.vector.reciprocal(rinv[:, b:b + 1], psumrow[:, b:b + 1]).then_inc(s_ri, 1)
                dve.wait_ge(s_ri, u + 1)
                if gated:
                    nc.vector.tensor_scalar(prob[:, b, 0:n], prob[:, b, 0:n], rinv[:, b:b + 1], gate[:, i, gcol:gcol + 1],
                                            ALU.mult, ALU.mult).then_inc(s_pr, 1)
                else:
                    nc.vector.tensor_scalar(prob[:, b, 0:n], prob[:, b, 0:n], rinv[:, b:b + 1], None, ALU.mult).then_inc(s_pr, 1)

            def unit_lo(u, loc):
                dve.wait_ge(s_pth, u + 1)
                n, b = (loc[1] + 1) * P, loc[0] % 2
                nc.vector.tensor_tensor(ptl[:, b, 0:n], ps[:, BT + b, 0:n], pth[:, b, 0:n].bitcast(F32), ALU.subtract).then_inc(s_ptl, 1)

            def head_lo(count, par, half, pair, oh=oh, ol=ol):
                dve.wait_ge(s_oh, count)
                rows = slice(half * HD, (half + 1) * HD)
                sel = (lambda a: a[rows, pair, :]) if isinstance(pair, int) else \
                    (lambda a: a[rows, bass.ds(pair, 1), :].rearrange("p a s -> p (a s)"))
                nc.vector.tensor_tensor(sel(ol), ps[0:HD, BO + par, :], sel(oh).bitcast(F32), ALU.subtract).then_inc(s_ol, 1)

            def cmp_mask(H):
                dve.wait_ge(s_cs, H + 1)
                if H:
                    dve.wait_ge(s_ct, H)
                nc.vector.tensor_tensor(csm[:, :, :], ps[:, BX, 0:QT * NCMP].rearrange("p (m n) -> p m n", m=QT), cmask[:, :, :],
                                        ALU.add).then_inc(s_cmask, 1)
                dve.wait_ge(s_cmask, H + 1)
                nc.vector.tensor_reduce(cstat[:, 0, :], csm[:, :, :], AX.X, ALU.max).then_inc(s_cmax, 1)

            def cmp_difference(H):
                dve.wait_ge(s_cmax, H + 1)
                nc.vector.tensor_scalar(cstat[:, 1, :], cstat[:, 0, :], FLOOR, None, ALU.max).then_inc(s_cfl, 1)
                dve.wait_ge(s_cfl, H + 1)
                nc.vector.tensor_tensor(csm[:, :, :], csm[:, :, :], cstat[:, 1, :].unsqueeze(2).to_broadcast([P, QT, NCMP]),
                                        ALU.subtract).then_inc(s_cdf, 1)

            def cmp_sum(H):
                dve.wait_ge(s_ce, H + 1)
                nc.vector.tensor_reduce(cstat[:, 2, :], csm[:, :, :], AX.X, ALU.add).then_inc(s_csum, 1)
                dve.wait_ge(s_csum, H + 1)
                nc.vector.tensor_scalar(cstat[:, 2, :], cstat[:, 2, :], 1e-30, None, ALU.max).then_inc(s_csf, 1)

            def cmp_inverse(H):
                dve.wait_ge(s_csf, H + 1)
                nc.vector.reciprocal(cstat[:, 3, :], cstat[:, 2, :]).then_inc(s_cinv, 1)

            def cmp_gate(H):
                dve.wait_ge(s_cinv, H + 1)
                nc.vector.tensor_tensor(cstat[:, 3, :], cstat[:, 3, :], gate[:, :, 3 * H], ALU.mult).then_inc(s_cg, 1)

            def cmp_scale(H):
                dve.wait_ge(s_cg, H + 1)
                nc.vector.tensor_tensor(csm[:, :, :], csm[:, :, :], cstat[:, 3, :].unsqueeze(2).to_broadcast([P, QT, NCMP]),
                                        ALU.mult).then_inc(s_cp, 1)

            for k in range(2):
                item_dve(0, k)
            item_dve(0, 2)
            conv_copy(1)
            for step in (cmp_mask, cmp_difference, cmp_sum, cmp_inverse, cmp_gate, cmp_scale):
                step(0)
            unit_max(0, (0, 0))
            unit_max(1, (1, 0))
            unit_scale(0, (0, 0), True, 1)
            for g in range(GROUPS):
                for v in range(32):
                    u, w = 32 * g + v, v % 8
                    H = u // 8
                    item = (g, 3) if v < 8 else (g + 1, v // 8 - 1)
                    turned = v < 8 or g < GROUPS - 1
                    following = H + 1 < HEADS
                    if u + 2 < NSA_UNITS:
                        unit_max(u + 2, (u + 2, (u + 2) % 8 // 2))
                    if w == 7 and following:
                        cmp_inverse(H + 1)
                    if u + 1 < NSA_UNITS:
                        unit_scale(u + 1, (u + 1, (u + 1) % 8 // 2), True, 3 * ((u + 1) // 8) + 1 + (u + 1) % 2)
                    if turned and w == (3 if item[1] == 1 else 2):
                        item_dve(*item)
                    if w == 4 and following:
                        cmp_mask(H + 1)
                    if w == 5 and following:
                        cmp_difference(H + 1)
                    if w == 7 and following:
                        cmp_gate(H + 1)
                    unit_lo(u, (u, w // 2))
                    if w == 6 and following:
                        cmp_sum(H + 1)
                    if w == 7 and following:
                        cmp_scale(H + 1)
                    if w == 1 and u > 8:
                        head_lo(H, (H - 1) % 2, (H - 1) % 2, (H - 1) // 2)
            head_lo(HEADS, 1, 1, KB - 1)

            def z_one(c, j, bank, zn):
                xs = lambda a: a[:, bass.ds(j, 1), :].rearrange("p a s -> p (a s)")
                dve.wait_ge(s_wu, c + 1)
                nc.vector.scalar_tensor_tensor(out=xs(z), in0=xs(xh).bitcast(F32), scalar=ALPHA, in1=ps[:, bank, :],
                                               op0=ALU.mult, op1=ALU.add).then_inc(s_z1, 1)
                dve.wait_ge(s_z1, Z0 + zn + 1)
                nc.vector.scalar_tensor_tensor(out=xs(z), in0=xs(xl).bitcast(F32), scalar=ALPHA, in1=xs(z),
                                               op0=ALU.mult, op1=ALU.add).then_inc(s_z2, 1)
                dve.wait_ge(s_z2, zn + 1)
                nc.vector.tensor_tensor(zsum, zsum, xs(z), ALU.add).then_inc(s_zs, 1)

            def out_dve(c0, n):
                nc.vector.memset(zsum, 0.0).then_inc(s_zs0, 1)
                dve.wait_ge(s_zs0, n + 1)
                with dve.Fori(0, 2) as i:
                    for r in range(3):
                        z_one(c0 + 3 * i + r, 3 * i + r, r, 8 * n + 3 * i + r)
                for j in range(6, KB):
                    z_one(c0 + j, j, j % 3, 8 * n + j)

            def forget_setup():
                nc.vector.memset(fone[:, :], 1.0).then_inc(s_fd, 1)
                for par in range(2):
                    nc.vector.memset(biasq[par][0:4, :, :].bitcast(F32), 1.0).then_inc(s_fd, 1)
                    nc.vector.memset(biask[par][0:4, :, :].bitcast(F32), 1.0).then_inc(s_fd, 1)
                dve.wait_ge(s_fw, 1)
                nc.vector.tensor_tensor(wf_l[:, :, :], wf_raw[:, :, :], wf_h[:, :, :].bitcast(F32), ALU.subtract).then_inc(s_fw, 1)

            def ln_dve(n, final):
                g0 = (n // 2) * 8 + (0 if n % 2 == 0 else 32)
                dve.wait_ge(s_mean, n + 1)
                for k in range(KB):
                    nc.vector.tensor_tensor(z[:, k, :], z[:, k, :], ps[:, 6, :], ALU.subtract).then_inc(s_cent, 1)
                if n == 1:
                    forget_setup()
                dve.wait_ge(s_std, n + 1)
                nc.vector.reciprocal(rstd, std).then_inc(s_rstd, 1)
                dve.wait_ge(s_rstd, n + 1)
                dve.wait_ge(s_cent, 8 * (n + 1))

                def affine(k):
                    nc.vector.tensor_scalar(z[:, k, :], z[:, k, :], vecs[:, g0 + k:g0 + k + 1], vecs[:, g0 + 16 + k:g0 + 17 + k],
                                            ALU.mult, ALU.add).then_inc(s_y, 1)

                for k in range(KB + 2):
                    if k < KB:
                        nc.vector.tensor_tensor(z[:, k, :], z[:, k, :], rstd, ALU.mult).then_inc(s_nrm, 1)
                    if final:
                        if k - 1 in (3, 6):
                            dve.wait_ge(s_nrm, 8 * n + k)
                            affine(k - 1)
                        continue
                    if 0 < k <= KB:
                        dve.wait_ge(s_xh, 8 * (n + 1) + k)
                        affine(k - 1)
                    if k - 2 in XL_DVE:
                        dve.wait_ge(s_y, 8 * n + k - 1)
                        nc.vector.tensor_tensor(xl[:, k - 2, :], z[:, k - 2, :], xh[:, k - 2, :].bitcast(F32), ALU.subtract).then_inc(s_x, 1)

            def ffn_dve(l, c_up, c_dn, n):
                def taps(buf, j, blk, bank, c2):
                    dve.wait_ge(s_c0, c2 + 1)
                    nc.vector.scalar_tensor_tensor(out=buf[:, 1:SEQ], in0=ps[:, bank, 0:SEQ - 1], scalar=conv[:, l, 1, bass.ds(blk, 1)],
                                                   in1=buf[:, 1:SEQ], op0=ALU.mult, op1=ALU.add).then_inc(s_c1, 1)
                    dve.wait_ge(s_c1, c2 + 1)
                    nc.vector.scalar_tensor_tensor(out=buf[:, 2:SEQ], in0=ps[:, bank, 0:SEQ - 2], scalar=conv[:, l, 0, bass.ds(blk, 1)],
                                                   in1=buf[:, 2:SEQ], op0=ALU.mult, op1=ALU.add).then_inc(s_c2, 1)

                def pair(j, bank):
                    jj = FB * l + j
                    taps(ua, j, j, bank, 2 * jj)
                    taps(ub, j, FB + j, bank + 1, 2 * jj + 1)
                    dve.wait_ge(s_gelu, jj + 1)
                    dve.wait_ge(s_c2, 2 * jj + 2)
                    nc.vector.tensor_tensor(gf, ga, ub, ALU.mult).then_inc(s_g, 1)
                    dve.wait_ge(s_gh, jj + 1)
                    sel = lambda a: a[:, bass.ds(j, 1), :].rearrange("p a s -> p (a s)")
                    nc.vector.tensor_tensor(sel(gl), gf, sel(gh).bitcast(F32), ALU.subtract).then_inc(s_gl, 1)

                pair(0, 0)
                with dve.Fori(0, (FB - 1) // 3) as i:
                    for r in range(3):
                        pair(1 + 3 * i + r, (2 + 2 * r) % 6)
                nc.vector.memset(zsum, 0.0).then_inc(s_zs0, 1)
                dve.wait_ge(s_zs0, n + 1)
                with dve.Fori(0, KB // 2) as i:
                    for q in range(2):
                        z_one(c_dn + 6 * i + 3 * q + 2, 2 * i + q, q, 8 * n + 2 * i + q)

            out_dve(C_WO0, 0)
            ln_dve(0, False)
            ffn_dve(0, C_UP0, C_DN0, 1)
            ln_dve(1, False)

            def fox_lo(par, r, n):
                dve.wait_ge(s_ph, n + 1)
                if r == 0:
                    nc.vector.scalar_tensor_tensor(out=fql[par][:, :], in0=ps[:, BP, :], scalar=SCALE, in1=fqh[par][:, :].bitcast(F32),
                                                   op0=ALU.mult, op1=ALU.subtract).then_inc(s_pl, 1)
                elif r == 1:
                    nc.vector.tensor_tensor(fkl[par][:, :], ps[:, BX, :], fkh[par][:, :].bitcast(F32), ALU.subtract).then_inc(s_pl, 1)
                else:
                    nc.vector.tensor_tensor(fvl[par][:, :, :], ps[:, BX, :].rearrange("p (m c) -> p m c", m=QT), fvh[par][:, :, :].bitcast(F32),
                                            ALU.subtract).then_inc(s_pl, 1)

            hs = slice(0, HEADS)
            dve.wait_ge(s_fp, 1)
            nc.vector.tensor_scalar(fz[hs, :], ps[hs, BT, :], bf[:, 0:1], None, ALU.add).then_inc(s_fd, 1)
            dve.wait_ge(s_fa, 2)
            nc.vector.tensor_scalar(fe[hs, :], fe[hs, :], 1.0, None, ALU.add).then_inc(s_fd, 1)
            fox_lo(0, 0, NSA_ITEMS)
            dve.wait_ge(s_fa, 3)
            dve.wait_ge(s_fd, 7)
            nc.vector.scalar_tensor_tensor(out=fz[hs, :], in0=fz[hs, :], scalar=0.0, in1=fe[hs, :], op0=ALU.min, op1=ALU.subtract).then_inc(s_fd, 1)
            dve.wait_ge(s_fd, 8)
            nc.vector.tensor_tensor_scan(fcum[hs, :], fone[hs, :], fz[hs, :], 0.0, ALU.mult, ALU.add).then_inc(s_fd, 1)
            fox_lo(0, 1, NSA_ITEMS + 1)
            dve.wait_ge(s_fa, 4)
            dve.wait_ge(s_fd, 9)
            nc.vector.tensor_tensor(cstack[hs, 1, :], fcum[hs, :], cstack[hs, 0, :].bitcast(F32), ALU.subtract).then_inc(s_fd, 1)
            nc.vector.tensor_scalar(cstack[hs, 2, :], cstack[hs, 0, :].bitcast(F32), -1.0, None, ALU.mult).then_inc(s_fd, 1)
            dve.wait_ge(s_fd, 10)
            nc.vector.tensor_scalar(cstack[hs, 3, :], cstack[hs, 1, :].bitcast(F32), -1.0, None, ALU.mult).then_inc(s_fd, 1)
            fox_lo(0, 2, NSA_ITEMS + 2)
            unit_max(NSA_UNITS, (0, 0))
            unit_max(NSA_UNITS + 1, (1, 1))
            unit_scale(NSA_UNITS, (0, 0), False)

            def fox_stages(pair, par, first=False, more=True):
                U = NSA_UNITS + 8 * pair
                for v in range(8):
                    if more or v + 2 < 8:
                        unit_max(U + v + 2, (v + 2, (v + 2) % 4))
                    if more or v + 1 < 8:
                        unit_scale(U + v + 1, (v + 1, (v + 1) % 4), False)
                    if v == 1 and not first:
                        fox_lo(par, 2, NSA_ITEMS + 3 * pair + 2)
                    if more and v in (2, 5):
                        fox_lo(1 - par, v // 4, NSA_ITEMS + 3 * (pair + 1) + v // 4)
                    unit_lo(U + v, (v, v % 4))
                    if v == 1 and not first:
                        head_lo(HEADS + 2 * pair, 1, 1, pair - 1, oh2, ol2)
                    if v == 5:
                        head_lo(HEADS + 2 * pair + 1, 0, 0, pair, oh2, ol2)

            fox_stages(0, 0, first=True)
            with dve.Fori(0, 3) as i:
                for r in range(2):
                    fox_stages(1 + r + 2 * i, (1 + r) % 2)
            fox_stages(7, 1, more=False)
            head_lo(2 * HEADS, 1, 1, KB - 1, oh2, ol2)

            out_dve(C_WO1, 2)
            ln_dve(2, False)
            ffn_dve(1, C_UP1, C_DN1, 3)
            ln_dve(3, True)
            for half in range(2):
                for m in range(1, QT, 2):
                    dve.wait_ge(s_yt, 4 * half + m + 1)
                    nc.vector.tensor_copy(onat[:, m, half * 512:(half + 1) * 512], ps[:, 2 * m + half, :]).then_inc(s_yd, 1)


_INS = ["x", "nsa_w_in", "nsa_b_gate", "nsa_pe", "nsa_phik_w1", "nsa_phik_b1", "nsa_phik_w2", "nsa_phiv_w1", "nsa_phiv_b1",
        "nsa_phiv_w2", "nsa_w_o", "fox_w_in", "fox_b_f", "fox_w_o", "ffn_w_up", "ffn_conv_w", "ffn_conv_b", "ffn_w_down",
        "ln1_g", "ln1_b", "ln2_g", "ln2_b"]


def shape_constants():
    import numpy as np
    f = np.float32
    inv = (f(10000.0) ** (-np.arange(0, HD, 2, dtype=f) / f(HD))).astype(f)
    ang = np.arange(SEQ, dtype=f)[:, None] * inv[None, :]
    ang = np.concatenate([ang, ang, ang, ang], axis=1)
    rot = np.zeros((P, P), f)
    for d in range(P):
        if d % HD < HD // 2:
            rot[d + HD // 2, d] = -1.0
        else:
            rot[d - HD // 2, d] = 1.0
    q, k = np.arange(P)[:, None], np.arange(P)[None, :]
    tok = np.arange(QT)[None, :, None] * P + np.arange(P)[:, None, None]
    end = np.arange(NCMP)[None, None, :] * CMP_STRIDE + CMP_LEN - 1
    return {
        "c_ident": np.eye(P, dtype=f), "c_causal": np.where(k <= q, 0.0, NEG).astype(f), "c_ones": np.full((P, P), 1.0 / D, f),
        "c_rot": rot, "c_cmask": np.where(end <= tok, 0.0, NEG).astype(f),
        "c_cos": np.ascontiguousarray(np.cos(ang).T.astype(f)), "c_sin": np.ascontiguousarray(np.sin(ang).T.astype(f)),
    }


def kernel(**inputs):
    import numpy as np
    import concourse.bacc as bacc
    from concourse.bass_utils import run_bass_kernel_spmd

    nc = bacc.Bacc("TRN2", target_bir_lowering=False, num_devices=1)
    arrays, t = {}, {}
    for name, a in [(n, inputs[n]) for n in _INS] + list(shape_constants().items()):
        a = np.ascontiguousarray(a)
        arrays[f"in_{name}"] = a
        t[name] = nc.dram_tensor(f"in_{name}", a.shape, F32, kind="ExternalInput").ap()
    t["cum"] = nc.dram_tensor("cum", (4, HEADS, SEQ), F32, kind="Internal").ap()
    out = nc.dram_tensor("out_0", (1, SEQ, D), F32, kind="ExternalOutput").ap()
    build_trunk(nc, t, out)
    r = run_bass_kernel_spmd(nc, [arrays], core_ids=[0])
    return r.results[0]["out_0"]
```

```python
from contextlib import ExitStack

import concourse.bass as bass
from concourse import mybir

F32 = mybir.dt.float32
F32R = mybir.dt.float32r
BF16 = mybir.dt.bfloat16
ALU = mybir.AluOpType
ACT = mybir.ActivationFunctionType
AX = mybir.AxisListType

P = 128
D, SEQ, DEPTH = 1024, 512, 2
HD = 64
HEADS = D // HD
GROUPS, REP = 4, 4
KV = GROUPS * HD
CMP_LEN, CMP_STRIDE, PHI = 32, 16, 256
NCMP = (SEQ - CMP_LEN) // CMP_STRIDE + 1
NG = 3 * HEADS
FF = 2816
FB = FF // P
KB = D // P
QT = SEQ // P
LP = CMP_LEN // 2
ALPHA = (2 * DEPTH) ** 0.25
EPS = 1e-5
SCALE = HD ** -0.5
NEG = -1e30
FLOOR = -1e28

R = 3
C_NSA = 0
C_WO0 = C_NSA + 4 + 4 * GROUPS
C_UP0 = C_WO0 + KB
C_DN0 = C_UP0 + 2 * FB
C_FOX = C_DN0 + 3 * KB
C_WO1 = C_FOX + 3 * KB
C_UP1 = C_WO1 + KB
C_DN1 = C_UP1 + 2 * FB
C_END = C_DN1 + 3 * KB
DN_BLOCKS = (8, 8, FB - 16)

NSA_UNITS = HEADS * QT * 2
FOX_UNITS = HEADS * QT
NSA_ITEMS = 4 * GROUPS
U_ACT = NSA_UNITS - 32
NSHIFT = 5
FOX_STEPS = [(0, 4), (4, 8), (8, 12), (12, 16), (16, 18), (18, 20), (20, 22), (22, 24)]
XL_DVE = (7,)
XL_POOL = tuple(k for k in range(KB) if k not in XL_DVE)
LESS_DVE = (0, 6, 7)
LESS_POOL = tuple(k for k in range(KB) if k not in LESS_DVE)


def build_trunk(nc, t, out):
    with ExitStack() as ctx:
        def sb(name, shape, dt=F32):
            return ctx.enter_context(nc.sbuf_tensor(name, shape, dt))

        def sem(name):
            return ctx.enter_context(nc.semaphore(name))

        xh = sb("xh", [P, KB, SEQ], F32R)
        xl = sb("xl", [P, KB, SEQ], F32R)
        raw = sb("raw", [P, R, KB, P])
        wh = sb("wh", [P, R, KB, P], F32R)
        wl = sb("wl", [P, R, KB, P], F32R)
        work = sb("work", [P, 5 * SEQ])
        ident = sb("ident", [P, P])
        identb = sb("identb", [P, P], BF16)
        causal = sb("causal", [P, P])
        causalb = sb("causalb", [P, P], BF16)
        onesd = sb("onesd", [P, P])
        rotm = sb("rotm", [P, P])
        cmask = sb("cmask", [P, QT, NCMP])
        conv_nat = sb("conv_nat", [FB * 2, 4, P])
        vec_nat = sb("vec_nat", [68, P])
        pe_nat = sb("pe_nat", [LP, P])
        conv = sb("conv", [P, DEPTH, 4, 2 * FB])
        vecs = sb("vecs", [P, 68])
        pe2 = sb("pe2", [P, LP])
        eps = sb("eps", [P, 1])
        bgate = sb("bgate", [NG, 1])
        gate = sb("gate", [P, QT, NG])
        kcd = sb("kcd", [P, GROUPS * NCMP])
        vcd = sb("vcd", [NCMP, GROUPS, HD])
        ghid = sb("ghid", [P, 2, GROUPS * NCMP])
        w2k = sb("w2k", [P, 2, HD])
        w2v = sb("w2v", [P, 2, HD])
        negmax = sb("negmax", [P, 4])
        psumrow = sb("psumrow", [P, 4])
        rinv = sb("rinv", [P, 4])
        ginv = sb("ginv", [P, 4])
        csm = sb("csm", [P, QT, NCMP])
        cstat = sb("cstat", [P, 4, QT])
        bf = sb("bf", [HEADS, 1])
        table = sb("table", [P, 1])
        warm = sb("warm", [P, P], BF16)
        ps = ctx.enter_context(nc.psum_tensor("ps", [P, 8, 512], F32))

        def overlay(*phases):
            made = []
            for n, phase in enumerate(phases):
                stay = ctx if n == len(phases) - 1 else ExitStack()
                made.append([stay.enter_context(nc.sbuf_tensor(name, shape, dt)) for name, shape, dt in phase])
                if stay is not ctx:
                    stay.close()
            return made

        (prob, pth, ptl), (cstack,), (z,) = overlay(
            [("prob", [P, 4, SEQ], F32), ("pth", [P, 2, SEQ], F32R), ("ptl", [P, 2, SEQ], F32R)],
            [("cstack", [P, 4, SEQ], F32R)],
            [("z", [P, KB, SEQ], F32)])

        def parities(names):
            return [(f"{name}{p}", shape, dt) for p in range(2) for name, shape, dt in names]

        o_parts = [("oh{}", [P, KB, SEQ], F32R), ("ol{}", [P, KB, SEQ], F32R)]
        nsa_state = [("qs", [P, REP, SEQ], F32R), ("ks", [P, 2, SEQ], F32R), ("kw", [P, 2, SEQ], F32R), ("vh", [P, QT, P], F32R), ("vl", [P, QT, P], F32R), ("qf", [P, 2, SEQ], F32)]
        fox_state = [("fqs", [P, 2, SEQ], F32R), ("fkd", [P, 2, 2, SEQ], F32R),
                     ("fvh", [P, QT, P], F32R), ("fvl", [P, QT, P], F32R), ("biasq", [P, 2, SEQ], F32R), ("biask", [P, 2, SEQ], F32R)]
        prologue, nsa, fox, (onat,), (gh, gl) = overlay(
            [("w1k", [P, LP, PHI], F32), ("w1v", [P, LP, PHI], F32), ("parity0", [P, 12 * SEQ], F32),
             ("kc2", [P, GROUPS, SEQ], F32), ("kp", [P, LP, GROUPS * NCMP], F32),
             ("wg_raw", [P, KB, NG], F32), ("wg_h", [P, KB, NG], F32R), ("wg_l", [P, KB, NG], F32R)],
            [("oh", [P, KB, SEQ], F32R), ("ol", [P, KB, SEQ], F32R)] + parities(nsa_state)
            + [("cosT", [P, SEQ], F32), ("sinT", [P, SEQ], F32)],
            [("oh2", [P, KB, SEQ], F32R), ("ol2", [P, KB, SEQ], F32R)] + parities(fox_state)
            + [("wf_raw", [P, KB, HEADS], F32), ("wf_h", [P, KB, HEADS], F32R), ("wf_l", [P, KB, HEADS], F32R),
               ("fz", [P, SEQ], F32), ("fe", [P, SEQ], F32), ("fone", [P, SEQ], F32), ("fcum", [P, SEQ], F32)],
            [("onat", [P, QT, D], F32)],
            [("gh", [P, FB, SEQ], F32R), ("gl", [P, FB, SEQ], F32R)])
        w1k, w1v, _, kc2, kp, wg_raw, wg_h, wg_l = prologue
        oh, ol = nsa[0:2]
        qs, ks, kw, vh, vl, qf = ([nsa[2 + n], nsa[8 + n]] for n in range(6))
        cosT, sinT = nsa[14:16]
        oh2, ol2 = fox[0:2]
        fqs, fkd, fvh, fvl, biasq, biask = ([fox[2 + n], fox[8 + n]] for n in range(6))
        wf_raw, wf_h, wf_l, fz, fe, fone, fcum = fox[14:21]
        halves = (slice(0, HD), slice(HD, P))
        xnat = z[:, :, :].rearrange("p (m a) s -> p m (a s)", m=QT)
        tmpf, rot1, rot2 = (work[:, n * SEQ:(n + 1) * SEQ] for n in range(3))
        gate_t = work[0:NG, 3 * SEQ:4 * SEQ]
        pct = work[:, 3 * SEQ:5 * SEQ].rearrange("p (a s) -> p a s", a=2)
        ua, ub, ga, gf = (work[:, n * SEQ:(n + 1) * SEQ] for n in range(4))
        zsum = work[:, 4 * SEQ:5 * SEQ]
        sq = work[:, 0:2 * SEQ].rearrange("p (a s) -> p a s", a=2)
        sqsum, shift = (work[:, n * SEQ:(n + 1) * SEQ] for n in (2, 3))
        rstd, std, var, delta = work[:, 0:SEQ], sqsum, shift, zsum

        BP, BX, BS, BT, BO = 0, 1, 2, 4, 6
        B_SHIFT, B_DELTA, B_SQ = 3, 4, 5
        B_DOWN = 6

        s_raw = [sem(f"raw_landed{n}") for n in range(R)]
        s_wh = sem("w_hi")
        s_wl = sem("w_lo")
        s_wu = sem("w_used")
        s_ld = [sem(f"loaded{n}") for n in range(12)]
        s_cst = sem("consts_ready")
        s_vt = sem("vectors_turned")
        s_vc = sem("vectors_ready")
        s_xn = [sem(f"x_landed{n}") for n in range(QT)]
        s_xt = sem("x_turned")
        s_xh = sem("x_hi")
        s_x = sem("x_lo")
        s_xp = sem("x_lo_pool")
        s_gw = sem("gate_w_split")
        s_gp = sem("gate_products")
        s_gt = sem("gates_turned")
        s_ge = sem("gate_steps")
        s_kc = sem("cmp_source")
        s_kp = sem("cmp_blocks")
        s_hid = sem("cmp_hidden")
        s_gel = sem("cmp_gelu")
        s_cmpo = sem("cmp_out")
        s_cmpr = sem("cmp_ready")
        s_pf = sem("proj_copied")
        s_px = sem("proj_turned")
        s_r1 = sem("rope_cos")
        s_r2 = sem("rope_sin")
        s_r3 = sem("rope_sum")
        s_ph = sem("proj_hi")
        s_pl = sem("proj_lo")
        s_pll = sem("proj_lo_first_half")
        s_phb = sem("odd_keys_hi")
        s_plb = sem("odd_keys_lo")
        s_sw = [sem(f"keys_doubled{p}") for p in range(2)]
        s_sc = sem("scores")
        s_nm = sem("neg_max")
        s_ex = sem("exps")
        s_ri = sem("sum_inverse")
        s_gi = sem("gated_inverse")
        s_pr = sem("probs")
        s_pt = sem("probs_turned")
        s_pth = sem("pt_hi")
        s_ptl = sem("pt_lo")
        s_pv = sem("pv_done")
        s_oh = sem("o_hi")
        s_ol = sem("o_lo")
        s_cs = sem("cmp_scores")
        s_cmask = sem("cmp_masked")
        s_cmax = sem("cmp_max")
        s_cfl = sem("cmp_max_finite")
        s_cdf = sem("cmp_differences")
        s_csum = sem("cmp_sum")
        s_csf = sem("cmp_sum_floored")
        s_cinv = sem("cmp_sum_inverse")
        s_cg = sem("cmp_gated_inverse")
        s_cp = sem("cmp_probs")
        s_ce = sem("cmp_exp")
        s_ct = sem("cmp_probs_turned")
        s_cc = sem("cmp_probs_copied")
        s_fw = sem("forget_w_split")
        s_fp = sem("forget_products")
        s_fa = sem("forget_act_steps")
        s_fd = sem("forget_dve_steps")
        s_fm = sem("forget_ones")
        s_cd = sem("cum_stored")
        s_bl = [sem(f"cum_rows{p}") for p in range(2)]
        s_c0 = sem("conv_tap2")
        s_c1 = sem("conv_tap1")
        s_c2 = sem("conv_tap0")
        s_gelu = sem("gelu")
        s_g = sem("gated")
        s_gh = sem("gated_hi")
        s_gl = sem("gated_lo")
        s_za = sem("z_from_lo")
        s_zb = sem("z_from_x")
        s_z1 = sem("z_whole")
        s_zs = sem("z_summed")
        s_zl = sem("x_less_shift")
        s_m1 = sem("shift_product")
        s_shift = sem("shift")
        s_cent = sem("shifted")
        s_sq = sem("squared")
        s_acc = sem("squares_summed")
        s_pa = sem("squares_product")
        s_m2 = sem("delta_products")
        s_e = sem("mean_square")
        s_dl = sem("delta_copied")
        s_d2 = sem("delta_squared")
        s_vr = sem("variance")
        s_sub = sem("centred_dve")
        s_subp = sem("centred_pool")
        s_std = sem("std")
        s_rstd = sem("rstd")
        s_nrm = sem("normed")
        s_y = sem("affine_dve")
        s_ya = sem("affine_act")
        s_yt = sem("y_turned")
        s_yc = sem("y_copied_act")
        s_yd = sem("y_copied_dve")
        s_out = sem("out_stored")

        block = ctx.enter_context(nc.Block())

        @block.sync
        def _(sp):
            small = [
                (ident[:, :], t["c_ident"]), (causal[:, :], t["c_causal"]), (onesd[:, :], t["c_ones"]),
                (rotm[:, :], t["c_rot"]), (cmask[:, :, :], t["c_cmask"]),
            ]
            for m in range(QT):
                sp.dma_start(xnat[:, m, :], t["x"][0, m * P:(m + 1) * P, :]).then_inc(s_xn[m], 16)
                if m == 0:
                    sp.dma_start(small[0][0], small[0][1]).then_inc(s_ld[0], 16)

            def load(c, slot, src, nk=KB):
                if not isinstance(c, int) or c >= R:
                    sp.wait_ge(s_wl, c - (R - 1))
                sp.dma_start(raw[:, slot, 0:nk, :], src).then_inc(s_raw[slot], 16)

            def cols(w, a):
                return w[:, bass.ds(a, P)].rearrange("(k p) c -> p k c", p=P)

            w_nsa = t["nsa_w_in"][0]
            for c in range(R):
                load(c, c % R, cols(w_nsa, D + c * P))
            sp.dma_start(wg_raw[:, :, :], t["nsa_w_in"][0][:, D + 6 * KV:D + 6 * KV + NG].rearrange("(k p) c -> p k c", p=P)).then_inc(s_ld[6], 16)
            sp.dma_start(bgate[:, :], t["nsa_b_gate"].rearrange("a n -> n a")).then_inc(s_ld[6], 16)
            sp.dma_start(pe_nat[:, :], t["nsa_pe"][0].rearrange("(l two) d -> l (two d)", two=2)).then_inc(s_ld[5], 16)
            sp.dma_start(vec_nat[0:16, :], t["ln1_g"].rearrange("l (k p) -> (l k) p", p=P)).then_inc(s_ld[5], 16)
            sp.dma_start(vec_nat[16:32, :], t["ln1_b"].rearrange("l (k p) -> (l k) p", p=P)).then_inc(s_ld[5], 16)
            sp.dma_start(vec_nat[32:48, :], t["ln2_g"].rearrange("l (k p) -> (l k) p", p=P)).then_inc(s_ld[5], 16)
            sp.dma_start(vec_nat[48:64, :], t["ln2_b"].rearrange("l (k p) -> (l k) p", p=P)).then_inc(s_ld[5], 16)
            sp.dma_start(vec_nat[64:66, :], t["nsa_phik_b1"].rearrange("l (k p) -> (l k) p", p=P)).then_inc(s_ld[5], 16)
            sp.dma_start(vec_nat[66:68, :], t["nsa_phiv_b1"].rearrange("l (k p) -> (l k) p", p=P)).then_inc(s_ld[5], 16)
            sp.dma_start(w1k[:, :, :], t["nsa_phik_w1"][0].rearrange("(k p) c -> p k c", p=P)).then_inc(s_ld[8], 16)
            load(3, 3 % R, cols(w_nsa, D + 3 * P))
            sp.dma_start(w2k[:, :, :], t["nsa_phik_w2"][0].rearrange("(k p) c -> p k c", p=P)).then_inc(s_ld[7], 16)
            sp.dma_start(w2v[:, :, :], t["nsa_phiv_w2"][0].rearrange("(k p) c -> p k c", p=P)).then_inc(s_ld[7], 16)
            for n, (dst, src) in enumerate(small[1:]):
                sp.dma_start(dst, src).then_inc(s_ld[1 + n], 16)
            sp.dma_start(w1v[:, :, :], t["nsa_phiv_w1"][0].rearrange("(k p) c -> p k c", p=P)).then_inc(s_ld[9], 16)
            sp.dma_start(cosT[:, :], t["c_cos"]).then_inc(s_ld[10], 16)
            sp.dma_start(sinT[:, :], t["c_sin"]).then_inc(s_ld[10], 16)
            sp.dma_start(conv_nat[:, 0:3, :], t["ffn_conv_w"][0].rearrange("w (b p) -> b w p", p=P)).then_inc(s_ld[11], 16)
            sp.dma_start(conv_nat[:, 3, :], t["ffn_conv_b"][0].rearrange("(b p) -> b p", p=P)).then_inc(s_ld[11], 16)
            wsv = w_nsa[:, D + 2 * KV:D + 6 * KV].rearrange("(k p) (two r) -> p k two r", p=P, two=2)
            for g in range(GROUPS):
                c = 4 + 4 * g
                for n, r0 in ((0, 0), (1, KV)):
                    sp.wait_ge(s_wl, c + n - (R - 1))
                    for b in range(2):
                        sp.dma_start(raw[:, (c + n) % R, :, b * HD:(b + 1) * HD],
                                     wsv[:, :, b, r0 + g * HD:r0 + (g + 1) * HD]).then_inc(s_raw[(c + n) % R], 16)
                for n in range(2):
                    load(c + 2 + n, (c + 2 + n) % R, cols(w_nsa, g * REP * HD + n * P))
                if g == 0:
                    sp.wait_ge(s_vt, 6)
                    sp.dma_start(conv_nat[:, 0:3, :], t["ffn_conv_w"][1].rearrange("w (b p) -> b w p", p=P)).then_inc(s_ld[11], 16)
                    sp.dma_start(conv_nat[:, 3, :], t["ffn_conv_b"][1].rearrange("(b p) -> b p", p=P)).then_inc(s_ld[11], 16)

            def load_out(c0, w):
                with sp.Fori(0, 2) as i:
                    for r in range(3):
                        load(c0 + 3 * i + r, (c0 + r) % R, cols(w, (3 * i + r) * P))
                for j in range(6, KB):
                    load(c0 + j, (c0 + j) % R, cols(w, j * P))

            def load_ffn(l, c_up, c_dn):
                up, dn = t["ffn_w_up"][l], t["ffn_w_down"][l]
                load(c_up, c_up % R, cols(up, 0))
                load(c_up + 1, (c_up + 1) % R, cols(up, FF))
                with sp.Fori(0, (FB - 1) // 3) as i:
                    for r in range(3):
                        c = c_up + 2 + 2 * r
                        load(c + 6 * i, c % R, cols(up, (1 + 3 * i + r) * P))
                        load(c + 1 + 6 * i, (c + 1) % R, cols(up, FF + (1 + 3 * i + r) * P))
                with sp.Fori(0, KB) as i:
                    for r in range(3):
                        nk = DN_BLOCKS[r]
                        src = dn[r * 8 * P:(r * 8 + nk) * P, bass.ds(i * P, P)].rearrange("(k p) c -> p k c", p=P)
                        load(c_dn + 3 * i + r, (c_dn + r) % R, src, nk)

            load_out(C_WO0, t["nsa_w_o"][0])
            load_ffn(0, C_UP0, C_DN0)

            w_fox = t["fox_w_in"][0]
            for r in range(3):
                load(C_FOX + r, (C_FOX + r) % R, cols(w_fox, r * D))
            sp.wait_ge(s_wu, C_FOX)
            sp.dma_start(wf_raw[:, :, :], w_fox[:, 3 * D:3 * D + HEADS].rearrange("(k p) c -> p k c", p=P)).then_inc(s_ld[6], 16)
            sp.dma_start(bf[:, :], t["fox_b_f"].rearrange("a h -> h a")).then_inc(s_ld[6], 16)
            for r in range(3):
                load(C_FOX + 3 + r, (C_FOX + r) % R, cols(w_fox, P + r * D))
            sp.wait_ge(s_fd, 7)
            sp.wait_ge(s_fm, 5)
            sp.dma_start(t["cum"].rearrange("r h s -> h r s"), cstack[0:HEADS, :, :].bitcast(F32)).then_inc(s_cd, 16)
            sp.wait_ge(s_cd, 16)

            def load_rows(pair, par, used):
                if used is not None:
                    sp.wait_ge(s_sc, used)
                sp.dma_start(biasq[par][2:4, :, :].bitcast(F32), t["cum"][0:2, bass.ds(2 * pair, 2), :]).then_inc(s_bl[par], 16)
                sp.dma_start(biask[par][0:2, :, :].bitcast(F32), t["cum"][2:4, bass.ds(2 * pair, 2), :]).then_inc(s_bl[par], 16)

            load_rows(0, 0, None)
            load_rows(1, 1, None)
            with sp.Fori(0, 3) as i:
                for par in range(2):
                    pair = 2 * i + par + 2
                    for r in range(3):
                        load(C_FOX + 3 * pair + r, (C_FOX + r) % R, cols(w_fox, pair * P + r * D))
                    load_rows(pair, par, NSA_UNITS + 8 * (2 * i + par + 1))
            load_out(C_WO1, t["fox_w_o"][0])
            load_ffn(1, C_UP1, C_DN1)
            for n in range(2 * QT):
                m, half = n % QT, n // QT
                sp.wait_ge((s_yc, s_yd)[m % 2], n // 2 + 1)
                sp.dma_start(out[0, m * P:(m + 1) * P, half * 512:(half + 1) * 512],
                             onat[:, m, half * 512:(half + 1) * 512]).then_inc(s_out, 16)
            sp.wait_ge(s_out, 16 * 2 * QT)

        @block.gpsimd
        def _(pool):
            def lo(c, slot, nk=KB):
                pool.wait_ge(s_wh, c + 1)
                nc.gpsimd.tensor_tensor(wl[:, slot, 0:nk, :], raw[:, slot, 0:nk, :],
                                        wh[:, slot, 0:nk, :].bitcast(F32), ALU.subtract).then_inc(s_wl, 1)

            def los(c0, n):
                with pool.Fori(0, n // R) as i:
                    for r in range(R):
                        lo(c0 + R * i + r, (c0 + r) % R)
                for c in range(c0 + n // R * R, c0 + n):
                    lo(c, c % R)

            def los_down(c0):
                with pool.Fori(0, KB) as i:
                    for r in range(R):
                        lo(c0 + R * i + r, (c0 + r) % R, DN_BLOCKS[r])

            def rope_pool(g, k):
                n, par = 4 * g + k, g % 2
                rn = n - (n + 2) // 4
                pool.wait_ge(s_pf, n + 1)
                if g == 0 and k == 0:
                    pool.wait_ge(s_ld[10], 32)
                if n:
                    pool.wait_ge(s_pl, n)
                nc.gpsimd.tensor_tensor(rot1, tmpf if k == 0 else qf[par][:, k - 2, :], cosT[:, :], ALU.mult).then_inc(s_r1, 1)
                pool.wait_ge(s_r1, rn + 1)
                pool.wait_ge(s_r2, rn + 1)
                nc.gpsimd.tensor_tensor(rot1, rot1, rot2, ALU.add).then_inc(s_r3, 1)
                pool.wait_ge(s_ph, n + 1)
                pool.wait_ge(s_r3, rn + 1)
                for h, rows in enumerate(halves):
                    dh, dl = ((ks, kw)[h][par][rows, 0, :], (ks, kw)[h][par][rows, 1, :]) if k == 0 else \
                        (qs[par][rows, 2 * (k - 2) + h, :], qs[par][halves[1 - h], 2 * (k - 2) + h, :])
                    nc.gpsimd.tensor_tensor(dl, rot1[rows, :], dh.bitcast(F32), ALU.subtract).then_inc((s_pll, s_pl)[h], 1)
                    pool.wait_ge((s_pll, s_pl)[h], (rn, n)[h] + 1)

            def ln_pool(n, final):
                pool.wait_ge(s_dl, n + 1)
                for k in LESS_POOL:
                    pool.wait_ge(s_cent, 8 * n + k + 1)
                    pool.wait_ge(s_sq, 8 * n + k + 1)
                    nc.gpsimd.tensor_tensor(z[:, k, :], z[:, k, :], delta, ALU.subtract).then_inc(s_subp, 1)
                if final:
                    return
                for k in XL_POOL:
                    pool.wait_ge(s_y, 8 * n + k + 1)
                    nc.gpsimd.tensor_tensor(xl[:, k, :], z[:, k, :], xh[:, k, :].bitcast(F32), ALU.subtract).then_inc(s_xp, 1)

            for c in range(7):
                lo(c, c % R)
            for n in range(NSA_ITEMS):
                if n % 4 != 1:
                    rope_pool(n // 4, n % 4)
                lo(n + 7, (n + 7) % R)
            los(NSA_ITEMS + 7, C_UP0 + 3 - (NSA_ITEMS + 7))
            ln_pool(0, False)
            los(C_UP0 + 3, C_DN0 - (C_UP0 + 3))
            los_down(C_DN0)
            los(C_FOX, 3)
            ln_pool(1, False)
            nc.gpsimd.memset(fone[:, :], 1.0).then_inc(s_fm, 1)
            lo(C_FOX + 3, C_FOX % R)
            for ones in [b[par][0:4, :, :].bitcast(F32) for par in range(2) for b in (biasq, biask)]:
                nc.gpsimd.memset(ones, 1.0).then_inc(s_fm, 1)
            los(C_FOX + 4, C_UP1 + 3 - (C_FOX + 4))
            ln_pool(2, False)
            los(C_UP1 + 3, C_DN1 - (C_UP1 + 3))
            los_down(C_DN1)
            ln_pool(3, True)

        @block.scalar
        def _(act):
            RAW_EXTRA = [0, 0, 0]
            for g in range(GROUPS):
                for n in range(2):
                    RAW_EXTRA[(4 + 4 * g + n) % R] += 1

            def landed(c):
                return sum(2 if 4 <= x < C_WO0 and (x - 4) % 4 < 2 else 1 for x in range(c + 1) if x % R == c % R)

            def hi(c, slot, nk=KB, n=None):
                act.wait_ge(s_raw[slot], 16 * (landed(c) if n is None else n))
                if not isinstance(c, int) or c >= R:
                    act.wait_ge(s_wu, c - (R - 1))
                nc.scalar.activation(wh[:, slot, 0:nk, :], raw[:, slot, 0:nk, :], ACT.Copy).then_inc(s_wh, 1)

            def hi_at(base, k, i=0, step=0, nk=KB):
                c = base + k
                n = c // R + 1 + RAW_EXTRA[c % R]
                hi(c + step * i if step else c, c % R, nk, n + (step // R) * i if step else n)

            for k in range(KB):
                act.wait_ge(s_xt, k + 1)
                nc.scalar.activation(xh[:, k, :], ps[:, k, :], ACT.Copy).then_inc(s_xh, 1)
                if k == 1:
                    hi(0, 0)
                if k == 4:
                    hi(1, 1)
            hi(2, 2)
            act.wait_ge(s_ld[6], 32)
            nc.scalar.activation(wg_h[:, :, :], wg_raw[:, :, :], ACT.Copy).then_inc(s_gw, 1)

            def cmp_source(c):
                act.wait_ge(s_wu, c + 1)
                if c >= 2:
                    act.wait_ge(s_kp, 8)
                for half in range(2):
                    g = 2 * (c % 2) + half
                    nc.scalar.activation(kc2[0:HD, g, :], ps[half * HD:(half + 1) * HD, c % 2, :], ACT.Copy)
                    last = nc.scalar.activation(kc2[HD:P, g, 0:SEQ - 1], ps[half * HD:(half + 1) * HD, c % 2, 1:SEQ], ACT.Copy)
                last.then_inc(s_kc, 1)

            def cmp_gelu(src):
                act.wait_ge(s_hid, src + 1)
                act.wait_ge(s_vc, 1)
                if src:
                    act.wait_ge(s_cmpo, 1)
                for hb in range(2):
                    last = nc.scalar.activation(ghid[:, hb, :], ps[:, 2, hb * P:hb * P + GROUPS * NCMP], ACT.Gelu_apprx_tanh,
                                                bias=vecs[:, 64 + 2 * src + hb:65 + 2 * src + hb])
                last.then_inc(s_gel, 1)

            for c in range(2):
                cmp_source(c)
                hi(c + 3, (c + 3) % R)
            cmp_source(2)
            hi(5, 5 % R)
            act.wait_ge(s_gt, 1)
            nc.scalar.activation(gate[:, :, :], ps[:, 4, 0:QT * NG].rearrange("p (m n) -> p m n", m=QT), ACT.Exp, scale=-1.0).then_inc(s_ge, 1)
            cmp_gelu(0)
            cmp_source(3)
            hi(6, 6 % R)
            act.wait_ge(s_cmpo, 1)
            nc.scalar.activation(kcd[0:HD, :], ps[0:HD, 3, 0:GROUPS * NCMP], ACT.Copy)
            nc.scalar.activation(kcd[HD:P, :], ps[0:HD, 3, 0:GROUPS * NCMP], ACT.Copy).then_inc(s_cmpr, 1)

            def item_copy(g, k):
                n = 4 * g + k
                act.wait_ge(s_wu, 4 + n + 1)
                if n and k < 2:
                    act.wait_ge(s_pl, n)
                if g >= 2:
                    act.wait_ge(s_pv, 32 * (g - 1))
                if k < 2:
                    nc.scalar.activation(tmpf, ps[:, BP, :], ACT.Copy).then_inc(s_pf, 1)
                else:
                    nc.scalar.activation(qf[g % 2][:, k - 2, :], ps[:, BP, :], ACT.Copy, scale=SCALE).then_inc(s_pf, 1)

            def item_hi(g, k):
                n, par = 4 * g + k, g % 2
                if k == 1:
                    act.wait_ge(s_px, n + 1)
                    nc.scalar.activation(vh[par][:, :, :], ps[:, BX, :].rearrange("p (m c) -> p m c", m=QT), ACT.Copy).then_inc(s_ph, 1)
                else:
                    act.wait_ge(s_r3, n - (n + 2) // 4 + 1)
                    for h, rows in enumerate(halves):
                        dst = (ks, kw)[h][par][rows, 0, :] if k == 0 else qs[par][rows, 2 * (k - 2) + h, :]
                        last = nc.scalar.activation(dst, rot1[rows, :], ACT.Copy)
                    last.then_inc(s_ph, 1)

            def double_keys(g):
                par = g % 2
                act.wait_ge(s_pl, 4 * g + 1)
                act.dma_start(ks[par][HD:P, :, :].bitcast(F32), ks[par][0:HD, :, :].bitcast(F32)).then_inc(s_sw[par], 16)
                act.dma_start(kw[par][0:HD, :, :].bitcast(F32), kw[par][HD:P, :, :].bitcast(F32)).then_inc(s_sw[par], 16)

            def unit_exp(u, loc):
                act.wait_ge(s_nm, u + 1)
                if not isinstance(u, int) or u >= 4:
                    act.wait_ge(s_pt, u - 3)
                i = loc[1]
                n = (i + 1) * P
                nc.scalar.activation(prob[:, loc[0] % 4, 0:n], ps[:, BS + loc[0] % 2, 0:n], ACT.Exp,
                                     bias=negmax[:, loc[0] % 4:loc[0] % 4 + 1],
                                     accum_out=psumrow[:, loc[0] % 4:loc[0] % 4 + 1]).then_inc(s_ex, 1)

            def unit_scale(u, loc, count, ready, factor):
                act.wait_ge(ready, count)
                i, b = loc[1], loc[0] % 4
                nc.scalar.activation(prob[:, b, 0:(i + 1) * P], prob[:, b, 0:(i + 1) * P], ACT.Copy, scale=factor[:, b:b + 1]).then_inc(s_pr, 1)

            def unit_hi(u, loc):
                act.wait_ge(s_pt, u + 1)
                if not isinstance(u, int) or u >= 2:
                    act.wait_ge(s_pv, u - 1)
                n = (loc[1] + 1) * P
                nc.scalar.activation(pth[:, loc[0] % 2, 0:n], ps[:, BT + loc[0] % 2, 0:n], ACT.Copy).then_inc(s_pth, 1)

            def head_hi(u_end, par, half, pair, oh=oh):
                act.wait_ge(s_pv, u_end)
                nc.scalar.activation(oh[half * HD:(half + 1) * HD, pair, :] if isinstance(pair, int) else
                                     oh[half * HD:(half + 1) * HD, bass.ds(pair, 1), :].rearrange("p a s -> p (a s)"),
                                     ps[0:HD, BO + par, :], ACT.Copy).then_inc(s_oh, 1)

            def cmp_exp(H):
                act.wait_ge(s_cdf, H + 1)
                nc.scalar.activation(csm[:, :, :], csm[:, :, :], ACT.Exp).then_inc(s_ce, 1)

            item_copy(0, 0)
            hi(7, 7 % R)
            cmp_gelu(1)
            item_hi(0, 0)
            item_copy(0, 1)
            hi(8, 8 % R)
            act.wait_ge(s_cmpo, 2)
            nc.scalar.activation(vcd[:, :, :], ps[0:NCMP, 4, 0:GROUPS * HD].rearrange("p (g d) -> p g d", g=GROUPS), ACT.Copy).then_inc(s_cmpr, 1)
            item_hi(0, 1)
            double_keys(0)
            item_copy(0, 2)
            hi(9, 9 % R)
            item_hi(0, 2)
            cmp_exp(0)
            item_copy(0, 3)
            for g in range(GROUPS):
                for v in range(32):
                    u, w = 32 * g + v, v % 8
                    item = (g, 3) if v < 8 else (g + 1, v // 8 - 1)
                    turned = v < 8 or g < GROUPS - 1
                    for x in ([0, 1, 2] if u == 0 else [v + 2]):
                        uu = 32 * g + x
                        if uu < NSA_UNITS:
                            unit_exp(uu, (uu, uu % 8 // 2))
                    if U_ACT <= u + 1 < NSA_UNITS:
                        unit_scale(u + 1, (u + 1, (u + 1) % 8 // 2), u + 2 - U_ACT, s_gi, ginv)
                    if w == 6 and u + 2 < NSA_UNITS:
                        cmp_exp(u // 8 + 1)
                    if w == 5 and turned and item[1] == 0:
                        double_keys(item[0])
                    if g < GROUPS - 1 and w == 7:
                        item_copy(g + 1, v // 8)
                    unit_hi(u, (u, w // 2))
                    if w == 0:
                        act.wait_ge(s_ct, u // 8 + 1)
                        nc.scalar.activation(pct[0:NCMP, u // 8 % 2, :], ps[0:NCMP, BX, :], ACT.Copy).then_inc(s_cc, 1)
                    if w == 2 and u > 8:
                        head_hi(u - 2, (u // 8 - 1) % 2, (u // 8 - 1) % 2, (u // 8 - 1) // 2)
                    if turned and w == (2 if item[1] == 1 else 3):
                        item_hi(*item)
                    if g < GROUPS - 1 and w == 4:
                        c = 4 + 4 * (g + 1) + v // 8
                        hi(c + 2, (c + 2) % R)
            head_hi(NSA_UNITS, 1, 1, KB - 1)

            def load_table(func):
                nc.scalar.activation(table[:, :], eps[:, :], func)

            def shift_act(n):
                act.wait_ge(s_m1, n + 1)
                nc.scalar.activation(shift, ps[:, B_SHIFT, :], ACT.Copy, scale=KB / NSHIFT).then_inc(s_shift, 1)
                load_table(ACT.Sqrt)

            def square(n, k):
                act.wait_ge(s_cent, 8 * n + k + 1)
                if k >= 2:
                    act.wait_ge(s_acc, 6 * n + max(k - 2, 1))
                nc.scalar.activation(sq[:, k % 2, :], z[:, k, :], ACT.Square).then_inc(s_sq, 1)

            def out_act(c0, n):
                with act.Fori(0, 2) as i:
                    for r in range(3):
                        hi_at(c0, r + 2, i, 3)
                shift_act(n)
                for k in range(4):
                    square(n, k)
                hi_at(c0, 8)
                square(n, 4)
                square(n, 5)
                hi_at(c0, 9)
                square(n, 6)
                hi_at(c0, 10)
                square(n, 7)

            def ln_act(n, final):
                g0 = (n // 2) * 8 + (0 if n % 2 == 0 else 32)
                act.wait_ge(s_m2, 2 * n + 2)
                nc.scalar.activation(var, ps[:, B_DELTA, :], ACT.Square).then_inc(s_d2, 1)
                nc.scalar.activation(delta, ps[:, B_DELTA, :], ACT.Copy).then_inc(s_dl, 1)
                act.wait_ge(s_vr, n + 1)
                nc.scalar.activation(std, var, ACT.Sqrt, bias=eps[:, 0:1]).then_inc(s_std, 1)
                if n == 1:
                    act.wait_ge(s_ld[6], 64)
                    nc.scalar.activation(wf_h[:, :, :], wf_raw[:, :, :], ACT.Copy).then_inc(s_fw, 1)
                for k in range(KB):
                    if final and k in (3, 6):
                        continue
                    act.wait_ge(s_nrm, 8 * n + k + 1)
                    scale, bias = vecs[:, g0 + k:g0 + k + 1], vecs[:, g0 + 16 + k:g0 + 17 + k]
                    if final:
                        nc.scalar.activation(z[:, k, :], z[:, k, :], ACT.Identity, scale=scale, bias=bias).then_inc(s_ya, 1)
                    else:
                        nc.scalar.activation(xh[:, k, :], z[:, k, :], ACT.Identity, scale=scale, bias=bias).then_inc(s_xh, 1)
                if not final:
                    load_table(ACT.Exp if n == 1 else ACT.Gelu_apprx_tanh)

            def ffn_act(l, c_up, c_dn, n):
                def pair(j, ca, i=0, step=0):
                    c = ca + step * i
                    jj = FB * l + j
                    hi_at(ca, 2 if step else 3, i, step)
                    act.wait_ge(s_wu, c + 1)
                    if not isinstance(j, int) or jj > 0:
                        act.wait_ge(s_g, jj)
                    bk = (ca - c_up) % 6
                    nc.scalar.activation(ua, ps[:, bk, :], ACT.Identity, scale=conv[:, l, 2, bass.ds(j, 1)],
                                         bias=conv[:, l, 3, bass.ds(j, 1)]).then_inc(s_c0, 1)
                    act.wait_ge(s_c2, 2 * jj + 1)
                    nc.scalar.activation(ga, ua, ACT.Gelu_apprx_tanh).then_inc(s_gelu, 1)
                    if step:
                        hi_at(ca, 3, i, step)
                    act.wait_ge(s_wu, c + 2)
                    nc.scalar.activation(ub, ps[:, bk + 1, :], ACT.Identity, scale=conv[:, l, 2, bass.ds(FB + j, 1)],
                                         bias=conv[:, l, 3, bass.ds(FB + j, 1)]).then_inc(s_c0, 1)
                    act.wait_ge(s_g, jj + 1)
                    nc.scalar.activation(gh[:, bass.ds(j, 1), :].rearrange("p a s -> p (a s)"), gf, ACT.Copy).then_inc(s_gh, 1)

                pair(0, c_up)
                with act.Fori(0, (FB - 1) // 3) as i:
                    for r in range(3):
                        pair(1 + 3 * i + r, c_up + 2 + 2 * r, i, 6)
                def dn_hi(j, r, i=0, step=0):
                    if j < KB - 1 or r == 0:
                        hi_at(c_dn + 3 * j, r + 2, i, step, DN_BLOCKS[(r + 2) % 3])
                    elif l == 0:
                        hi_at(c_dn + 3 * KB, r - 1)

                with act.Fori(0, KB - 3) as i:
                    for r in range(3):
                        dn_hi(0, r, i, 3)
                dn_hi(5, 0)
                shift_act(n)
                for k in range(4):
                    square(n, k)
                dn_hi(5, 1)
                square(n, 4)
                dn_hi(5, 2)
                dn_hi(6, 0)
                square(n, 5)
                dn_hi(6, 1)
                dn_hi(6, 2)
                dn_hi(7, 0)
                square(n, 6)
                dn_hi(7, 1)
                dn_hi(7, 2)
                if l == 0:
                    hi_at(c_dn + 3 * KB, 2)
                square(n, 7)

            out_act(C_WO0, 0)
            ln_act(0, False)
            ffn_act(0, C_UP0, C_DN0, 1)
            ln_act(1, False)

            def fox_q_hi(c, par):
                act.wait_ge(s_wu, c + 1)
                for h, rows in enumerate(halves):
                    last = nc.scalar.activation(fqs[par][rows, h, :], ps[rows, BP, :], ACT.Copy, scale=SCALE)
                last.then_inc(s_ph, 1)

            def fox_k_hi(c, par, h):
                act.wait_ge(s_wu, c + 1)
                for rows in halves:
                    last = nc.scalar.activation(fkd[par][rows, h, 0, :], ps[halves[h], BX, :], ACT.Copy)
                last.then_inc((s_ph, s_phb)[h], 1)

            act.wait_ge(s_fd, 1)
            nc.scalar.activation(fe[0:HEADS, :], fz[0:HEADS, :], ACT.Abs).then_inc(s_fa, 1)
            act.wait_ge(s_fa, 1)
            nc.scalar.activation(fe[0:HEADS, :], fe[0:HEADS, :], ACT.Exp, scale=-1.0).then_inc(s_fa, 1)
            fox_q_hi(C_FOX, 0)
            hi_at(C_FOX, 3)
            act.wait_ge(s_fd, 2)
            nc.scalar.activation(fe[0:HEADS, :], fe[0:HEADS, :], ACT.Ln).then_inc(s_fa, 1)
            fox_k_hi(C_FOX + 1, 0, 0)
            act.wait_ge(s_fd, 4)
            nc.scalar.activation(cstack[0:HEADS, 0, :], fcum[0:HEADS, :], ACT.Copy).then_inc(s_fa, 1)
            fox_k_hi(C_FOX + 1, 0, 1)
            load_table(ACT.Exp)
            hi_at(C_FOX, 4)

            def fox_value_copy(c, n_lo, bank=BP):
                act.wait_ge(s_wu, c + 1)
                act.wait_ge(s_pl, n_lo)
                nc.scalar.activation(tmpf, ps[:, bank, :], ACT.Copy).then_inc(s_pf, 1)

            fox_value_copy(C_FOX + 2, NSA_ITEMS, BT + 1)
            act.wait_ge(s_px, NSA_ITEMS + 1)
            nc.scalar.activation(fvh[0][:, :, :], ps[:, BO + 1, :].rearrange("p (m c) -> p m c", m=QT), ACT.Copy).then_inc(s_ph, 1)

            def fox_value_hi(par, nv, used):
                act.wait_ge(s_px, nv)
                act.wait_ge(s_pv, used)
                nc.scalar.activation(fvh[par][:, :, :], ps[:, BX, :].rearrange("p (m c) -> p m c", m=QT), ACT.Copy).then_inc(s_ph, 1)

            def fox_stages(pair, p0, i, step, first=False, more=True):
                par = p0 % 2
                U = NSA_UNITS + 8 * pair
                for v in range(8):
                    if more or v + 2 < 8:
                        unit_exp(U + v + 2, (v + 2, (v + 2) % 4))
                    if more and v == 7:
                        fox_value_copy(C_FOX + 3 * (pair + 1) + 2, NSA_ITEMS + 3 * (pair + 1))
                    unit_hi(U + v, (v, v % 4))
                    if v == 0 and not first:
                        fox_value_hi(par, NSA_ITEMS + pair + 1, U - 8)
                    if v == 1 and not first:
                        head_hi(U, 1, 1, pair - 1, oh2)
                    if v == 5:
                        head_hi(U + 4, 0, 0, pair, oh2)
                    if more and v in (1, 3, 5):
                        act.wait_ge(s_sc, U)
                    if more and v == 1:
                        fox_q_hi(C_FOX + 3 * (pair + 1), 1 - par)
                    if more and v in (3, 5):
                        fox_k_hi(C_FOX + 3 * (pair + 1) + 1, 1 - par, v // 2 - 1)
                    if more and v in (0, 2, 5):
                        hi_at(C_FOX, 3 * (p0 + 1) + (0, 2, 5).index(v) + 2, i, 3 * step)

            act.wait_ge(s_cd, 16)
            unit_exp(NSA_UNITS, (0, 0))
            unit_exp(NSA_UNITS + 1, (1, 1))
            fox_stages(0, 0, 0, 0, first=True)
            with act.Fori(0, 3) as i:
                for r in range(2):
                    fox_stages(1 + r + 2 * i, 1 + r, i, 2)
            fox_stages(7, 7, 0, 0, more=False)
            head_hi(NSA_UNITS + FOX_UNITS, 1, 1, KB - 1, oh2)

            out_act(C_WO1, 2)
            ln_act(2, False)
            ffn_act(1, C_UP1, C_DN1, 3)
            ln_act(3, True)
            for half in range(2):
                for m in range(0, QT, 2):
                    act.wait_ge(s_yt, 4 * half + m + 1)
                    nc.scalar.activation(onat[:, m, half * 512:(half + 1) * 512], ps[:, 2 * m + half, :], ACT.Copy).then_inc(s_yc, 1)

        @block.tensor
        def _(pe):
            def mm3(o, ah, al, bh, bl, start, stop):
                nc.tensor.matmul(o, ah, bh, start=start, stop=False)
                nc.tensor.matmul(o, ah, bl, start=False, stop=False)
                return nc.tensor.matmul(o, al, bh, start=False, stop=stop)

            def keep_warm(n, bank):
                for _ in range(n):
                    nc.tensor.matmul(ps[:, bank, :], warm[:, :], warm[:, :].unsqueeze(1).to_broadcast([P, QT, P]), start=True, stop=True)

            pe.wait_ge(s_cst, 2)
            keep_warm(8, KB - 1)
            pe.wait_ge(s_ld[0], 16)
            for k in range(KB):
                for m in range(QT):
                    if k == 0:
                        pe.wait_ge(s_xn[m], 16)
                    last = nc.tensor.transpose(ps[:, k, m * P:(m + 1) * P], xnat[:, m, k * P:(k + 1) * P], ident[:, :])
                last.then_inc(s_xt, 1)

            def chunk(c, slot, bank, srch, srcl, k0=0, nk=KB, first=True, final=True):
                pe.wait_ge(s_wl, c + 1)
                for k in range(nk):
                    last = mm3(ps[:, bank, :], wh[:, slot, k, :], wl[:, slot, k, :], srch[:, k0 + k, :], srcl[:, k0 + k, :],
                               first and k == 0, final and k == nk - 1)
                last.then_inc(s_wu, 1)

            def kstep(c, slot, k, bank=BP):
                if k == 0:
                    pe.wait_ge(s_wl, c + 1)
                last = mm3(ps[:, bank, :], wh[:, slot, k, :], wl[:, slot, k, :], xh[:, k, :], xl[:, k, :], k == 0, k == KB - 1)
                if k == KB - 1:
                    last.then_inc(s_wu, 1)

            def x_fresh(n, k):
                if n == 0:
                    pe.wait_ge(s_x, k + 1)
                elif k in XL_DVE:
                    pe.wait_ge(s_x, KB + len(XL_DVE) * (n - 1) + XL_DVE.index(k) + 1)
                else:
                    pe.wait_ge(s_xp, len(XL_POOL) * (n - 1) + XL_POOL.index(k) + 1)

            def fresh_products(n, k, products):
                pe.wait_ge(s_xh, KB * n + k + 1)
                for o, w_h, w_l in products:
                    nc.tensor.matmul(o, w_h, xh[:, k, :], start=k == 0, stop=False)
                    nc.tensor.matmul(o, w_l, xh[:, k, :], start=False, stop=False)
                x_fresh(n, k)
                return [nc.tensor.matmul(o, w_h, xl[:, k, :], start=False, stop=k == KB - 1) for o, w_h, w_l in products]

            for k in range(KB):
                x_fresh(0, k)
                kstep(0, 0, k)
            chunk(1, 1, BX, xh, xl)
            pe.wait_ge(s_gw, 2)
            for k in range(KB):
                last = mm3(ps[0:NG, 5, :], wg_h[:, k, :], wg_l[:, k, :], xh[:, k, :], xl[:, k, :], k == 0, k == KB - 1)
            last.then_inc(s_gp, 1)
            pe.wait_ge(s_ld[5], 16 * 7)
            nc.tensor.transpose(ps[:, 6, 0:68], vec_nat[:, :], ident[0:68, 0:68]).then_inc(s_vt, 1)
            nc.tensor.transpose(ps[:, 6, 128:128 + LP], pe_nat[:, :], ident[0:LP, 0:LP]).then_inc(s_vt, 1)
            pe.wait_ge(s_kc, 1)
            chunk(2, 2, BP, xh, xl)
            pe.wait_ge(s_ge, 1)
            for m in range(QT):
                last = nc.tensor.transpose(ps[:, 4, m * NG:(m + 1) * NG], gate_t[:, m * P:(m + 1) * P], ident[0:NG, 0:NG])
            last.then_inc(s_gt, 1)

            def cmp_hidden(src):
                pe.wait_ge(s_kp, 8 * (src + 1))
                pe.wait_ge(s_ld[8 + src], 16)
                if src:
                    pe.wait_ge(s_gel, 1)
                for hb in range(2):
                    for lp in range(LP):
                        last = nc.tensor.matmul(ps[:, 2, hb * P:hb * P + GROUPS * NCMP], (w1k, w1v)[src][:, lp, hb * P:(hb + 1) * P],
                                                kp[:, lp, :], start=(lp == 0), stop=(lp == LP - 1))
                last.then_inc(s_hid, 1)

            def conv_turn(l):
                pe.wait_ge(s_ld[11], 32 * (l + 1))
                if l:
                    pe.wait_ge(s_vc, 3)
                for w in range(4):
                    nc.tensor.transpose(ps[:, 7, w * P:w * P + 2 * FB], conv_nat[:, w, :], ident[0:2 * FB, 0:2 * FB]).then_inc(s_vt, 1)

            cmp_hidden(0)
            pe.wait_ge(s_kc, 2)
            chunk(3, 0, BX, xh, xl)
            pe.wait_ge(s_gel, 1)
            pe.wait_ge(s_ld[7], 32)
            for hb in range(2):
                last = nc.tensor.matmul(ps[0:HD, 3, 0:GROUPS * NCMP], w2k[:, hb, :], ghid[:, hb, :], start=(hb == 0), stop=(hb == 1))
            last.then_inc(s_cmpo, 1)

            def item_turn(g, k):
                n = 4 * g + k
                pe.wait_ge(s_pf, n + 1)
                if k == 1:
                    for m in range(QT):
                        last = nc.tensor.transpose(ps[:, BX, m * P:(m + 1) * P], tmpf[:, m * P:(m + 1) * P], ident[:, :])
                else:
                    src = tmpf if k == 0 else qf[g % 2][:, k - 2, :]
                    last = nc.tensor.matmul(ps[:, BX, :], rotm[:, :], src, start=True, stop=True)
                last.then_inc(s_px, 1)

            def item_steps(n):
                if n:
                    pe.wait_ge(s_pf, n)
                for kk in range(KB):
                    kstep(4 + n, (4 + n) % R, kk)

            pe.wait_ge(s_kc, 3)
            item_steps(0)
            conv_turn(0)
            cmp_hidden(1)
            pe.wait_ge(s_ld[3], 16)
            pe.wait_ge(s_kc, 4)
            item_turn(0, 0)
            item_steps(1)
            pe.wait_ge(s_gel, 2)
            for g in range(GROUPS):
                for hb in range(2):
                    last = nc.tensor.matmul(ps[0:NCMP, 4, g * HD:(g + 1) * HD], ghid[:, hb, g * NCMP:(g + 1) * NCMP], w2v[:, hb, :],
                                            start=(hb == 0), stop=(hb == 1))
            last.then_inc(s_cmpo, 1)
            pe.wait_ge(s_pl, 1)
            item_turn(0, 1)
            item_steps(2)
            conv_turn(1)
            pe.wait_ge(s_pl, 2)
            item_turn(0, 2)

            def mask(bank, i, stop=True):
                return nc.tensor.matmul(ps[:, bank, i * P:(i + 1) * P], identb[:, :], causalb[:, :], start=False, stop=stop)

            def nsa_scores(u):
                g, v = u // 32, u % 32
                h, i, br = v // 8, v % 8 // 2, v % 2
                par = g % 2
                if v % 8 == 0:
                    pe.wait_ge(s_pl, 4 * g + 3 + h // 2)
                    if h == 0:
                        pe.wait_ge(s_sw[par], 32 * (g // 2 + 1))
                if u >= 2:
                    pe.wait_ge(s_ex, u - 1)
                n, b = (i + 1) * P, BS + u % 2
                for part in range(2):
                    nc.tensor.matmul(ps[:, b, 0:n], qs[par][:, h, i * P:n], (ks, kw)[br][par][:, part, 0:n], start=part == 0, stop=False)
                mask(b, i).then_inc(s_sc, 1)

            def cmp_scores(H):
                g, h = H // 4, H % 4
                rows = slice(h % 2 * HD, h % 2 * HD + HD)
                n = min(H + 3, NSA_ITEMS) - 1
                if n % 4 == 1:
                    pe.wait_ge(s_pl, n + 1)
                else:
                    pe.wait_ge(s_r2, n - (n + 2) // 4 + 1)
                pe.wait_ge(s_pf, 4 * g + 3 + h // 2)
                for i in range(QT):
                    last = nc.tensor.matmul(ps[:, BX, i * NCMP:(i + 1) * NCMP], qf[g % 2][rows, h // 2, i * P:(i + 1) * P],
                                            kcd[rows, g * NCMP:(g + 1) * NCMP], start=True, stop=True)
                last.then_inc(s_cs, 1)

            def cmp_turn(H):
                pe.wait_ge(s_cp, H + 1)
                for i in range(QT):
                    last = nc.tensor.transpose(ps[0:NCMP, BX, i * P:(i + 1) * P], csm[:, i, :], ident[:, :])
                last.then_inc(s_ct, 1)

            def turn(u, loc):
                pe.wait_ge(s_pr, u + 1)
                if not isinstance(u, int) or u >= 2:
                    pe.wait_ge(s_ptl, u - 1)
                for kt in range(loc[1] + 1):
                    last = nc.tensor.transpose(ps[:, BT + loc[0] % 2, kt * P:(kt + 1) * P], prob[:, loc[0] % 4, kt * P:(kt + 1) * P], ident[:, :])
                last.then_inc(s_pt, 1)

            def pv(u, loc, bank, v_h, v_l, start, stop):
                pe.wait_ge(s_ptl, u + 1)
                i, b = loc[1], loc[0] % 2
                o = ps[0:HD, bank, i * P:(i + 1) * P]
                for kt in range(i + 1):
                    last = mm3(o, v_h[:, kt, :], v_l[:, kt, :], pth[:, b, kt * P:(kt + 1) * P], ptl[:, b, kt * P:(kt + 1) * P],
                               start and kt == 0, stop and kt == i)
                last.then_inc(s_pv, 1)

            def nsa_pv(u):
                g, v = u // 32, u % 32
                h, i, br = v // 8, v % 8 // 2, v % 2
                H = 4 * g + h
                bank = BO + H % 2
                if v % 8 == 0:
                    if H >= 2:
                        pe.wait_ge(s_ol, H - 1)
                    pe.wait_ge(s_cc, H + 1)
                if br == 0:
                    nc.tensor.matmul(ps[0:HD, bank, i * P:(i + 1) * P], vcd[:, g, :], pct[0:NCMP, H % 2, i * P:(i + 1) * P], start=True, stop=False)
                cs = slice(br * HD, (br + 1) * HD)
                pv(u, (u, i), bank, vh[g % 2][:, :, cs], vl[g % 2][:, :, cs], False, br == 1)

            pe.wait_ge(s_cst, 4)
            pe.wait_ge(s_cmpr, 2)
            cmp_scores(0)
            item_steps(3)
            pe.wait_ge(s_vc, 4)
            pe.wait_ge(s_ge, 4)
            nsa_scores(0)
            nsa_scores(1)
            for g in range(GROUPS):
                for v in range(32):
                    u = 32 * g + v
                    if u + 2 < NSA_UNITS:
                        nsa_scores(u + 2)
                    if v % 8 == 0:
                        turn(u, (u, v % 8 // 2))
                    if g < GROUPS - 1:
                        n = 4 * (g + 1) + v // 8
                        if v % 8 == 0:
                            pe.wait_ge(s_pf, n)
                        kstep(4 + n, (4 + n) % R, v % 8)
                    if v % 8 == 4 and u + 4 < NSA_UNITS:
                        cmp_scores(u // 8 + 1)
                    if u >= 2:
                        nsa_pv(u - 2)
                    if v % 8 == 0:
                        cmp_turn(u // 8)
                    else:
                        turn(u, (u, v % 8 // 2))
                    if v % 8 == 1 and (g < GROUPS - 1 or v == 1):
                        pe.wait_ge(s_cc, u // 8 + 1)
                        item_turn(*((g + 1, v // 8 - 1) if v > 1 else (g, 3)))
            nsa_pv(NSA_UNITS - 2)
            nsa_pv(NSA_UNITS - 1)

            def mean_matmul(bank, src, start, stop, done):
                nc.tensor.matmul(ps[:, bank, :], onesd[:, :], src, start=start, stop=stop).then_inc(done, 1)

            def ln_step(n, j, kk):
                if (j, kk) == (NSHIFT, 3):
                    pe.wait_ge(s_zs, 5 * n + 4)
                    mean_matmul(B_SHIFT, zsum, True, True, s_m1)
                if (j, kk) == (KB - 1, 6):
                    pe.wait_ge(s_zs, 5 * (n + 1))
                    mean_matmul(B_DELTA, zsum, True, False, s_m2)
                    pe.wait_ge(s_acc, 6 * (n + 1))
                    mean_matmul(B_SQ, sqsum, True, False, s_pa)

            def ln_pe(n):
                pe.wait_ge(s_cent, 8 * (n + 1))
                mean_matmul(B_DELTA, z[:, 7, :], False, True, s_m2)
                pe.wait_ge(s_sq, 8 * (n + 1))
                mean_matmul(B_SQ, sq[:, 1, :], False, True, s_e)
                keep_warm(32, 2)

            def out_pe(c0, heads, n, oh, ol):
                pe.wait_ge(s_ol, heads - 2)
                pe.wait_ge(s_ld[2], 16)
                for j in range(KB):
                    c, bank = c0 + j, j % 3
                    if j >= 3:
                        pe.wait_ge(s_z1, NSHIFT * n + j - 2)
                    pe.wait_ge(s_wl, c + 1)
                    for k in range(KB):
                        if j == 0 and k == KB - 1:
                            pe.wait_ge(s_ol, heads)
                        last = mm3(ps[:, bank, :], wh[:, c % R, k, :], wl[:, c % R, k, :], oh[:, k, :], ol[:, k, :], k == 0, k == KB - 1)
                        if k == KB - 1:
                            last.then_inc(s_wu, 1)
                        ln_step(n, j, k)
                ln_pe(n)

            def ffn_pe(l, c_up, c_dn, fresh, n):
                pe.wait_ge(s_wl, c_up + 2)
                for k in range(KB):
                    last = fresh_products(fresh, k, [(ps[:, r, :], wh[:, (c_up + r) % R, k, :], wl[:, (c_up + r) % R, k, :])
                                                     for r in range(2)])[-1]
                last.then_inc(s_wu, 2)
                with pe.Fori(0, (FB - 1) // 3) as i:
                    for r in range(3):
                        for b in range(2):
                            c = c_up + 2 + 2 * r + b
                            chunk(c + 6 * i, c % R, (c - c_up) % 6, xh, xl)

                def down(j, bank, i=0, first=False):
                    if not first:
                        if j == KB - 1:
                            pe.wait_ge(s_cent, 8 * n + j - 1)
                        else:
                            pe.wait_ge(s_z1, NSHIFT * n + j + i - 1)
                    for r in range(3):
                        c = c_dn + 3 * j + r
                        if first:
                            pe.wait_ge(s_gl, FB * l + 8 * r + DN_BLOCKS[r])
                        pe.wait_ge(s_wl, c + 3 * i + 1)
                        for k in range(DN_BLOCKS[r]):
                            kk = 8 * r + k
                            last = mm3(ps[:, bank, :], wh[:, c % R, k, :], wl[:, c % R, k, :], gh[:, kk, :], gl[:, kk, :], kk == 0, kk == FB - 1)
                            if k == DN_BLOCKS[r] - 1:
                                last.then_inc(s_wu, 1)
                            if isinstance(i, int):
                                ln_step(n, j, kk)

                down(0, B_DOWN, first=True)
                with pe.Fori(0, 2) as i:
                    for q in range(2):
                        down(1 + q, B_DOWN + 1 - q, 2 * i)
                for j in range(5, KB):
                    down(j, B_DOWN + j % 2)
                ln_pe(n)

            out_pe(C_WO0, HEADS, 0, oh, ol)
            ffn_pe(0, C_UP0, C_DN0, 1, 1)

            pe.wait_ge(s_fw, 2)
            pe.wait_ge(s_wl, C_FOX + 2)
            for k in range(KB):
                forget, queries, keys = fresh_products(2, k, [(ps[0:HEADS, BT, :], wf_h[:, k, :], wf_l[:, k, :])] + [
                    (ps[:, bank, :], wh[:, (C_FOX + r) % R, k, :], wl[:, (C_FOX + r) % R, k, :]) for r, bank in enumerate((BP, BX))])
            forget.then_inc(s_fp, 1)
            queries.then_inc(s_wu, 1)
            keys.then_inc(s_wu, 1)

            def value_turn(n, bank=BX):
                pe.wait_ge(s_pf, n)
                for m in range(QT):
                    last = nc.tensor.transpose(ps[:, bank, m * P:(m + 1) * P], tmpf[:, m * P:(m + 1) * P], ident[:, :])
                last.then_inc(s_px, 1)

            for k in range(KB):
                kstep(C_FOX + 2, (C_FOX + 2) % R, k, BT + 1)

            def fox_scores(u, v, par, pair, rows_landed):
                h, i = v // 4, v % 4
                if v == 0:
                    pe.wait_ge(s_pl, NSA_ITEMS + 3 * pair + 2)
                    pe.wait_ge(s_bl[par], rows_landed)
                if v == 4:
                    pe.wait_ge(s_plb, pair + 1)
                pe.wait_ge(s_ex, u - 1)
                n, b = (i + 1) * P, BS + v % 2
                for part in range(2):
                    nc.tensor.matmul(ps[:, b, 0:n], fqs[par][:, h, i * P:n], fkd[par][:, h, part, 0:n], start=part == 0, stop=False)
                nc.tensor.matmul(ps[:, b, 0:n], biasq[par][0:4, h, i * P:n], biask[par][0:4, h, 0:n], start=False, stop=False)
                mask(b, i).then_inc(s_sc, 1)

            def fox_pv(u, v, par, pair):
                h, i = v // 4, v % 4
                if i == 0:
                    pe.wait_ge(s_ol, HEADS + 2 * pair + h - 1)
                if v == 0:
                    pe.wait_ge(s_pl, NSA_ITEMS + 3 * pair + 3)
                cs = slice(h * HD, (h + 1) * HD)
                pv(u, (v, i), BO + h, fvh[par][:, :, cs], fvl[par][:, :, cs], True, True)

            def fox_stages(pair, par, rows_next, first=False, more=True):
                U = NSA_UNITS + 8 * pair
                for v in range(8):
                    if v + 2 < 8:
                        fox_scores(U + v + 2, v + 2, par, pair, None)
                    elif more:
                        fox_scores(U + v + 2, v - 6, 1 - par, pair + 1, rows_next)
                    if v == 0:
                        turn(U + v, (v, v % 4))
                    if more:
                        for s in range(*FOX_STEPS[v]):
                            if first and s < KB:
                                continue
                            r, k = s // KB, s % KB
                            if k == 0 and r:
                                pe.wait_ge(s_pl, NSA_ITEMS + 3 * (pair + 1) + r - 1)
                            if k == 0 and not r:
                                pe.wait_ge(s_pf, NSA_ITEMS + pair + 1)
                            kstep(C_FOX + 3 * (pair + 1) + r, (C_FOX + r) % R, k, (BP, BX, BP)[r])
                    if v >= 2:
                        fox_pv(U + v - 2, v - 2, par, pair)
                    elif not first:
                        fox_pv(U + v - 2, v + 6, 1 - par, pair - 1)
                    if v:
                        turn(U + v, (v, v % 4))
                    if v == 0 and not first:
                        pe.wait_ge(s_plb, pair + 1)
                        value_turn(NSA_ITEMS + pair + 1)

            pe.wait_ge(s_pl, NSA_ITEMS + 1)
            for k in range(KB):
                kstep(C_FOX + 3, C_FOX % R, k)
            value_turn(NSA_ITEMS + 1, BO + 1)
            fox_scores(NSA_UNITS, 0, 0, 0, 32)
            fox_scores(NSA_UNITS + 1, 1, 0, 0, None)
            fox_stages(0, 0, 32, first=True)
            with pe.Fori(0, 3) as i:
                for r in range(2):
                    fox_stages(1 + r + 2 * i, (1 + r) % 2, 32 * (2 + i))
            fox_stages(7, 1, None, more=False)
            fox_pv(NSA_UNITS + FOX_UNITS - 2, 6, 1, 7)
            fox_pv(NSA_UNITS + FOX_UNITS - 1, 7, 1, 7)

            out_pe(C_WO1, 2 * HEADS, 2, oh2, ol2)
            ffn_pe(1, C_UP1, C_DN1, 3, 3)
            for k in range(KB):
                if k in (3, 6):
                    pe.wait_ge(s_y, 3 * KB + k // 3)
                else:
                    pe.wait_ge(s_ya, k + 1 - k // 3)
                for m in range(QT):
                    last = nc.tensor.transpose(ps[:, 2 * m + k // 4, k % 4 * P:(k % 4 + 1) * P], z[:, k, m * P:(m + 1) * P], ident[:, :])
                    if k % 4 == 3:
                        last.then_inc(s_yt, 1)

        @block.vector
        def _(dve):
            nc.vector.memset(eps[:, :], EPS).then_inc(s_cst, 1)
            nc.vector.memset(warm[:, :], 0.0).then_inc(s_cst, 1)
            dve.wait_ge(s_ld[0], 16)
            nc.vector.tensor_copy(identb[:, :], ident[:, :]).then_inc(s_cst, 1)
            for k in range(KB):
                dve.wait_ge(s_xh, k + 1)
                nc.vector.tensor_tensor(xl[:, k, :], ps[:, k, :], xh[:, k, :].bitcast(F32), ALU.subtract).then_inc(s_x, 1)
            dve.wait_ge(s_gw, 1)
            nc.vector.tensor_tensor(wg_l[:, :, :], wg_raw[:, :, :], wg_h[:, :, :].bitcast(F32), ALU.subtract).then_inc(s_gw, 1)
            def cmp_blocks(src):
                dve.wait_ge(s_vc, 2)
                if src:
                    dve.wait_ge(s_hid, 1)
                for g in range(GROUPS):
                    if g % 2 == 0:
                        dve.wait_ge(s_kc, 2 * src + g // 2 + 1)
                    view = kc2[:, g, :].rearrange("p (n l two) -> p l n two", l=8, two=2)
                    for h in range(2):
                        nc.vector.tensor_tensor(kp[:, 8 * h:8 * h + 8, g * NCMP:(g + 1) * NCMP], view[:, :, h:h + NCMP, 0],
                                                pe2[:, 8 * h:8 * h + 8].unsqueeze(2).to_broadcast([P, 8, NCMP]), ALU.add).then_inc(s_kp, 1)

            dve.wait_ge(s_gp, 1)
            nc.vector.tensor_scalar(gate_t, ps[0:NG, 5, :], bgate[:, 0:1], None, ALU.add).then_inc(s_ge, 1)
            dve.wait_ge(s_vt, 2)
            nc.vector.tensor_copy(vecs[:, :], ps[:, 6, 0:68]).then_inc(s_vc, 1)
            nc.vector.tensor_copy(pe2[:, :], ps[:, 6, 128:128 + LP]).then_inc(s_vc, 1)
            cmp_blocks(0)
            dve.wait_ge(s_ge, 2)
            nc.vector.tensor_scalar(gate[:, :, :], gate[:, :, :], 1.0, None, ALU.add).then_inc(s_ge, 1)
            dve.wait_ge(s_ge, 3)
            nc.vector.reciprocal(gate[:, :, :], gate[:, :, :]).then_inc(s_ge, 1)
            for n in range(4):
                dve.wait_ge(s_ld[1 + n], 16)
            nc.vector.tensor_copy(causalb[:, :], causal[:, :]).then_inc(s_cst, 1)
            cmp_blocks(1)

            def conv_copy(l):
                dve.wait_ge(s_vt, 6 + 4 * l)
                nc.vector.tensor_copy(conv[:, l, :, :], ps[:, 7, :].rearrange("p (w c) -> p w c", w=4)[:, :, 0:2 * FB]).then_inc(s_vc, 1)

            conv_copy(0)

            dve.wait_ge(s_ld[10], 32)

            def item_dve(g, k):
                n, par = 4 * g + k, g % 2
                dve.wait_ge(s_px, n + 1)
                if k == 1:
                    dve.wait_ge(s_ph, n + 1)
                    nc.vector.tensor_tensor(vl[par][:, :, :], ps[:, BX, :].rearrange("p (m c) -> p m c", m=QT), vh[par][:, :, :].bitcast(F32),
                                            ALU.subtract).then_inc(s_pl, 1)
                    return
                rn = n - (n + 2) // 4
                if rn:
                    dve.wait_ge(s_r3, rn)
                nc.vector.tensor_tensor(rot2, ps[:, BX, :], sinT[:, :], ALU.mult).then_inc(s_r2, 1)

            def unit_max(u, loc):
                dve.wait_ge(s_sc, u + 1)
                n = (loc[1] + 1) * P
                nc.vector.tensor_reduce(negmax[:, loc[0] % 4:loc[0] % 4 + 1], ps[:, BS + loc[0] % 2, 0:n], AX.X, ALU.max,
                                        negate=True).then_inc(s_nm, 1)

            def unit_scale(u, loc, gated, gcol=None):
                i, b = loc[1], loc[0] % 4
                n = (i + 1) * P
                dve.wait_ge(s_ex, u + 1)
                nc.vector.reciprocal(rinv[:, b:b + 1], psumrow[:, b:b + 1]).then_inc(s_ri, 1)
                dve.wait_ge(s_ri, u + 1)
                if gated:
                    nc.vector.tensor_scalar(prob[:, b, 0:n], prob[:, b, 0:n], rinv[:, b:b + 1], gate[:, i, gcol:gcol + 1],
                                            ALU.mult, ALU.mult).then_inc(s_pr, 1)
                else:
                    nc.vector.tensor_scalar(prob[:, b, 0:n], prob[:, b, 0:n], rinv[:, b:b + 1], None, ALU.mult).then_inc(s_pr, 1)

            def gated_inverse(u, loc, gcol):
                b = loc[0] % 4
                dve.wait_ge(s_ex, u + 1)
                nc.vector.reciprocal(rinv[:, b:b + 1], psumrow[:, b:b + 1]).then_inc(s_ri, 1)
                dve.wait_ge(s_ri, u + 1)
                nc.vector.tensor_tensor(ginv[:, b:b + 1], rinv[:, b:b + 1], gate[:, loc[1], gcol:gcol + 1], ALU.mult).then_inc(s_gi, 1)

            def unit_lo(u, loc):
                dve.wait_ge(s_pth, u + 1)
                n, b = (loc[1] + 1) * P, loc[0] % 2
                nc.vector.tensor_tensor(ptl[:, b, 0:n], ps[:, BT + b, 0:n], pth[:, b, 0:n].bitcast(F32), ALU.subtract).then_inc(s_ptl, 1)

            def head_lo(count, par, half, pair, oh=oh, ol=ol):
                dve.wait_ge(s_oh, count)
                rows = slice(half * HD, (half + 1) * HD)
                sel = (lambda a: a[rows, pair, :]) if isinstance(pair, int) else \
                    (lambda a: a[rows, bass.ds(pair, 1), :].rearrange("p a s -> p (a s)"))
                nc.vector.tensor_tensor(sel(ol), ps[0:HD, BO + par, :], sel(oh).bitcast(F32), ALU.subtract).then_inc(s_ol, 1)

            def cmp_mask(H):
                dve.wait_ge(s_cs, H + 1)
                if H:
                    dve.wait_ge(s_ct, H)
                nc.vector.tensor_tensor(csm[:, :, :], ps[:, BX, 0:QT * NCMP].rearrange("p (m n) -> p m n", m=QT), cmask[:, :, :],
                                        ALU.add).then_inc(s_cmask, 1)
                dve.wait_ge(s_cmask, H + 1)
                nc.vector.tensor_reduce(cstat[:, 0, :], csm[:, :, :], AX.X, ALU.max).then_inc(s_cmax, 1)

            def cmp_difference(H):
                dve.wait_ge(s_cmax, H + 1)
                nc.vector.tensor_scalar(cstat[:, 1, :], cstat[:, 0, :], FLOOR, None, ALU.max).then_inc(s_cfl, 1)
                dve.wait_ge(s_cfl, H + 1)
                nc.vector.tensor_tensor(csm[:, :, :], csm[:, :, :], cstat[:, 1, :].unsqueeze(2).to_broadcast([P, QT, NCMP]),
                                        ALU.subtract).then_inc(s_cdf, 1)

            def cmp_sum(H):
                dve.wait_ge(s_ce, H + 1)
                nc.vector.tensor_reduce(cstat[:, 2, :], csm[:, :, :], AX.X, ALU.add).then_inc(s_csum, 1)
                dve.wait_ge(s_csum, H + 1)
                nc.vector.tensor_scalar(cstat[:, 2, :], cstat[:, 2, :], 1e-30, None, ALU.max).then_inc(s_csf, 1)

            def cmp_inverse(H):
                dve.wait_ge(s_csf, H + 1)
                nc.vector.reciprocal(cstat[:, 3, :], cstat[:, 2, :]).then_inc(s_cinv, 1)

            def cmp_gate(H):
                dve.wait_ge(s_cinv, H + 1)
                nc.vector.tensor_tensor(cstat[:, 3, :], cstat[:, 3, :], gate[:, :, 3 * H], ALU.mult).then_inc(s_cg, 1)

            def cmp_scale(H):
                dve.wait_ge(s_cg, H + 1)
                nc.vector.tensor_tensor(csm[:, :, :], csm[:, :, :], cstat[:, 3, :].unsqueeze(2).to_broadcast([P, QT, NCMP]),
                                        ALU.mult).then_inc(s_cp, 1)

            for k in range(2):
                item_dve(0, k)
            item_dve(0, 2)
            conv_copy(1)
            for step in (cmp_mask, cmp_difference, cmp_sum, cmp_inverse, cmp_gate, cmp_scale):
                step(0)
            unit_max(0, (0, 0))
            unit_max(1, (1, 0))
            unit_scale(0, (0, 0), True, 1)
            for g in range(GROUPS):
                for v in range(32):
                    u, w = 32 * g + v, v % 8
                    H = u // 8
                    item = (g, 3) if v < 8 else (g + 1, v // 8 - 1)
                    turned = v < 8 or g < GROUPS - 1
                    following = H + 1 < HEADS
                    if u + 2 < NSA_UNITS:
                        unit_max(u + 2, (u + 2, (u + 2) % 8 // 2))
                    if w == 7 and following:
                        cmp_inverse(H + 1)
                    if u + 1 < U_ACT:
                        unit_scale(u + 1, (u + 1, (u + 1) % 8 // 2), True, 3 * ((u + 1) // 8) + 1 + (u + 1) % 2)
                    elif u + 1 < NSA_UNITS:
                        gated_inverse(u + 1, (u + 1, (u + 1) % 8 // 2), 3 * ((u + 1) // 8) + 1 + (u + 1) % 2)
                    if turned and w == (3 if item[1] == 1 else 2):
                        item_dve(*item)
                    if w == 4 and following:
                        cmp_mask(H + 1)
                    if w == 5 and following:
                        cmp_difference(H + 1)
                    if w == 7 and following:
                        cmp_gate(H + 1)
                    if u:
                        unit_lo(u - 1, (u - 1, (u - 1) % 8 // 2))
                    if w == 6 and following:
                        cmp_sum(H + 1)
                    if w == 7 and following:
                        cmp_scale(H + 1)
                    if w == 3 and u > 8:
                        head_lo(H, (H - 1) % 2, (H - 1) % 2, (H - 1) // 2)
            unit_lo(NSA_UNITS - 1, (NSA_UNITS - 1, 3))
            head_lo(HEADS, 1, 1, KB - 1)

            def z_sum(n, j):
                dve.wait_ge(s_z1, NSHIFT * n + j + 1)
                if j > 1:
                    dve.wait_ge(s_zs, 5 * n + j - 1)
                nc.vector.tensor_tensor(zsum, z[:, 0, :] if j == 1 else zsum, z[:, j, :], ALU.add).then_inc(s_zs, 1)

            def square_sum(n, k):
                dve.wait_ge(s_sq, 8 * n + k + 1)
                if k > 1:
                    dve.wait_ge(s_acc, 6 * n + k - 1)
                nc.vector.tensor_tensor(sqsum, sq[:, 0, :] if k == 1 else sqsum, sq[:, k % 2, :], ALU.add).then_inc(s_acc, 1)

            def statistics(n, less_shift, add_product):
                dve.wait_ge(s_shift, n + 1)
                for k in range(KB):
                    if k >= 3:
                        square_sum(n, k - 2)
                    if k == KB - 1:
                        square_sum(n, k - 1)
                    if k < NSHIFT:
                        nc.vector.tensor_tensor(z[:, k, :], z[:, k, :], shift, ALU.subtract).then_inc(s_cent, 1)
                    else:
                        less_shift(k)
                        dve.wait_ge(s_zl, (KB - NSHIFT) * n + k - NSHIFT + 1)
                        add_product(k)
                    if k == KB - 2:
                        dve.wait_ge(s_cent, 8 * n + k + 1)
                        nc.vector.tensor_tensor(zsum, z[:, k - 1, :], z[:, k, :], ALU.add).then_inc(s_zs, 1)

            def out_dve(c0, n):
                def from_x(j):
                    nc.vector.tensor_scalar(z[:, j, :], xl[:, j, :].bitcast(F32), ALPHA, None, ALU.mult).then_inc(s_za, 1)
                    dve.wait_ge(s_za, 4 * n + j + 1)
                    nc.vector.scalar_tensor_tensor(out=z[:, j, :], in0=xh[:, j, :].bitcast(F32), scalar=ALPHA, in1=z[:, j, :],
                                                   op0=ALU.mult, op1=ALU.add).then_inc(s_zb, 1)

                def add_product(j, done=s_cent):
                    dve.wait_ge(s_wu, c0 + j + 1)
                    dve.wait_ge(s_zb, 4 * n + j + 1)
                    nc.vector.tensor_tensor(z[:, j, :], z[:, j, :], ps[:, j % 3, :], ALU.add).then_inc(done, 1)

                def less_shift(j):
                    dve.wait_ge(s_zb, 4 * n + j + 1)
                    nc.vector.tensor_tensor(z[:, j, :], z[:, j, :], shift, ALU.subtract).then_inc(s_zl, 1)

                for j in range(3):
                    from_x(j)
                for j in range(NSHIFT):
                    add_product(j, s_z1)
                    if j:
                        z_sum(n, j)
                    if j < NSHIFT - 1:
                        from_x(3 + j)
                from_x(KB - 1)
                statistics(n, less_shift, add_product)

            def ln_dve(n, final):
                g0 = (n // 2) * 8 + (0 if n % 2 == 0 else 32)

                def less_delta(k):
                    dve.wait_ge(s_sq, 8 * n + k + 1)
                    nc.vector.tensor_tensor(z[:, k, :], z[:, k, :], delta, ALU.subtract).then_inc(s_sub, 1)

                dve.wait_ge(s_cent, 8 * (n + 1))
                dve.wait_ge(s_d2, n + 1)
                dve.wait_ge(s_e, n + 1)
                nc.vector.tensor_tensor(var, ps[:, B_SQ, :], var, ALU.subtract).then_inc(s_vr, 1)
                dve.wait_ge(s_dl, n + 1)
                less_delta(0)
                dve.wait_ge(s_std, n + 1)
                nc.vector.reciprocal(rstd, std).then_inc(s_rstd, 1)
                dve.wait_ge(s_rstd, n + 1)

                def affine(k):
                    nc.vector.tensor_scalar(z[:, k, :], z[:, k, :], vecs[:, g0 + k:g0 + k + 1], vecs[:, g0 + 16 + k:g0 + 17 + k],
                                            ALU.mult, ALU.add).then_inc(s_y, 1)

                for k in range(KB + 2):
                    if k < KB:
                        if k in LESS_DVE:
                            dve.wait_ge(s_sub, len(LESS_DVE) * n + LESS_DVE.index(k) + 1)
                        else:
                            dve.wait_ge(s_subp, len(LESS_POOL) * n + LESS_POOL.index(k) + 1)
                        nc.vector.tensor_tensor(z[:, k, :], z[:, k, :], rstd, ALU.mult).then_inc(s_nrm, 1)
                    if n == 1 and k == 0:
                        dve.wait_ge(s_fw, 1)
                        nc.vector.tensor_tensor(wf_l[:, :, :], wf_raw[:, :, :], wf_h[:, :, :].bitcast(F32), ALU.subtract).then_inc(s_fw, 1)
                    if k in (2, 4):
                        less_delta(LESS_DVE[k // 2])
                    if final:
                        if k - 1 in (3, 6):
                            dve.wait_ge(s_nrm, 8 * n + k)
                            affine(k - 1)
                        continue
                    if 0 < k <= KB:
                        dve.wait_ge(s_xh, 8 * (n + 1) + k)
                        affine(k - 1)
                    if k - 2 in XL_DVE:
                        dve.wait_ge(s_y, 8 * n + k - 1)
                        nc.vector.tensor_tensor(xl[:, k - 2, :], z[:, k - 2, :], xh[:, k - 2, :].bitcast(F32), ALU.subtract).then_inc(s_x, 1)

            def ffn_dve(l, c_up, c_dn, n):
                def taps(buf, j, blk, bank, c2):
                    dve.wait_ge(s_c0, c2 + 1)
                    nc.vector.scalar_tensor_tensor(out=buf[:, 1:SEQ], in0=ps[:, bank, 0:SEQ - 1], scalar=conv[:, l, 1, bass.ds(blk, 1)],
                                                   in1=buf[:, 1:SEQ], op0=ALU.mult, op1=ALU.add).then_inc(s_c1, 1)
                    dve.wait_ge(s_c1, c2 + 1)
                    nc.vector.scalar_tensor_tensor(out=buf[:, 2:SEQ], in0=ps[:, bank, 0:SEQ - 2], scalar=conv[:, l, 0, bass.ds(blk, 1)],
                                                   in1=buf[:, 2:SEQ], op0=ALU.mult, op1=ALU.add).then_inc(s_c2, 1)

                def pair(j, bank):
                    jj = FB * l + j
                    taps(ua, j, j, bank, 2 * jj)
                    taps(ub, j, FB + j, bank + 1, 2 * jj + 1)
                    dve.wait_ge(s_gelu, jj + 1)
                    dve.wait_ge(s_c2, 2 * jj + 2)
                    nc.vector.tensor_tensor(gf, ga, ub, ALU.mult).then_inc(s_g, 1)
                    dve.wait_ge(s_gh, jj + 1)
                    sel = lambda a: a[:, bass.ds(j, 1), :].rearrange("p a s -> p (a s)")
                    nc.vector.tensor_tensor(sel(gl), gf, sel(gh).bitcast(F32), ALU.subtract).then_inc(s_gl, 1)

                pair(0, 0)
                with dve.Fori(0, (FB - 1) // 3) as i:
                    for r in range(3):
                        pair(1 + 3 * i + r, (2 + 2 * r) % 6)

                for j in range(NSHIFT):
                    dve.wait_ge(s_wu, c_dn + 3 * j + 3)
                    nc.vector.scalar_tensor_tensor(out=z[:, j, :], in0=z[:, j, :], scalar=ALPHA, in1=ps[:, B_DOWN + j % 2, :],
                                                   op0=ALU.mult, op1=ALU.add).then_inc(s_z1, 1)
                    if j:
                        z_sum(n, j)

                def less_shift(j):
                    nc.vector.scalar_tensor_tensor(out=z[:, j, :], in0=z[:, j, :], scalar=ALPHA, in1=shift,
                                                   op0=ALU.mult, op1=ALU.subtract).then_inc(s_zl, 1)

                def add_product(j):
                    dve.wait_ge(s_wu, c_dn + 3 * j + 3)
                    nc.vector.tensor_tensor(z[:, j, :], z[:, j, :], ps[:, B_DOWN + j % 2, :], ALU.add).then_inc(s_cent, 1)

                statistics(n, less_shift, add_product)

            out_dve(C_WO0, 0)
            ln_dve(0, False)
            ffn_dve(0, C_UP0, C_DN0, 1)
            ln_dve(1, False)

            def fox_k_lo(par, h):
                rows = halves[h]
                for to in halves:
                    last = nc.vector.tensor_tensor(fkd[par][to, h, 1, :], ps[rows, BX, :], fkd[par][rows, h, 0, :].bitcast(F32), ALU.subtract)
                last.then_inc((s_pl, s_plb)[h], 1)

            def fox_lo(par, r, n, bank=BX):
                dve.wait_ge(s_ph, n + 1)
                if r == 0:
                    for h, rows in enumerate(halves):
                        last = nc.vector.scalar_tensor_tensor(out=fqs[par][halves[1 - h], h, :], in0=ps[rows, BP, :], scalar=SCALE,
                                                              in1=fqs[par][rows, h, :].bitcast(F32), op0=ALU.mult, op1=ALU.subtract)
                    last.then_inc(s_pl, 1)
                elif r == 1:
                    fox_k_lo(par, 0)
                else:
                    nc.vector.tensor_tensor(fvl[par][:, :, :], ps[:, bank, :].rearrange("p (m c) -> p m c", m=QT), fvh[par][:, :, :].bitcast(F32),
                                            ALU.subtract).then_inc(s_pl, 1)

            hs = slice(0, HEADS)
            dve.wait_ge(s_fp, 1)
            nc.vector.tensor_scalar(fz[hs, :], ps[hs, BT, :], bf[:, 0:1], None, ALU.add).then_inc(s_fd, 1)
            dve.wait_ge(s_fa, 2)
            nc.vector.tensor_scalar(fe[hs, :], fe[hs, :], 1.0, None, ALU.add).then_inc(s_fd, 1)
            fox_lo(0, 0, NSA_ITEMS)
            dve.wait_ge(s_fa, 3)
            dve.wait_ge(s_fd, 2)
            nc.vector.scalar_tensor_tensor(out=fz[hs, :], in0=fz[hs, :], scalar=0.0, in1=fe[hs, :], op0=ALU.min, op1=ALU.subtract).then_inc(s_fd, 1)
            dve.wait_ge(s_fd, 3)
            dve.wait_ge(s_fm, 1)
            nc.vector.tensor_tensor_scan(fcum[hs, :], fone[hs, :], fz[hs, :], 0.0, ALU.mult, ALU.add).then_inc(s_fd, 1)
            fox_lo(0, 1, NSA_ITEMS + 1)
            dve.wait_ge(s_fa, 4)
            dve.wait_ge(s_fd, 4)
            nc.vector.tensor_tensor(cstack[hs, 1, :], fcum[hs, :], cstack[hs, 0, :].bitcast(F32), ALU.subtract).then_inc(s_fd, 1)
            nc.vector.tensor_scalar(cstack[hs, 2, :], cstack[hs, 0, :].bitcast(F32), -1.0, None, ALU.mult).then_inc(s_fd, 1)
            dve.wait_ge(s_fd, 5)
            nc.vector.tensor_scalar(cstack[hs, 3, :], cstack[hs, 1, :].bitcast(F32), -1.0, None, ALU.mult).then_inc(s_fd, 1)
            dve.wait_ge(s_phb, 1)
            fox_k_lo(0, 1)
            fox_lo(0, 2, NSA_ITEMS + 2, BO + 1)
            unit_max(NSA_UNITS, (0, 0))
            unit_max(NSA_UNITS + 1, (1, 1))
            unit_scale(NSA_UNITS, (0, 0), False)

            def fox_stages(pair, par, first=False, more=True):
                U = NSA_UNITS + 8 * pair
                for v in range(8):
                    if more or v + 2 < 8:
                        unit_max(U + v + 2, (v + 2, (v + 2) % 4))
                    if more or v + 1 < 8:
                        unit_scale(U + v + 1, (v + 1, (v + 1) % 4), False)
                    if v == 1 and not first:
                        fox_lo(par, 2, NSA_ITEMS + 3 * pair + 2)
                    if more and v in (2, 4):
                        fox_lo(1 - par, v // 4, NSA_ITEMS + 3 * (pair + 1) + v // 4)
                    if more and v == 6:
                        dve.wait_ge(s_phb, pair + 2)
                        fox_k_lo(1 - par, 1)
                    if v:
                        unit_lo(U + v - 1, (v - 1, (v - 1) % 4))
                    elif not first:
                        unit_lo(U - 1, (7, 3))
                    if v == 2 and not first:
                        head_lo(HEADS + 2 * pair, 1, 1, pair - 1, oh2, ol2)
                    if v == 6:
                        head_lo(HEADS + 2 * pair + 1, 0, 0, pair, oh2, ol2)

            fox_stages(0, 0, first=True)
            with dve.Fori(0, 3) as i:
                for r in range(2):
                    fox_stages(1 + r + 2 * i, (1 + r) % 2)
            fox_stages(7, 1, more=False)
            unit_lo(NSA_UNITS + FOX_UNITS - 1, (7, 3))
            head_lo(2 * HEADS, 1, 1, KB - 1, oh2, ol2)

            out_dve(C_WO1, 2)
            ln_dve(2, False)
            ffn_dve(1, C_UP1, C_DN1, 3)
            ln_dve(3, True)
            for half in range(2):
                for m in range(1, QT, 2):
                    dve.wait_ge(s_yt, 4 * half + m + 1)
                    nc.vector.tensor_copy(onat[:, m, half * 512:(half + 1) * 512], ps[:, 2 * m + half, :]).then_inc(s_yd, 1)


_INS = ["x", "nsa_w_in", "nsa_b_gate", "nsa_pe", "nsa_phik_w1", "nsa_phik_b1", "nsa_phik_w2", "nsa_phiv_w1", "nsa_phiv_b1",
        "nsa_phiv_w2", "nsa_w_o", "fox_w_in", "fox_b_f", "fox_w_o", "ffn_w_up", "ffn_conv_w", "ffn_conv_b", "ffn_w_down",
        "ln1_g", "ln1_b", "ln2_g", "ln2_b"]


def shape_constants():
    import numpy as np
    f = np.float32
    inv = (f(10000.0) ** (-np.arange(0, HD, 2, dtype=f) / f(HD))).astype(f)
    ang = np.arange(SEQ, dtype=f)[:, None] * inv[None, :]
    ang = np.concatenate([ang, ang, ang, ang], axis=1)
    rot = np.zeros((P, P), f)
    for d in range(P):
        if d % HD < HD // 2:
            rot[d + HD // 2, d] = -1.0
        else:
            rot[d - HD // 2, d] = 1.0
    q, k = np.arange(P)[:, None], np.arange(P)[None, :]
    tok = np.arange(QT)[None, :, None] * P + np.arange(P)[:, None, None]
    end = np.arange(NCMP)[None, None, :] * CMP_STRIDE + CMP_LEN - 1
    return {
        "c_ident": np.eye(P, dtype=f), "c_causal": np.where(k <= q, 0.0, NEG).astype(f), "c_ones": np.full((P, P), 1.0 / D, f),
        "c_rot": rot, "c_cmask": np.where(end <= tok, 0.0, NEG).astype(f),
        "c_cos": np.ascontiguousarray(np.cos(ang).T.astype(f)), "c_sin": np.ascontiguousarray(np.sin(ang).T.astype(f)),
    }


def kernel(**inputs):
    import numpy as np
    import concourse.bacc as bacc
    from concourse.bass_utils import run_bass_kernel_spmd

    nc = bacc.Bacc("TRN2", target_bir_lowering=False, num_devices=1)
    arrays, t = {}, {}
    for name, a in [(n, inputs[n]) for n in _INS] + list(shape_constants().items()):
        a = np.ascontiguousarray(a)
        arrays[f"in_{name}"] = a
        t[name] = nc.dram_tensor(f"in_{name}", a.shape, F32, kind="ExternalInput").ap()
    t["cum"] = nc.dram_tensor("cum", (4, HEADS, SEQ), F32, kind="Internal").ap()
    out = nc.dram_tensor("out_0", (1, SEQ, D), F32, kind="ExternalOutput").ap()
    build_trunk(nc, t, out)
    r = run_bass_kernel_spmd(nc, [arrays], core_ids=[0])
    return r.results[0]["out_0"]
```
